# Optimizing a Trainium2 kernel written in Bass

```python
import jax, jax.numpy as jnp
from jax import lax
import numpy as np

D_MODEL = 1024
BATCH = 1
SEQ = 512
DEPTH = 1

EPS = 1e-6
ROPE_THETA = 500000.0
ROT_FRAC = 4
GLA_HEADS = 4
GLA_DK = 64
GLA_DV = 128
GLA_GATE_RANK = 16
GLA_TAU = 16.0
GLA_CHUNK = 64
DSA_HEADS = 8
DSA_HD = 64
IDX_HEADS = 8
IDX_DIM = 64
DSA_TOPK_MAX = 256
Q_BLOCK = 128
N_GROUPS = 4
EXPERTS_PER_GROUP = 8
N_EXPERTS = N_GROUPS * EXPERTS_PER_GROUP
EXPERT_TOPK = 2
D_EXPERT = D_MODEL // 4
N_BRANCHES = 2
N_MOD = 6

GLA_QK = GLA_HEADS * GLA_DK
GLA_V = GLA_HEADS * GLA_DV
DSA_W = DSA_HEADS * DSA_HD
IDX_Q = IDX_HEADS * IDX_DIM
SPLIT_SIZES = (GLA_QK, GLA_QK, GLA_V, GLA_V, GLA_GATE_RANK,
               DSA_W, DSA_W, DSA_W, IDX_Q, IDX_DIM, IDX_HEADS,
               N_BRANCHES * D_MODEL)
D_IN = sum(SPLIT_SIZES)

kernel_name = "hybrid_gla_dsa_hmoe_block"

def rmsnorm(x, g):
    x32 = x.astype(jnp.float32)
    y = x32 * lax.rsqrt(jnp.mean(x32 * x32, axis=-1, keepdims=True) + EPS)
    return (y * g.astype(jnp.float32)).astype(x.dtype)

def layernorm(x, g):
    x32 = x.astype(jnp.float32)
    mu = jnp.mean(x32, axis=-1, keepdims=True)
    xc = x32 - mu
    y = xc * lax.rsqrt(jnp.mean(xc * xc, axis=-1, keepdims=True) + EPS)
    return (y * g.astype(jnp.float32)).astype(x.dtype)

def rope_partial(x, pos):
    hd = x.shape[-1]
    rot = hd // ROT_FRAC
    half = rot // 2
    freqs = jnp.power(jnp.float32(ROPE_THETA), -jnp.arange(half, dtype=jnp.float32) * 2.0 / rot)
    ang = pos.astype(jnp.float32)[:, :, None, None] * freqs
    cos, sin = jnp.cos(ang), jnp.sin(ang)
    x32 = x.astype(jnp.float32)
    x1, x2 = x32[..., :half], x32[..., half:rot]
    out = jnp.concatenate([x1 * cos - x2 * sin, x1 * sin + x2 * cos, x32[..., rot:]], axis=-1)
    return out.astype(x.dtype)

def gla_chunked(q, k, v, la):
    B, S, H, dk = q.shape
    dv = v.shape[-1]
    C = GLA_CHUNK
    N = S // C

    def to_chunks(t):
        return t.astype(jnp.float32).reshape(B, N, C, H, t.shape[-1]).transpose(1, 0, 3, 2, 4)

    causal = jnp.tril(jnp.ones((C, C), dtype=bool))

    def step(state, inp):
        qc, kc, vc, lac = inp
        b = jnp.cumsum(lac, axis=2)
        o_inter = jnp.einsum('bhtd,bhdv->bhtv', qc * jnp.exp(b), state)
        diff = b[:, :, :, None, :] - b[:, :, None, :, :]
        decay = jnp.exp(jnp.where(causal[:, :, None], diff, -jnp.inf))
        scores = jnp.einsum('bhtd,bhsd,bhtsd->bhts', qc, kc, decay)
        o = o_inter + jnp.einsum('bhts,bhsv->bhtv', scores, vc)
        b_last = b[:, :, -1:, :]
        state = (jnp.exp(b_last[:, :, 0, :])[..., None] * state
                 + jnp.einsum('bhsd,bhsv->bhdv', kc * jnp.exp(b_last - b), vc))
        return state, o

    s0 = jnp.zeros((B, H, dk, dv), jnp.float32)
    _, o = lax.scan(step, s0, (to_chunks(q), to_chunks(k), to_chunks(v), to_chunks(la)))
    return o.transpose(1, 0, 3, 2, 4).reshape(B, S, H, dv).astype(q.dtype)

def dsa_attention(q, k, v, qi, ki, wi):
    B, S, H, hd = q.shape
    topk = min(DSA_TOPK_MAX, S // 4)
    nb = S // Q_BLOCK

    def blocks(t):
        return t.reshape((B, nb, Q_BLOCK) + t.shape[2:]).swapaxes(0, 1)

    qpos = jnp.arange(S, dtype=jnp.int32).reshape(nb, Q_BLOCK)
    kpos = jnp.arange(S, dtype=jnp.int32)
    ki32 = ki.astype(jnp.float32)

    def one_block(inp):
        qb, qib, wib, tb = inp
        logits = jnp.einsum('bqhd,bsd->bqhs', qib.astype(jnp.float32), ki32) * (IDX_DIM ** -0.5)
        idx_score = jnp.einsum('bqhs,bqh->bqs', jax.nn.relu(logits), wib.astype(jnp.float32))
        visible = kpos[None, :] <= tb[:, None]
        idx_score = jnp.where(visible[None], idx_score, -jnp.inf)
        _, sel = lax.top_k(idx_score, topk)
        k_sel = jax.vmap(lambda kk, ii: kk[ii])(k, sel)
        v_sel = jax.vmap(lambda vv, ii: vv[ii])(v, sel)
        valid = sel <= tb[None, :, None]
        s = jnp.einsum('bqhd,bqkhd->bhqk', qb.astype(jnp.float32), k_sel.astype(jnp.float32)) * (hd ** -0.5)
        s = jnp.where(valid[:, None], s, -jnp.inf)
        p = jax.nn.softmax(s, axis=-1)
        return jnp.einsum('bhqk,bqkhd->bqhd', p, v_sel.astype(jnp.float32)).astype(q.dtype)

    out = lax.map(one_block, (blocks(q), blocks(qi), blocks(wi), qpos))
    return out.swapaxes(0, 1).reshape(B, S, H, hd)

def hier_moe(h, w_rg, b_rg, w_re, b_re, w_g, w_u, w_d):
    B, S, D = h.shape
    T = B * S
    ht = h.reshape(T, D)
    g_prob = jax.nn.softmax((ht @ w_rg + b_rg).astype(jnp.float32), axis=-1)
    g_sel = jnp.argmax(g_prob, axis=-1)
    p_g = jnp.take_along_axis(g_prob, g_sel[:, None], axis=1)[:, 0]
    e_logits = (ht @ w_re + b_re).astype(jnp.float32).reshape(T, N_GROUPS, EXPERTS_PER_GROUP)
    e_in = jnp.take_along_axis(e_logits, g_sel[:, None, None], axis=1)[:, 0]
    e_prob = jax.nn.softmax(e_in, axis=-1)
    top_p, top_i = lax.top_k(e_prob, EXPERT_TOPK)
    top_p = top_p / jnp.sum(top_p, axis=-1, keepdims=True)
    eid = g_sel[:, None] * EXPERTS_PER_GROUP + top_i
    combine = jnp.sum(jax.nn.one_hot(eid, N_EXPERTS, dtype=jnp.float32)
                      * (p_g[:, None] * top_p)[..., None], axis=1)
    hg = jnp.einsum('td,edf->tef', ht, w_g)
    hu = jnp.einsum('td,edf->tef', ht, w_u)
    act = jax.nn.silu(hg) * hu * combine[..., None].astype(hg.dtype)
    y = jnp.einsum('tef,efd->td', act, w_d)
    return y.reshape(B, S, D)

def setup_inputs(seed: int = 0) -> dict:
    key = jax.random.key(seed)
    ks = jax.random.split(key, 32)
    D = D_MODEL

    def nrm(k, shape, scale):
        return jax.random.normal(k, shape, jnp.float32) * scale

    def gain(k, n):
        return 1.0 + 0.02 * jax.random.normal(k, (DEPTH, n), jnp.float32)

    return {
        "x": nrm(ks[0], (BATCH, SEQ, D), 1.0),
        "c": nrm(ks[1], (BATCH, D), 1.0),
        "positions": jnp.broadcast_to(jnp.arange(SEQ, dtype=jnp.int32), (BATCH, SEQ)),
        "w_ada": nrm(ks[2], (DEPTH, D, N_MOD * D), 0.2 * D ** -0.5),
        "b_ada": nrm(ks[3], (DEPTH, N_MOD * D), 0.02),
        "g_pre_mix": gain(ks[4], D),
        "g_post_mix": gain(ks[5], D),
        "g_pre_ffn": gain(ks[6], D),
        "g_post_ffn": gain(ks[7], D),
        "w_in": nrm(ks[8], (DEPTH, D, D_IN), D ** -0.5),
        "w_gla_a2": nrm(ks[9], (DEPTH, GLA_GATE_RANK, GLA_QK), GLA_GATE_RANK ** -0.5),
        "b_gla_a": nrm(ks[10], (DEPTH, GLA_QK), 0.1),
        "g_gla_out": gain(ks[11], GLA_DV),
        "g_idx_k": gain(ks[12], IDX_DIM),
        "w_proj_gla": nrm(ks[13], (DEPTH, GLA_V, D), GLA_V ** -0.5),
        "w_proj_dsa": nrm(ks[14], (DEPTH, DSA_W, D), DSA_W ** -0.5),
        "w_out": nrm(ks[15], (DEPTH, D, D), D ** -0.5),
        "w_router_g": nrm(ks[16], (DEPTH, D, N_GROUPS), D ** -0.5),
        "b_router_g": nrm(ks[17], (DEPTH, N_GROUPS), 0.01),
        "w_router_e": nrm(ks[18], (DEPTH, D, N_EXPERTS), D ** -0.5),
        "b_router_e": nrm(ks[19], (DEPTH, N_EXPERTS), 0.01),
        "w_e_gate": nrm(ks[20], (DEPTH, N_EXPERTS, D, D_EXPERT), D ** -0.5),
        "w_e_up": nrm(ks[21], (DEPTH, N_EXPERTS, D, D_EXPERT), D ** -0.5),
        "w_e_down": nrm(ks[22], (DEPTH, N_EXPERTS, D_EXPERT, D), D_EXPERT ** -0.5),
    }

def reference(x, c, positions, w_ada, b_ada, g_pre_mix, g_post_mix, g_pre_ffn, g_post_ffn,
              w_in, w_gla_a2, b_gla_a, g_gla_out, g_idx_k, w_proj_gla, w_proj_dsa, w_out,
              w_router_g, b_router_g, w_router_e, b_router_e, w_e_gate, w_e_up, w_e_down):
    B, S, D = x.shape
    offsets = [int(o) for o in np.cumsum(SPLIT_SIZES)[:-1]]
    for l in range(DEPTH):
        mod = (jax.nn.silu(c) @ w_ada[l] + b_ada[l]).reshape(B, N_MOD, D)
        shift_m, scale_m, gate_m, shift_f, scale_f, gate_f = [mod[:, i][:, None, :] for i in range(N_MOD)]

        h = rmsnorm(x, g_pre_mix[l]) * (1.0 + scale_m) + shift_m
        proj = h @ w_in[l]
        (gq, gk, gv, gg, ga_low, dq, dk, dv, iq, ik, iw, bg) = jnp.split(proj, offsets, axis=-1)

        q_a = gq.reshape(B, S, GLA_HEADS, GLA_DK) * (GLA_DK ** -0.5)
        k_a = gk.reshape(B, S, GLA_HEADS, GLA_DK)
        v_a = gv.reshape(B, S, GLA_HEADS, GLA_DV)
        la = jax.nn.log_sigmoid((ga_low @ w_gla_a2[l] + b_gla_a[l]).astype(jnp.float32)) / GLA_TAU
        o_a = gla_chunked(q_a, k_a, v_a, la.reshape(B, S, GLA_HEADS, GLA_DK))
        o_a = rmsnorm(o_a, g_gla_out[l]) * jax.nn.silu(gg.reshape(B, S, GLA_HEADS, GLA_DV))
        y_gla = o_a.reshape(B, S, GLA_V) @ w_proj_gla[l]

        q_b = rope_partial(dq.reshape(B, S, DSA_HEADS, DSA_HD), positions)
        k_b = rope_partial(dk.reshape(B, S, DSA_HEADS, DSA_HD), positions)
        v_b = dv.reshape(B, S, DSA_HEADS, DSA_HD)
        qi = rope_partial(iq.reshape(B, S, IDX_HEADS, IDX_DIM), positions)
        ki = rope_partial(layernorm(ik, g_idx_k[l])[:, :, None, :], positions)[:, :, 0, :]
        wi = iw * (IDX_HEADS ** -0.5)
        o_b = dsa_attention(q_b, k_b, v_b, qi, ki, wi)
        y_dsa = o_b.reshape(B, S, DSA_W) @ w_proj_dsa[l]

        gates = jax.nn.sigmoid(bg.reshape(B, S, N_BRANCHES, D))
        mix = gates[:, :, 0] * y_gla + gates[:, :, 1] * y_dsa
        out = mix @ w_out[l]
        x = x + gate_m * rmsnorm(out, g_post_mix[l])

        h = rmsnorm(x, g_pre_ffn[l]) * (1.0 + scale_f) + shift_f
        y = hier_moe(h, w_router_g[l], b_router_g[l], w_router_e[l], b_router_e[l],
                     w_e_gate[l], w_e_up[l], w_e_down[l])
        x = x + gate_f * rmsnorm(y, g_post_ffn[l])
    return x


_drawn_inputs = setup_inputs


def setup_inputs(seed=0):
    import zlib

    import numpy as np

    out = dict(_drawn_inputs(seed))
    spreads = {}
    factors = {'g_pre_mix': 4.93,
     'g_post_mix': 8.0,
     'g_pre_ffn': 2.994,
     'g_post_ffn': 8.0,
     'b_gla_a': 5.221,
     'g_gla_out': 7.908,
     'g_idx_k': 6.909,
     'b_router_g': 5.991,
     'b_router_e': 5.545}
    for name, (base, spread) in spreads.items():
        noise = np.random.default_rng([zlib.crc32(name.encode()), seed]).standard_normal(out[name].shape)
        drawn = base * np.exp(spread * noise) if base else spread * noise
        out[name] = __import__('jax').numpy.asarray(drawn.astype(out[name].dtype))
    for name, factor in factors.items():
        out[name] = (out[name] * factor).astype(out[name].dtype)
    return out
```

```python
from contextlib import ExitStack

import numpy as np

import concourse.bass as bass
from concourse import mybir

ALU = mybir.AluOpType
ACT = mybir.ActivationFunctionType
F32 = mybir.dt.float32
I32 = mybir.dt.int32
U32 = mybir.dt.uint32
AX = mybir.AxisListType

P = 128
D = 1024
SEQ = 512
TT = SEQ // P
KD = D // P
EPS = 1e-6
GLA_H, GLA_DK, GLA_DV, RANK = 4, 64, 128, 16
TAU = 16.0
HEADS, HD = 8, 64
TOPK = min(256, SEQ // 4)
ROT = HD // 4
HALF = ROT // 2
THETA = 500000.0
GROUPS, PER_GROUP = 4, 8
NE = GROUPS * PER_GROUP
DE = D // 4
PAIRS = HEADS // 2
SIZES = (256, 256, 512, 512, RANK, 512, 512, 512, 512, 64, 8, 2 * D)
OFF = [0] + [int(v) for v in np.cumsum(SIZES)]
(O_GQ, O_GK, O_GV, O_GG, O_GA, O_DQ, O_DK, O_DV, O_IQ, O_IK, O_IW, O_BG) = OFF[:12]
NS = RANK + 64 + 8
BLK = 32
NB = P // BLK
CLAMP = 40.0
HIDE = -1e30
TAKEN = -3e38
SLOT = 64
NPAIR = NE // 2
NOV = 16
NPALL = NPAIR + NOV // 2
WELEM = 3 * D * DE // P


class Bank:

    def __init__(self, full, free):
        self.full, self.free, self.at = full, free, {}

    def turn(self, name):
        assert name not in self.at, name
        self.at[name] = len(self.at)
        return self.at[name]


def layer(nc, x, c, positions, w_ada, b_ada, g_pre_mix, g_post_mix, g_pre_ffn, g_post_ffn, w_in,
          w_gla_a2, b_gla_a, g_gla_out, g_idx_k, w_proj_gla, w_proj_dsa, w_out, w_router_g,
          b_router_g, w_router_e, b_router_e, w_e_gate, w_e_up, w_e_down, out):
    xn_dram = nc.dram_tensor("xn_dram", (SEQ, D), F32, kind="Internal").ap()
    y_dram = nc.dram_tensor("y_dram", (NPALL * P, D), F32, kind="Internal").ap()
    slot_dram = nc.dram_tensor("slot_dram", (NPALL * P, 1), U32, kind="Internal").ap()

    x_v = x[0].rearrange("(t p) d -> p t d", p=P)
    out_v = out[0].rearrange("(t p) d -> p t d", p=P)
    win_v = w_in[0].rearrange("(k p) n -> p k n", p=P)
    ada_v = w_ada[0].rearrange("(k p) n -> p k n", p=P)
    pg_v = w_proj_gla[0].rearrange("(k p) n -> p k n", p=P)
    pd_v = w_proj_dsa[0].rearrange("(k p) n -> p k n", p=P)
    wo_v = w_out[0].rearrange("(k p) n -> p k n", p=P)
    weg_v = w_e_gate[0].rearrange("e (k p) f -> e p k f", p=P)
    weu_v = w_e_up[0].rearrange("e (k p) f -> e p k f", p=P)
    wed_v = w_e_down[0].rearrange("e (k p) n -> e p k n", p=P)

    with ExitStack() as ctx:
        def sb(name, shape, dt=F32):
            return ctx.enter_context(nc.sbuf_tensor(name, shape, dt))

        def sem(name):
            return ctx.enter_context(nc.semaphore(name))

        arena = sb("arena", [P, 4 * WELEM])
        ring = arena[:, 0:4 * 4096].rearrange("p (s n) -> p s n", s=4)
        hT = arena[:, 16384:20480].rearrange("p (k n) -> p k n", k=KD)
        prob = arena[:, 20480:22528].rearrange("p (b h n) -> p b h n", b=2, h=2)
        probT = arena[:, 22528:24576].rearrange("p (b h n) -> p b h n", b=2, h=2)
        relu = prob[:, 0, :, :]
        wexp = arena[:, :].rearrange("p (s n) -> p s n", s=4)

        qi_mem = sb("qi_mem", [P, 2048])
        qiT = qi_mem[:, :].rearrange("p (c n) -> p c n", c=4)
        expo = qi_mem[:, 0:1792].rearrange("p (r n) -> p r n", r=2)
        xres = qi_mem[:, :].rearrange("p (b n) -> p b n", b=2)
        kiT = sb("kiT", [P, SEQ])
        qT = sb("qT", [P, PAIRS, SEQ])
        gfb = qT[:, 0:2, :].rearrange("p a n -> p (a n)")
        kv = sb("kv", [P, 4096])
        kT = kv[:, 0:2048].rearrange("p (c n) -> p c n", c=PAIRS)
        val = kv[:, 2048:4096].rearrange("p (t n) -> p t n", t=TT)
        mix = kv[:, :].rearrange("p (t n) -> p t n", t=TT)
        xg = kv[:, 0:2048].rearrange("p (b n) -> p b n", b=2)
        h2g = kv[:, 2048:4096].rearrange("p (b k n) -> p b k n", b=2, k=KD)
        yc = kv[:, :].rearrange("p (b w n) -> p b w n", b=2, w=2)
        gqk = sb("gqk", [P, 4, SEQ])
        gvs = sb("gvs", [P, 4096])
        gv = gvs[:, 0:2048].rearrange("p (t n) -> p t n", t=TT)
        gs = gvs[:, 2048:4096].rearrange("p (t n) -> p t n", t=TT)
        x1 = gvs[:, :].rearrange("p (t n) -> p t n", t=TT)
        mask = sb("mask", [P, TT - 1, SEQ])
        sig_mem = sb("sig_mem", [P, 4096])
        x_in = sig_mem[:, :].rearrange("p (t n) -> p t n", t=TT)
        zz = sig_mem[:, :].rearrange("p (w r n) -> p w r n", w=4, r=2)
        sig = sig_mem[:, :].rearrange("p (a t n) -> p a t n", a=2, t=TT)
        xn2 = sig_mem[:, 0:2048].rearrange("p (b n) -> p b n", b=2)
        h2T = sig_mem[:, 2048:4096].rearrange("p (b k n) -> p b k n", b=2, k=KD)
        yb = sig_mem[:, 0:2048].rearrange("p (b n) -> p b n", b=2)
        gact = sig_mem[:, 2048:2560].rearrange("p (b n) -> p b n", b=2)
        aact = sig_mem[:, 2560:3072].rearrange("p (b n) -> p b n", b=2)
        actT = sig_mem[:, 3072:3584].rearrange("p (b k n) -> p b k n", b=2, k=2)
        stage_mem = sb("stage_mem", [P, 2048])
        stage = stage_mem[:, :].rearrange("p (s n) -> p s n", s=4)
        mixT = stage_mem[:, :].rearrange("p (b k n) -> p b k n", b=2, k=KD)
        diag = stage_mem[:, :].rearrange("p (w n) -> p w n", w=2)
        gla_mem = sb("gla_mem", [P, 2560])
        bT = gla_mem[:, 0:1024].rearrange("p (r n) -> p r n", r=2)
        scT = gla_mem[:, 1024:1536].rearrange("p (h n) -> p h n", h=4)
        kN = gla_mem[:, 1536:1792]
        state = gla_mem[:, 1792:2048].rearrange("p (r n) -> p r n", r=2)
        oan = gla_mem[:, 2048:2560]
        gmb = gla_mem[:, 1024:2048]
        w_small = gvs[:, 0:KD * NS].rearrange("p (k n) -> p k n", k=KD)
        ikw = gvs[:, KD * NS:(KD + TT) * NS].rearrange("p (t n) -> p t n", t=TT)
        kin = sig_mem[:, 3072:3584].rearrange("p (t a n) -> p t a n", t=TT, a=2)
        w_rt = sb("w_rt", [P, KD, GROUPS + NE])
        ident = sb("ident", [P, P])
        ones = sb("ones", [P, P])
        before = sb("before", [P, P])
        upto = sb("upto", [P, P])
        causal0 = sb("causal0", [P, P])
        vrows = gla_mem[0:42, 1536:1664]
        vT = sb("vT", [P, 42])
        rows = gla_mem[0:1, 1664:1892]
        rowb = sb("rowb", [P, 228])
        g_out_b, g_ki_b, b_rt_b = rowb[:, 0:128], rowb[:, 128:192], rowb[:, 192:228]
        bada = sb("bada", [16, 3, P])
        mrow = gla_mem[:, 1024:1536]
        m16 = sb("m16", [16, 3, P])
        modT = sb("modT", [P, 3, 16])
        cs = sb("cs", [P, KD])
        c32 = sb("c32", [P, KD, 32])
        scale1 = sb("scale1", [P, KD])
        scale2 = sb("scale2", [P, KD])
        gatev = sb("gatev", [P, 2, KD])
        posi = sb("posi", [P, TT], I32)
        posf = sb("posf", [P, TT])
        rope = sb("rope", [P, 4, TT, HALF])
        nsin = sb("nsin", [P, TT, HALF])
        rtmp = sb("rtmp", [P, HEADS, ROT])
        st = sb("st", [P, 64])
        wi = sb("wi", [P, TT, 8])
        m8 = sb("m8", [P, 8])
        sm = sb("sm", [P, 2, 8])
        dec = sb("dec", [P, 2])
        a2 = gvs[0:RANK, (KD + TT) * NS:(KD + TT) * NS + 256]
        gaT = sig_mem[0:RANK, 3584:4096]
        mask_f = mask[:, :, :].rearrange("p a n -> p (a n)")
        lg = sb("lg", [P, TT, GROUPS + NE])
        gp = sb("gp", [P, TT, 8])
        top = sb("top", [P, TT, 8])
        topi = sb("topi", [P, TT, 8], U32)
        etop = sb("etop", [P, TT, 8])
        etopi = sb("etopi", [P, TT, 8], U32)
        rt = sb("rt", [P, 16, TT])
        ohg = sb("ohg", [P, TT, 2, GROUPS])
        el = mask_f[:, 0:128].rearrange("p (t e) -> p t e", t=TT)
        e1 = mask_f[:, 128:256].rearrange("p (t e) -> p t e", t=TT)
        e2 = mask_f[:, 256:384].rearrange("p (t e) -> p t e", t=TT)
        em = mask_f[:, 384:512].rearrange("p (t e) -> p t e", t=TT)
        rpos = mask_f[:, 512:640].rearrange("p (t e) -> p t e", t=TT)
        rtmp3 = mask_f[:, 640:768].rearrange("p (t e) -> p t e", t=TT)
        cnt = mask_f[:, 768:1024].rearrange("p (a e) -> p a e", a=8)
        ovc = mask_f[:, 1024:1536].rearrange("p (a e) -> p a e", a=NOV)
        ovi = sb("ovi", [P, NOV + 2], I32)
        ovf = sb("ovf", [P, NOV + 2])
        iota = sb("iota", [P, NE], I32)
        iotaf = sb("iotaf", [P, NE])
        tokid = sb("tokid", [P, TT], I32)
        slotpos = sb("slotpos", [P, TT, 2], U32)
        slot_r = gla_mem[0:NPALL, 0:P].bitcast(U32)
        slot_f = gla_mem[0:NPALL, P:2 * P]
        slot_i = sb("slot_i", [P, NPALL], U32)
        slot_c = sb("slot_c", [P, 2], U32)
        zero_i = sb("zero_i", [NPALL, P], U32)

        names = ["A0", "A1", "S0", "S1", "T0", "T1", "O", "G"]
        ps, bank = {}, {}
        for n in names:
            ps[n] = ctx.enter_context(nc.psum_tensor("ps" + n, [P, 512], F32))
            bank[n] = Bank(sem(n + "_full"), sem(n + "_free"))

        ld_x = [sem(f"ld_x{t}") for t in range(TT)]
        ld_vec, ld_rows, ld_pos, ld_bada = (sem(n) for n in ("ld_vec", "ld_rows", "ld_pos", "ld_bada"))
        ld_small, ld_a2, ld_rt = sem("ld_small"), sem("ld_a2"), sem("ld_rt")
        ring_in = [sem(f"ring_in{i}") for i in range(4)]
        ring_out = sem("ring_out")
        const_ready, rows_cast = sem("const_ready"), sem("rows_cast")
        vT_ready, rowb_ready, c_ready = sem("vT_ready"), sem("rowb_ready"), sem("c_ready")
        ss_ready, rs_ready, xn_ready = sem("ss_ready"), sem("rs_ready"), sem("xn_ready")
        hraw, h_ready = sem("hraw"), sem("h_ready")
        mrow_ready, m16_in, m16_ready, mod_ready = (sem(n) for n in ("mrow_ready", "m16_in", "m16_ready", "mod_ready"))
        sin_in, sin_out, rope_ready = sem("sin_in"), sem("sin_out"), sem("rope_ready")
        stage_in, stage_roped, stage_out = sem("stage_in"), sem("stage_roped"), sem("stage_out")
        ikw_in, ki_ready, wi_ready = sem("ikw_in"), sem("ki_ready"), sem("wi_ready")
        qiT_ready, kiT_ready, qT_ready, kT_ready, val_ready = (sem(n) for n in ("qiT_ready", "kiT_ready", "qT_ready", "kT_ready", "val_ready"))
        gaT_ready, z_in, zexp_ready, b_ready = (sem(n) for n in ("gaT_ready", "z_in", "zexp_ready", "b_ready"))
        relu_ready, relu_used, mask_ready, causal_ready = (sem(n) for n in ("relu_ready", "relu_used", "mask_ready", "causal_ready"))
        s_masked, p_exp, p_ready, p_used = (sem(n) for n in ("s_masked", "p_exp", "p_ready", "p_used"))
        pT_ready, ob_ready = [sem("pT_ready0"), sem("pT_ready1")], sem("ob_ready")
        gqk_ready, gv_ready, gs_in, gs_ready = (sem(n) for n in ("gqk_ready", "gv_ready", "gs_in", "gs_ready"))
        ex_in, ex_exp, ex_ready, ex_used = (sem(n) for n in ("ex_in", "ex_exp", "ex_ready", "ex_used"))
        kN_ready, sc_ready, state_ready, oss_ready, oms_ready, osq_ready, oan_ready, oa_ready = (
            sem(n) for n in ("kN_ready", "sc_ready", "state_ready", "oss_ready", "oms_ready", "osq_ready", "oan_ready", "oa_ready"))
        sig_ready, mix_ready = sem("sig_ready"), sem("mix_ready")
        mixT_ready = [sem("mixT_act"), sem("mixT_dve")]
        h2T_ready = [sem("h2T_dve"), sem("h2T_act")]
        h2g_ready = [sem("h2g_dve"), sem("h2g_act")]
        gd_ready, gm_ready = sem("gd_ready"), sem("gm_ready")
        ld_xr, xr_used = [sem("ld_xr0"), sem("ld_xr1")], sem("xr_used")
        rss_ready, rms_ready, rsq_ready, x1_ready, xss_ready, xms_ready, xsq_ready, xn2_ready = (
            sem(n) for n in ("rss_ready", "rms_ready", "rsq_ready", "x1_ready", "xss_ready", "xms_ready", "xsq_ready", "xn2_ready"))
        xn2_stored = [sem("xn2_stored0"), sem("xn2_stored1")]
        lg_ready, ge_in, ge_out, em_ready, pos_ready, route_ready = (
            sem(n) for n in ("lg_ready", "ge_in", "ge_out", "em_ready", "pos_ready", "route_ready"))
        slot_zeroed, slot_set, slot_in, slot_cast, slot_ready = (sem(n) for n in ("slot_zeroed", "slot_set", "slot_in", "slot_cast", "slot_ready"))
        we_in, we_used = [sem("we_in0"), sem("we_in1")], sem("we_used")
        xg_in, idx_set, silu_ready, act_ready, actT_ready, yb_ready = (
            sem(n) for n in ("xg_in", "idx_set", "silu_ready", "act_ready", "actT_ready", "yb_ready"))
        y_stored = [sem("y_stored0"), sem("y_stored1")]
        yc_in, fss_ready, fms_ready, fsq_ready, fin_ready, out_done = (
            [sem("yc_in0"), sem("yc_in1")], sem("fss_ready"), sem("fms_ready"), sem("fsq_ready"), sem("fin_ready"), sem("out_done"))
        dstep, pstep, fin_y, h2m_ready, gf_ready = (sem(n) for n in ("dstep", "pstep", "fin_y", "h2m_ready", "gf_ready"))
        sin_in2, c32_ready, lnv_ready, lnq_ready, pstep_const = (sem(n) for n in ("sin_in2", "c32_ready", "lnv_ready", "lnq_ready", "pstep_const"))
        fsq_in, ov_zero, ov_filled, idx_seen = sem("fsq_in"), sem("ov_zero"), sem("ov_filled"), sem("idx_seen")
        where, moe_base = {}, {}

        block = ctx.enter_context(nc.Block())

        items = [("ada", 0, q) for q in range(4)]
        items += [("in", O_IQ), ("in", O_DK), ("in", O_DQ), ("in", O_DV), ("in", O_GQ), ("in", O_GV), ("in", O_GG)]
        items += [("ada", 1, q) for q in range(4)] + [("ada", 2, q) for q in range(4)]
        items += [("in", O_BG), ("in", O_BG + D), ("proj", 0), ("in", O_BG + 512), ("in", O_BG + D + 512), ("proj", 1)]
        items += [("out", 0), ("out", 1)]
        item_at = {it: n for n, it in enumerate(items)}

        def slot_of(it):
            return ring[:, item_at[it] % 4, :]

        def ring_wait(eng, it):
            n = item_at[it]
            extra = sum(1 for m, o in enumerate(items[:n + 1]) if m % 4 == n % 4 and o[0] == "proj")
            eng.wait_ge(ring_in[n % 4], 16 * (n // 4 + 1 + extra))

        def filled(eng, turn, name=None):
            name = name or where[turn]
            eng.wait_ge(bank[name].full, bank[name].at[turn] + 1)
            return ps[name], bank[name].free

        @block.tensor
        def _(pe):
            def take(name, turn):
                n = bank[name].turn(turn)
                if n:
                    pe.wait_ge(bank[name].free, n)
                return ps[name]

            flip = {"T": 0, "A": 0}

            def take_next(kind, turn):
                name = f"{kind}{flip[kind] % 2}"
                flip[kind] += 1
                where[turn] = name
                return take(name, turn), bank[name].full

            pe.wait_ge(const_ready, 1)
            pe.wait_ge(ld_vec, 16 * 6)
            t, full = take_next("T", "vec")
            nc.tensor.transpose(t[:, 0:42], vrows[:, :], ident[0:42, 0:42]).then_inc(full, 1)
            pe.wait_ge(const_ready, 2)
            pe.wait_ge(ld_rows, 16 * 4)
            g = take("G", "rows")
            nc.tensor.matmul(g[:, 0:228], ones[0:1, :], rows[:, :], start=True, stop=True).then_inc(bank["G"].full, 1)
            for k in range(KD):
                t, full = take_next("T", ("x", k))
                for tt in range(TT):
                    if k == 0:
                        pe.wait_ge(xn_ready, tt + 1)
                    last = nc.tensor.transpose(t[:, tt * P:(tt + 1) * P], x_in[:, tt, k * P:(k + 1) * P], ident[:, :])
                last.then_inc(full, 1)

            def ada(grp):
                if grp == 0:
                    pe.wait_ge(c32_ready, 1)
                a, full = take_next("A", ("ada", grp))
                for k in range(KD):
                    it = ("ada", grp, k // 2)
                    if k % 2 == 0:
                        ring_wait(pe, it)
                    w = slot_of(it).rearrange("p (k n) -> p k n", k=2)
                    for j in range(4):
                        last = nc.tensor.matmul(a[32 * j:32 * j + 32, :], c32[:, k, :], w[:, k % 2, j * 512:(j + 1) * 512],
                                                start=(k == 0), stop=(k == KD - 1))
                    if k % 2 == 1:
                        last.then_inc(ring_out, 1)
                pe.wait_ge(ring_out, item_at[("ada", grp, 3)] + 1)
                pe.sem_inc(full, 1)

            def ada_turn(grp):
                pe.wait_ge(m16_ready, grp + 1)
                t, full = take_next("T", ("mod", grp))
                nc.tensor.transpose(t[:, 0:16], m16[:, grp, :], ident[0:16, 0:16]).then_inc(full, 1)

            ada(0)
            ada_turn(0)

            def inproj(it, tt, ncols=512, release=False):
                ring_wait(pe, it)
                a, full = take_next("A", (it, tt))
                w = slot_of(it).rearrange("p (k n) -> p k n", k=KD)
                for k in range(KD):
                    if tt == 0 and it == ("in", O_IQ):
                        pe.wait_ge(h_ready, k + 1)
                    last = nc.tensor.matmul(a[:, :], hT[:, k, tt * P:(tt + 1) * P], w[:, k, :], start=(k == 0), stop=(k == KD - 1))
                last.then_inc(full, 1)
                if tt == TT - 1:
                    pe.wait_ge(full, bank[where[(it, tt)]].at[(it, tt)] + 1)
                    pe.sem_inc(ring_out, 1)

            def inproj_T(it, cb):
                ring_wait(pe, it)
                a, full = take_next("A", (it, cb))
                w = slot_of(it).rearrange("p (k n) -> p k n", k=KD)
                for k in range(KD):
                    last = nc.tensor.matmul(a[:, :], w[:, k, cb * P:(cb + 1) * P], hT[:, k, :], start=(k == 0), stop=(k == KD - 1))
                last.then_inc(full, 1)
                if cb == 3:
                    pe.wait_ge(full, bank[where[(it, cb)]].at[(it, cb)] + 1)
                    pe.sem_inc(ring_out, 1)

            nstage = [0]

            def turn_stage(what, tt):
                pe.wait_ge(stage_roped, nstage[0] + 1)
                t, full = take_next("T", (what, tt))
                for cb in range(4):
                    last = nc.tensor.transpose(t[:, cb * P:(cb + 1) * P], stage[:, nstage[0] % 4, cb * P:(cb + 1) * P], ident[:, :])
                last.then_inc(full, 1)
                nstage[0] += 1

            for tt in range(TT):
                inproj(("in", O_IQ), tt)
            pe.wait_ge(ld_small, 32)
            for tt in range(TT):
                a, full = take_next("A", ("small", tt))
                for k in range(KD):
                    last = nc.tensor.matmul(a[:, 0:NS], hT[:, k, tt * P:(tt + 1) * P], w_small[:, k, :], start=(k == 0), stop=(k == KD - 1))
                last.then_inc(full, 1)
            for tt in range(TT):
                inproj(("in", O_DK), tt)
                turn_stage("iq", tt)
            pe.wait_ge(ki_ready, 1)
            t, full = take_next("T", "ki")
            for tt in range(TT):
                last = nc.tensor.transpose(t[:, tt * P:(tt + 1) * P], kin[:, tt, :, :].rearrange("p a n -> p (a n)"), ident[:, :])
            last.then_inc(full, 1)
            t, full = take_next("T", "ga")
            for tt in range(TT):
                last = nc.tensor.transpose(t[0:RANK, tt * P:(tt + 1) * P], ikw[:, tt, 0:RANK], ident[:, :])
            last.then_inc(full, 1)

            def index_scores(tq, hp):
                n = (tq + 1) * P
                if (tq, hp) == (1, 0):
                    pe.wait_ge(kiT_ready, 1)
                    pe.wait_ge(qiT_ready, TT)
                for hh in range(2):
                    s = take(f"S{hh}", ("idx", tq, hp))
                    nc.tensor.matmul(s[:, 0:n], qiT[64 * hh:64 * hh + 64, hp, tq * P:(tq + 1) * P], kiT[64 * hh:64 * hh + 64, 0:n],
                                     start=True, stop=True).then_inc(bank[f"S{hh}"].full, 1)

            fill = [lambda tt=tt: (inproj(("in", O_DQ), tt), turn_stage("dk", tt)) for tt in range(TT)]
            fill += [lambda tt=tt: (inproj(("in", O_DV), tt), turn_stage("dq", tt)) for tt in range(TT)]
            for n in range(3 * PAIRS):
                index_scores(1 + n // PAIRS, n % PAIRS)
                if n == 1:
                    pe.wait_ge(gaT_ready, 1)
                    pe.wait_ge(ld_a2, 16)
                    for r, name in enumerate(("G", "O")):
                        z = take(name, ("z", r))
                        nc.tensor.matmul(z[:, :], a2[:, r * P:(r + 1) * P], gaT[:, :], start=True, stop=True).then_inc(bank[name].full, 1)
                if n % 3 != 1:
                    fill.pop(0)()

            def attn_scores(u):
                tq, hp = u // PAIRS, u % PAIRS
                n = (tq + 1) * P
                if u == 0:
                    pe.wait_ge(kT_ready, TT)
                    pe.wait_ge(qT_ready, TT)
                for hh in range(2):
                    s = take(f"S{hh}", ("att", u))
                    nc.tensor.matmul(s[:, 0:n], qT[64 * hh:64 * hh + 64, hp, tq * P:(tq + 1) * P], kT[64 * hh:64 * hh + 64, hp, 0:n],
                                     start=True, stop=True).then_inc(bank[f"S{hh}"].full, 1)

            def attn_out(u):
                tq, hp = u // PAIRS, u % PAIRS
                for hh in range(2):
                    pe.wait_ge(p_ready, 2 * u + hh + 1)
                    t, full = take_next("T", ("p", u, hh))
                    for kb in range(tq + 1):
                        last = nc.tensor.transpose(t[:, kb * P:(kb + 1) * P], prob[:, u % 2, hh, kb * P:(kb + 1) * P], ident[:, :])
                    last.then_inc(full, 1)
                if u == 0:
                    pe.wait_ge(val_ready, TT)
                o = take("O", ("att", u))
                for kb in range(tq + 1):
                    for hh in range(2):
                        if kb == 0:
                            pe.wait_ge(pT_ready[hh], u + 1)
                        last = nc.tensor.matmul(o[64 * hh:64 * hh + 64, 0:P], val[:, kb, (2 * hp + hh) * HD:(2 * hp + hh + 1) * HD],
                                                probT[:, u % 2, hh, kb * P:(kb + 1) * P], start=(kb == 0), stop=(kb == tq))
                last.then_inc(bank["O"].full, 1)

            fill = [lambda cb=cb: inproj_T(("in", O_GQ), cb) for cb in range(4)]
            fill += [lambda tt=tt: inproj(("in", O_GV), tt) for tt in range(TT)]
            fill += [lambda tt=tt: inproj(("in", O_GG), tt) for tt in range(TT)]
            fill += [lambda: ada(1), lambda: (ada_turn(1), ada(2)), lambda: ada_turn(2)]
            for u in range(TT * PAIRS + 1):
                if u < TT * PAIRS:
                    attn_scores(u)
                if fill:
                    fill.pop(0)()
                if u:
                    attn_out(u - 1)

            fill = [lambda ab=ab, tt=tt: inproj(("in", O_BG + ab * D), tt) for ab in range(2) for tt in range(TT)]

            def gla_scores(ch):
                pe.wait_ge(ex_ready, ch + 1)
                t, full = take_next("T", ("kN", ch))
                for r in range(2):
                    last = nc.tensor.transpose(t[:, r * P:(r + 1) * P], expo[:, r, 768:896], ident[:, :])
                last.then_inc(full, 1)
                sc = [take(n, ("sc", ch)) for n in ("G", "O")]
                for r in range(2):
                    for i in range(NB):
                        for hh in range(2):
                            lo = 64 * hh
                            last = nc.tensor.matmul(sc[hh][:, r * P + i * BLK:r * P + (i + 1) * BLK], expo[lo:lo + 64, r, i * P:(i + 1) * P],
                                                    expo[lo:lo + 64, r, 512 + i * BLK:512 + (i + 1) * BLK], start=True, stop=True)
                            if r == 1 and i == NB - 1:
                                last.then_inc(bank["GO"[hh]].full, 1)

            def gla_out(ch):
                pe.wait_ge(sc_ready, 2 * ch + 2)
                pe.wait_ge(gv_ready, TT)
                o = [take(n, ("o", ch)) for n in ("G", "O")]
                if ch:
                    pe.wait_ge(state_ready, 2 * ch)
                for r in range(2):
                    for hh in range(2):
                        h, lo = 2 * r + hh, 64 * hh
                        if ch:
                            nc.tensor.matmul(o[hh][:, r * P:(r + 1) * P], expo[lo:lo + 64, r, 640:768], state[lo:lo + 64, r, :], start=True, stop=False)
                        last = nc.tensor.matmul(o[hh][:, r * P:(r + 1) * P], scT[:, h, :], gv[:, ch, h * P:(h + 1) * P], start=(ch == 0), stop=True)
                        if r == 1:
                            last.then_inc(bank["GO"[hh]].full, 1)
                if ch < TT - 1:
                    pe.wait_ge(kN_ready, ch + 1)
                    t, full = take_next("T", ("state", ch))
                    for r in range(2):
                        for hh in range(2):
                            h = 2 * r + hh
                            last = nc.tensor.matmul(t[64 * hh:64 * hh + 64, r * P:(r + 1) * P], kN[:, r * P + 64 * hh:r * P + 64 * hh + 64],
                                                    gv[:, ch, h * P:(h + 1) * P], start=True, stop=True)
                    last.then_inc(full, 1)

            def gla_turn(ch):
                pe.wait_ge(oan_ready, 4 * (ch + 1))
                t, full = take_next("T", ("oa", ch))
                for h in range(GLA_H):
                    last = nc.tensor.transpose(t[:, h * P:(h + 1) * P], oan[:, h * P:(h + 1) * P], ident[:, :])
                last.then_inc(full, 1)

            for ch in range(TT):
                gla_scores(ch)
                fill.pop(0)()
                gla_out(ch)
                fill.pop(0)()
                gla_turn(ch)

            def gate_rows(which, tag):
                pe.wait_ge(gd_ready, which + 1)
                for n, name in enumerate(("G", "O")):
                    g = take(name, (tag, n))
                    nc.tensor.matmul(g[:, :], ones[:, :], diag[:, which, n * 512:(n + 1) * 512], start=True, stop=True).then_inc(bank[name].full, 1)

            gate_rows(0, "gm")

            def branches(n, tt):
                ring_wait(pe, ("proj", n))
                w = slot_of(("proj", n)).rearrange("p (b k n) -> p b k n", b=2, k=4)
                for b, src in enumerate((gqk, qT)):
                    if n == 0 and tt == 0:
                        pe.wait_ge(oa_ready if b == 0 else ob_ready, TT if b == 0 else TT * PAIRS)
                    a, full = take_next("A", ("y", n, tt, b))
                    for k in range(4):
                        last = nc.tensor.matmul(a[:, :], src[:, k, tt * P:(tt + 1) * P], w[:, b, k, :], start=(k == 0), stop=(k == 3))
                    last.then_inc(full, 1)
                if tt == TT - 1:
                    pe.wait_ge(full, bank[where[("y", n, tt, 1)]].at[("y", n, tt, 1)] + 1)
                    pe.sem_inc(ring_out, 1)

            for tt in range(TT):
                branches(0, tt)
            for ab in range(2):
                for tt in range(TT):
                    inproj(("in", O_BG + ab * D + 512), tt)
            for tt in range(TT):
                branches(1, tt)

            def out_proj(tt):
                for half in range(2):
                    if half == 0:
                        pe.wait_ge(mix_ready, TT + tt + 1)
                    t, full = take_next("T", ("mix", tt, half))
                    for q in range(4):
                        k = 4 * half + q
                        last = nc.tensor.transpose(t[:, q * P:(q + 1) * P], mix[:, tt, k * P:(k + 1) * P], ident[:, :])
                    last.then_inc(full, 1)
                for n in range(2):
                    ring_wait(pe, ("out", n))
                    w = slot_of(("out", n)).rearrange("p (k n) -> p k n", k=KD)
                    a, full = take_next("A", ("out", tt, n))
                    for k in range(KD):
                        if n == 0 and k == 0:
                            pe.wait_ge(mixT_ready[0], tt + 1)
                            pe.wait_ge(mixT_ready[1], tt + 1)
                        last = nc.tensor.matmul(a[:, :], mixT[:, tt % 2, k, :], w[:, k, :], start=(k == 0), stop=(k == KD - 1))
                    last.then_inc(full, 1)
                if tt == TT - 1:
                    pe.wait_ge(full, bank[where[("out", tt, 1)]].at[("out", tt, 1)] + 1)
                    pe.sem_inc(ring_out, 2)

            def router(tt):
                pe.wait_ge(xn2_ready, tt + 1)
                for half in range(2):
                    t, full = take_next("T", ("x2", tt, half))
                    for q in range(4):
                        k = 4 * half + q
                        last = nc.tensor.transpose(t[:, q * P:(q + 1) * P], xn2[:, tt % 2, k * P:(k + 1) * P], ident[:, :])
                    last.then_inc(full, 1)
                for half in range(2):
                    pe.wait_ge(h2T_ready[half], 4 * (tt + 1))
                pe.wait_ge(ld_rt, 32)
                g = take("G", ("lg", tt))
                for k in range(KD):
                    last = nc.tensor.matmul(g[:, 0:GROUPS + NE], h2T[:, tt % 2, k, :], w_rt[:, k, :], start=(k == 0), stop=(k == KD - 1))
                last.then_inc(bank["G"].full, 1)

            for tt in range(TT + 1):
                if tt < TT:
                    out_proj(tt)
                if tt:
                    router(tt - 1)

            pe.wait_ge(em_ready, 1)
            g = take("G", "rank")
            for tt in range(TT):
                for i in range(tt + 1):
                    last = nc.tensor.matmul(g[:, tt * NE:(tt + 1) * NE], (before if i == tt else ones)[:, :], em[:, i, :], start=(i == 0), stop=(i == tt))
            last.then_inc(bank["G"].full, 1)
            o = take("O", "count")
            for i in range(TT):
                last = nc.tensor.matmul(o[:, 0:NE], ones[:, :], em[:, i, :], start=(i == 0), stop=(i == TT - 1))
            last.then_inc(bank["O"].full, 1)
            gate_rows(1, "gf")
            pe.wait_ge(slot_cast, 1)
            g = take("G", "slots")
            nc.tensor.transpose(g[:, 0:NPALL], slot_f[:, :], ident[0:NPALL, 0:NPALL]).then_inc(bank["G"].full, 1)

            base = {n: len(b.at) for n, b in bank.items()}
            moe_base.update(base)

            def pair(j, b, i):
                w0, w1 = (wexp[:, 2 * (1 - b) + q, :] for q in range(2))
                pe.wait_ge(xg_in, 16 * (j + 1))
                for half in range(2):
                    name = f"T{half}"
                    pe.wait_ge(bank[name].free, base[name] + j)
                    for q in range(4):
                        k = 4 * half + q
                        last = nc.tensor.transpose(ps[name][:, q * P:(q + 1) * P], xg[:, b, k * P:(k + 1) * P], ident[:, :])
                    last.then_inc(bank[name].full, 1)
                pe.wait_ge(bank["G"].free, base["G"] + j)
                pe.wait_ge(we_in[b], 96 * (i + 1))
                for half in range(2):
                    pe.wait_ge(h2g_ready[half], 4 * j + 4)
                for k in range(KD):
                    for q, w in enumerate((w0, w1)):
                        gu = w[:, 0:4096].rearrange("p (g k f) -> p g k f", g=2, k=KD)[:, :, k, :]
                        last = nc.tensor.matmul(ps["G"][64 * q:64 * q + 64, :].rearrange("p (g f) -> p g f", g=2), h2g[:, b, k, 64 * q:64 * q + 64], gu,
                                                start=(k == 0), stop=(k == KD - 1))
                last.then_inc(bank["G"].full, 1)
                pe.wait_ge(act_ready, j + 1)
                pe.wait_ge(bank["O"].free, base["O"] + j)
                for q in range(2):
                    last = nc.tensor.transpose(ps["O"][:, q * P:(q + 1) * P], aact[:, b, q * P:(q + 1) * P], ident[:, :])
                last.then_inc(bank["O"].full, 1)
                pe.wait_ge(actT_ready, j + 1)
                for n in range(2):
                    name = f"A{n}"
                    pe.wait_ge(bank[name].free, base[name] + j)
                    for kf in range(2):
                        for q, w in enumerate((w0, w1)):
                            wd = w[:, 4096:6144].rearrange("p (k n) -> p k n", k=2)
                            last = nc.tensor.matmul(ps[name][64 * q:64 * q + 64, :], actT[:, b, kf, 64 * q:64 * q + 64],
                                                    wd[:, kf, n * 512:(n + 1) * 512], start=(kf == 0), stop=(kf == 1))
                    last.then_inc(bank[name].full, 1)
                pe.wait_ge(bank["A1"].full, base["A1"] + j + 1)
                pe.sem_inc(we_used, 1)

            with pe.Fori(0, NPAIR // 2) as i:
                pair(2 * i, 0, i)
                pair(2 * i + 1, 1, i)
            pe.wait_ge(route_ready, 1)
            n_ov = pe.value_load(ovi[0:1, NOV:NOV + 1], min_val=0, max_val=NOV // 2)
            with pe.If(n_ov > 0):
                with pe.Fori(0, n_ov) as v:
                    pair(NPAIR + v, 0, NPAIR // 2 + v)

        @block.sync
        def _(sp):
            for tt in range(TT):
                sp.dma_start(x_in[:, tt, :], x_v[:, tt, :]).then_inc(ld_x[tt], 16)
            vecs = (g_pre_mix, g_pre_ffn, g_post_mix, g_post_ffn)
            for n, v in enumerate(vecs):
                sp.dma_start(vrows[8 * n:8 * n + 8, :], v[0].rearrange("(k p) -> k p", p=P)).then_inc(ld_vec, 16)
            sp.dma_start(vrows[32:34, :], b_gla_a[0].rearrange("(k p) -> k p", p=P)).then_inc(ld_vec, 16)
            sp.dma_start(vrows[34:42, :], c[0].rearrange("(k p) -> k p", p=P)).then_inc(ld_vec, 16)

            def load(n):
                it = items[n]
                if n >= 4:
                    sp.wait_ge(ring_out, n - 3)
                dst, s = ring[:, n % 4, :], ring_in[n % 4]
                if it[0] == "ada":
                    grp, q = it[1:]
                    sp.dma_start(dst.rearrange("p (k n) -> p k n", k=2), ada_v[:, 2 * q:2 * q + 2, grp * 2048:(grp + 1) * 2048]).then_inc(s, 16)
                elif it[0] == "in":
                    sp.dma_start(dst.rearrange("p (k n) -> p k n", k=KD), win_v[:, :, it[1]:it[1] + 512]).then_inc(s, 16)
                elif it[0] == "proj":
                    w = dst.rearrange("p (b k n) -> p b k n", b=2, k=4)
                    for b, src in enumerate((pg_v, pd_v)):
                        sp.dma_start(w[:, b, :, :], src[:, :, it[1] * 512:(it[1] + 1) * 512]).then_inc(s, 16)
                else:
                    sp.dma_start(dst.rearrange("p (k n) -> p k n", k=KD), wo_v[:, :, it[1] * 512:(it[1] + 1) * 512]).then_inc(s, 16)

            for n in range(4):
                load(n)
            sp.dma_start(w_small[:, :, 0:RANK], win_v[:, :, O_GA:O_GA + RANK]).then_inc(ld_small, 16)
            sp.dma_start(w_small[:, :, RANK:NS], win_v[:, :, O_IK:O_IK + 72]).then_inc(ld_small, 16)
            sp.dma_start(a2[:, :], w_gla_a2[0]).then_inc(ld_a2, 16)
            sp.dma_start(w_rt[:, :, 0:GROUPS], w_router_g[0].rearrange("(k p) n -> p k n", p=P)).then_inc(ld_rt, 16)
            sp.dma_start(w_rt[:, :, GROUPS:], w_router_e[0].rearrange("(k p) n -> p k n", p=P)).then_inc(ld_rt, 16)
            for n in range(4, len(items)):
                load(n)

            def experts(b, e0, e1_):
                for q, e in enumerate((e0, e1_)):
                    w = wexp[:, 2 * (1 - b) + q, :]
                    for dst, src, kk in ((w[:, 0:2048], weg_v, KD), (w[:, 2048:4096], weu_v, KD), (w[:, 4096:6144], wed_v, 2)):
                        sp.dma_start(dst.rearrange("p (k f) -> p k f", k=kk), src[bass.ds(e, 1), :, :, :].rearrange("a p k f -> p (a k) f")).then_inc(we_in[b], 16)

            sp.wait_ge(ring_out, item_at[("in", O_BG + D + 512)] + 1)
            sp.wait_ge(bank["O"].full, bank["O"].at[("att", TT * PAIRS - 1)] + 1)
            experts(0, 0, 1)
            sp.wait_ge(ring_out, len(items))
            experts(1, 2, 3)
            with sp.Fori(1, NPAIR // 2) as i:
                sp.wait_ge(we_used, 2 * i - 1)
                experts(0, 4 * i, 4 * i + 1)
                sp.wait_ge(we_used, 2 * i)
                experts(1, 4 * i + 2, 4 * i + 3)
            sp.wait_ge(route_ready, 1)
            n_ov = sp.value_load(ovi[0:1, NOV:NOV + 1], min_val=0, max_val=NOV // 2)
            with sp.If(n_ov > 0):
                with sp.Fori(0, n_ov) as v:
                    e_a = sp.value_load(ovi[0:1, bass.ds(2 * v, 1)], min_val=0, max_val=NE - 1)
                    e_b = sp.value_load(ovi[0:1, bass.ds(2 * v + 1, 1)], min_val=0, max_val=NE - 1)
                    sp.wait_ge(we_used, NPAIR + v)
                    experts(0, e_a, e_b)
            for tt in range(TT):
                sp.wait_ge(fin_ready, tt + 1)
                sp.dma_start(out_v[:, tt, :], x1[:, tt, :]).then_inc(out_done, 16)
            sp.wait_ge(out_done, 16 * TT)

        @block.gpsimd
        def _(pool):
            def step(ins):
                pstep_n[0] += 1
                ins.then_inc(pstep, 1)
                pool.wait_ge(pstep, pstep_n[0])

            pstep_n = [0]
            pool.dma_start(posi[:, :], positions[0].rearrange("(t p) -> p t", p=P), allow_slow_non_contiguous=True).then_inc(ld_pos, 16)
            pool.dma_start(rows[:, 0:128], g_gla_out).then_inc(ld_rows, 16)
            pool.dma_start(rows[:, 128:192], g_idx_k).then_inc(ld_rows, 16)
            pool.dma_start(rows[:, 192:196], b_router_g).then_inc(ld_rows, 16)
            pool.dma_start(rows[:, 196:228], b_router_e).then_inc(ld_rows, 16)
            pool.dma_start(bada[:, :, :], b_ada[0].rearrange("(g r p) -> r g p", r=16, p=P)).then_inc(ld_bada, 16)
            step(pool.memset(ident[:, :], 0.0))
            pool.affine_select(out=ident[:, :], in_=ident[:, :], compare_op=ALU.not_equal, fill=1.0, base=0,
                               pattern=[[-1, P]], channel_multiplier=1).then_inc(const_ready, 1)
            pool.memset(ones[:, :], 1.0).then_inc(const_ready, 1)
            pool.wait_ge(const_ready, 2)
            step(pool.affine_select(out=before[:, :], in_=ones[:, :], compare_op=ALU.is_gt, fill=0.0, base=0,
                                    pattern=[[1, P]], channel_multiplier=-1))
            step(pool.affine_select(out=upto[:, :], in_=ones[:, :], compare_op=ALU.is_ge, fill=0.0, base=0,
                                    pattern=[[1, P]], channel_multiplier=-1))
            step(pool.memset(causal0[:, :], 0.0))
            step(pool.affine_select(out=causal0[:, :], in_=causal0[:, :], compare_op=ALU.is_ge, fill=HIDE, base=0,
                                    pattern=[[-1, P]], channel_multiplier=1))
            step(pool.iota(iota[:, :], pattern=[[1, NE]], base=0, channel_multiplier=0))
            step(pool.iota(tokid[:, :], pattern=[[P, TT]], base=0, channel_multiplier=1))
            step(pool.memset(zero_i[:, :], 0))
            pool.dma_start(slot_dram.rearrange("(j p) a -> j (p a)", p=P), zero_i[:, :]).then_inc(slot_zeroed, 16)
            pool.memset(gp[:, :, :], HIDE).then_inc(const_ready, 1)
            pool.sem_inc(pstep_const, 1)

            def rotate(xv, cosv, sinv, nsinv, tmp):
                step(pool.tensor_tensor(tmp[..., 0:HALF], xv[..., HALF:ROT], nsinv, ALU.mult))
                step(pool.tensor_tensor(tmp[..., HALF:ROT], xv[..., 0:HALF], sinv, ALU.mult))
                step(pool.tensor_tensor(xv[..., 0:HALF], xv[..., 0:HALF], cosv, ALU.mult))
                step(pool.tensor_tensor(xv[..., HALF:ROT], xv[..., HALF:ROT], cosv, ALU.mult))
                return pool.tensor_tensor(xv[..., 0:ROT], xv[..., 0:ROT], tmp[..., 0:ROT], ALU.add)

            pool.wait_ge(rope_ready, 1)

            def rope_stage(n):
                pool.wait_ge(stage_in, n + 1)
                if n:
                    pool.wait_ge(stage_roped, n)
                tt = n % TT
                xv = stage[:, n % 4, :].rearrange("p (h d) -> p h d", h=HEADS)
                cs_, sn_, ns_ = (v.unsqueeze(1).broadcast_to([P, HEADS, HALF]) for v in (rope[:, 2, tt, :], rope[:, 3, tt, :], nsin[:, tt, :]))
                rotate(xv, cs_, sn_, ns_, rtmp[:, :, :]).then_inc(stage_roped, 1)

            for n in range(3 * TT):
                rope_stage(n)
            pool.wait_ge(slot_zeroed, 16)
            pool.wait_ge(pos_ready, 1)
            for tt in range(TT):
                for w in range(2):
                    pool.indirect_dma_start(out=slot_dram, out_offset=bass.IndirectOffsetOnAxis(ap=slotpos[:, tt, w:w + 1], axis=0),
                                            in_=tokid[:, tt:tt + 1].bitcast(U32), in_offset=None).then_inc(slot_set, 16)
            pool.wait_ge(slot_set, 16 * 2 * TT)
            pool.dma_start(slot_r[:, :], slot_dram.rearrange("(j p) a -> j (p a)", p=P)).then_inc(slot_in, 16)
            pool.wait_ge(slot_ready, 1)
            for b in range(2):
                pool.wait_ge(xn2_stored[b], 32)

            def gather(j, b, back):
                if back is not None:
                    pool.wait_ge(bank["T1"].full, moe_base["T1"] + back)
                    pool.wait_ge(idx_set, back)
                pool.tensor_copy(slot_c[:, b:b + 1], slot_i[:, bass.ds(j, 1)]).then_inc(idx_set, 1)
                pool.wait_ge(idx_set, j + 1)
                pool.sem_inc(idx_seen, 1)
                pool.indirect_dma_start(out=xg[:, b, :], out_offset=None, in_=xn_dram,
                                        in_offset=bass.IndirectOffsetOnAxis(ap=slot_c[:, b:b + 1], axis=0)).then_inc(xg_in, 16)

            gather(0, 0, None)
            pool.wait_ge(xg_in, 16)
            gather(1, 1, None)
            pool.wait_ge(xg_in, 32)
            with pool.Fori(1, NPAIR // 2) as i:
                gather(2 * i, 0, 2 * i - 1)
                pool.wait_ge(xg_in, 16 * (2 * i + 1))
                gather(2 * i + 1, 1, 2 * i)
                pool.wait_ge(xg_in, 16 * (2 * i + 2))
            n_ov = pool.value_load(ovi[0:1, NOV:NOV + 1], min_val=0, max_val=NOV // 2)

            def combine(rows_):
                for b in range(2):
                    pool.wait_ge(y_stored[b], 16 * NPAIR // 2)
                pool.wait_ge(we_used, NPAIR)
                for tt in range(TT):
                    if tt >= 2:
                        pool.wait_ge(fin_y, tt - 1)
                    for w in range(2):
                        pool.indirect_dma_start(out=yc[:, tt % 2, w, :], out_offset=None, in_=rows_,
                                                in_offset=bass.IndirectOffsetOnAxis(ap=slotpos[:, tt, w:w + 1], axis=0)).then_inc(yc_in[tt % 2], 16)

            with pool.If(n_ov > 0):
                pool.memset(stage_mem[:, :], 0.0).then_inc(ov_zero, 1)
                pool.wait_ge(ov_zero, 1)
                pool.dma_start(y_dram[NPAIR * P:, :].rearrange("(p j) n -> p (j n)", p=P).rearrange("p (a n) -> p a n", a=NOV // 4),
                               stage_mem[:, :].unsqueeze(1).broadcast_to([P, NOV // 4, 2 * D])).then_inc(ov_filled, 16)
                pool.wait_ge(ov_filled, 16)
                with pool.Fori(0, n_ov) as v:
                    gather(NPAIR + v, 0, NPAIR + v)
                    pool.wait_ge(xg_in, 16 * (NPAIR + v + 1))
                    pool.wait_ge(y_stored[0], 16 * (NPAIR // 2 + v + 1))
                combine(y_dram)
            with pool.Else():
                combine(y_dram[0:NPAIR * P, :])

        @block.scalar
        def _(act):
            scratch = prob[:, 0, :, :].rearrange("p h n -> p (h n)")
            for tt in range(TT):
                act.wait_ge(ld_x[tt], 16)
                nc.scalar.activation(scratch[:, 0:D], x_in[:, tt, :], ACT.Square, accum_out=st[:, tt:tt + 1]).then_inc(ss_ready, 1)
                act.wait_ge(ss_ready, tt + 1)
            act.wait_ge(rs_ready, 1)
            nc.scalar.activation(st[:, 8:12], st[:, 4:8], ACT.Sqrt).then_inc(ss_ready, 1)
            act.wait_ge(vT_ready, 1)
            nc.scalar.activation(cs[:, :], vT[:, 34:42], ACT.Sigmoid).then_inc(c_ready, 1)
            act.wait_ge(sin_in, 1)
            nc.scalar.activation(rope[:, 3, :, :], rope[:, 0, :, :], ACT.Sin).then_inc(sin_out, 1)
            nc.scalar.activation(rope[:, 2, :, :], rope[:, 0, :, :], ACT.Sin, scale=0.5).then_inc(sin_out, 1)
            for k in range(0, KD, 2):
                t, free = filled(act, ("x", k))
                nc.scalar.copy(hT[:, k, :], t[:, :]).then_inc(free, 1)
                act.wait_ge(free, bank[where[("x", k)]].at[("x", k)] + 1)
                act.sem_inc(hraw, 1)

            def mod_row(grp):
                a, free = filled(act, ("ada", grp))
                if grp:
                    act.wait_ge(m16_in, 16 * grp)
                nc.scalar.copy(mrow[:, :], a[:, :]).then_inc(free, 1)
                act.wait_ge(free, bank[where[("ada", grp)]].at[("ada", grp)] + 1)
                act.dma_start(m16[:, grp, :], mrow[0:P:32, :]).then_inc(m16_in, 16)

            mod_row(0)

            nst = [0]

            def to_stage(turn):
                a, free = filled(act, turn)
                n = nst[0]
                if n >= 4:
                    filled(act, stage_turns[n - 4])
                nc.scalar.copy(stage[:, n % 4, :], a[:, :]).then_inc(stage_in, 1)
                act.wait_ge(stage_in, n + 1)
                act.sem_inc(free, 1)
                nst[0] += 1

            stage_turns = [("iq", t) for t in range(TT)] + [("dk", t) for t in range(TT)] + [("dq", t) for t in range(TT)]

            def spread(turn, dst, done):
                t, free = filled(act, turn)
                nc.scalar.copy(dst, t[:, :].rearrange("p (c n) -> p c n", c=4)).then_inc(done, 1)
                act.wait_ge(done, spread_n.setdefault(done.name, 0) + 1)
                spread_n[done.name] += 1
                act.sem_inc(free, 1)

            spread_n = {}
            for tt in range(TT):
                to_stage((("in", O_IQ), tt))
            for tt in range(TT):
                a, free = filled(act, ("small", tt))
                nc.scalar.copy(ikw[:, tt, :], a[:, 0:NS]).then_inc(ikw_in, 1)
                act.wait_ge(ikw_in, tt + 1)
                act.sem_inc(free, 1)
            act.wait_ge(lnv_ready, 1)
            nc.scalar.activation(st[:, 56:60], st[:, 52:56], ACT.Sqrt).then_inc(lnq_ready, 1)
            for tt in range(TT):
                spread(("iq", tt), qiT[:, :, tt * P:(tt + 1) * P], qiT_ready)
                to_stage((("in", O_DK), tt))
            t, free = filled(act, "ki")
            nc.scalar.copy(kiT[:, :], t[:, :]).then_inc(kiT_ready, 1)
            act.wait_ge(kiT_ready, 1)
            act.sem_inc(free, 1)
            t, free = filled(act, "ga")
            nc.scalar.copy(gaT[:, :], t[0:RANK, :]).then_inc(gaT_ready, 1)
            act.wait_ge(gaT_ready, 1)
            act.sem_inc(free, 1)

            def do_dq(tt):
                spread(("dk", tt), kT[:, :, tt * P:(tt + 1) * P], kT_ready)
                to_stage((("in", O_DQ), tt))

            def do_dv(tt):
                spread(("dq", tt), qT[:, :, tt * P:(tt + 1) * P], qT_ready)
                a, free = filled(act, (("in", O_DV), tt))
                nc.scalar.copy(val[:, tt, :], a[:, :]).then_inc(val_ready, 1)
                act.wait_ge(val_ready, tt + 1)
                act.sem_inc(free, 1)

            fill = [lambda tt=tt: do_dq(tt) for tt in range(TT)] + [lambda tt=tt: do_dv(tt) for tt in range(TT)]
            for n in range(3 * PAIRS):
                tq, hp = 1 + n // PAIRS, n % PAIRS
                w = (tq + 1) * P
                for hh in range(2):
                    s, free = filled(act, ("idx", tq, hp), f"S{hh}")
                    if n:
                        act.wait_ge(relu_used, 2 * (n - 1) + hh + 1)
                    nc.scalar.activation(relu[:, hh, 0:w], s[:, 0:w], ACT.Relu, scale=64 ** -0.5).then_inc(relu_ready, 1)
                    act.wait_ge(relu_ready, 2 * n + hh + 1)
                    act.sem_inc(free, 1)
                if n == 6:
                    act.wait_ge(z_in, 1)
                    nc.scalar.activation(zz[:, 1, :, :], zz[:, 1, :, :], ACT.Exp).then_inc(zexp_ready, 1)
                    act.wait_ge(zexp_ready, 1)
                    nc.scalar.activation(zz[:, 2, :, :], zz[:, 1, :, :], ACT.Ln, bias=1.0).then_inc(zexp_ready, 1)
                if n % 3 != 1:
                    fill.pop(0)()

            def simple(turn, dst, done, count, **kw):
                a, free = filled(act, turn)
                nc.scalar.activation(dst, a[:, :], kw.get("func", ACT.Copy), scale=kw.get("scale", 1.0)).then_inc(done, 1)
                act.wait_ge(done, count)
                act.sem_inc(free, 1)

            fill = [lambda cb=cb: simple((("in", O_GQ), cb), gqk[:, cb, :], gqk_ready, cb + 1, scale=GLA_DK ** -0.5 if cb < 2 else 1.0) for cb in range(4)]
            fill += [lambda tt=tt: simple((("in", O_GV), tt), gv[:, tt, :], gv_ready, tt + 1) for tt in range(TT)]
            fill += [lambda tt=tt: simple((("in", O_GG), tt), gs[:, tt, :], gs_in, tt + 1) for tt in range(TT)]
            fill += [lambda: mod_row(1), lambda: mod_row(2), lambda: None]
            for u in range(TT * PAIRS + 1):
                tq, hp = u // PAIRS, u % PAIRS
                n = (tq + 1) * P
                if u < TT * PAIRS:
                    for hh in range(2):
                        act.wait_ge(s_masked, 2 * u + hh + 1)
                        z = 4 * (u % 2)
                        nc.scalar.activation(prob[:, u % 2, hh, 0:n], prob[:, u % 2, hh, 0:n], ACT.Exp, bias=sm[:, hh, z + 1:z + 2],
                                             scale=HD ** -0.5, accum_out=sm[:, hh, z + 2:z + 3]).then_inc(p_exp, 1)
                if fill:
                    fill.pop(0)()
                if u:
                    v = u - 1
                    vq, vp = v // PAIRS, v % PAIRS
                    m = (vq + 1) * P
                    t, free = filled(act, ("p", v, 0))
                    if v >= 2:
                        filled(act, ("att", v - 2), "O")
                    nc.scalar.copy(probT[:, v % 2, 0, 0:m], t[:, 0:m]).then_inc(pT_ready[0], 1)
                    act.wait_ge(pT_ready[0], v + 1)
                    act.sem_inc(free, 1)
                    o, free = filled(act, ("att", v), "O")
                    nc.scalar.copy(qT[:, vp, vq * P:(vq + 1) * P], o[:, 0:P]).then_inc(ob_ready, 1)
                    act.wait_ge(ob_ready, v + 1)
                    act.sem_inc(free, 1)
            nc.scalar.activation(gs[:, :, :], gs[:, :, :], ACT.Silu).then_inc(gs_in, 1)
            scratch = mask_f[:, 0:D]

            def sigmoid(half, ab, tt):
                turn = (("in", O_BG + ab * D + 512 * half), tt)
                if half:
                    act.wait_ge(mix_ready, tt + 1)
                simple(turn, sig[:, ab, tt, :], sig_ready, half * 2 * TT + ab * TT + tt + 1, func=ACT.Sigmoid)

            fill = [lambda ab=ab, tt=tt: sigmoid(0, ab, tt) for ab in range(2) for tt in range(TT)]
            for ch in range(TT):
                act.wait_ge(ex_in, ch + 1)
                nc.scalar.activation(expo[:, :, :], expo[:, :, :], ACT.Exp, scale=1.0 / TAU).then_inc(ex_exp, 1)
                t, free = filled(act, ("kN", ch))
                if 0 < ch:
                    filled(act, ("state", ch - 1))
                nc.scalar.copy(kN[:, :], t[:, 0:256]).then_inc(kN_ready, 1)
                act.wait_ge(kN_ready, ch + 1)
                act.sem_inc(free, 1)
                fill.pop(0)()
                for h in range(GLA_H):
                    o, _ = filled(act, ("o", ch), "GO"[h % 2])
                    r = h // 2
                    nc.scalar.activation(scratch[:, 0:P], o[:, r * P:(r + 1) * P], ACT.Square, accum_out=st[:, 16 + h:17 + h]).then_inc(oss_ready, 1)
                    act.wait_ge(oss_ready, 4 * ch + h + 1)
                act.wait_ge(oms_ready, ch + 1)
                nc.scalar.activation(st[:, 24:28], st[:, 20:24], ACT.Sqrt).then_inc(osq_ready, 1)
                fill.pop(0)()
            filled(act, ("o", TT - 1), "G")
            filled(act, ("o", TT - 1), "O")
            for tt in range(2):
                act.dma_start(xres[:, tt, :], x_v[:, tt, :]).then_inc(ld_xr[tt], 16)
            for ab in range(2):
                for tt in range(TT):
                    sigmoid(1, ab, tt)

            def rms_of(tt):
                for n in range(2):
                    a, _ = filled(act, ("out", tt, n))
                    nc.scalar.activation(scratch[:, 0:512], a[:, :], ACT.Square, accum_out=st[:, 28 + n:29 + n]).then_inc(rss_ready, 1)
                    act.wait_ge(rss_ready, 2 * tt + n + 1)
                act.wait_ge(rms_ready, tt + 1)
                nc.scalar.activation(st[:, 31:32], st[:, 30:31], ACT.Sqrt).then_inc(rsq_ready, 1)
                act.wait_ge(x1_ready, tt + 1)
                if tt + 2 < TT:
                    act.dma_start(xres[:, tt % 2, :], x_v[:, tt + 2, :]).then_inc(ld_xr[tt % 2], 16)
                nc.scalar.activation(scratch[:, 0:D], x1[:, tt, :], ACT.Square, accum_out=st[:, 33:34]).then_inc(xss_ready, 1)
                act.wait_ge(xss_ready, tt + 1)
                act.wait_ge(xms_ready, tt + 1)
                nc.scalar.activation(st[:, 35:36], st[:, 34:35], ACT.Sqrt).then_inc(xsq_ready, 1)
                act.wait_ge(xn2_ready, tt + 1)
                act.dma_start(xn_dram[tt * P:(tt + 1) * P, :], xn2[:, tt % 2, :]).then_inc(xn2_stored[tt % 2], 16)

            def shifted(dst, src, k, done):
                return nc.scalar.activation(dst, src, ACT.Identity, bias=modT[:, 1, 8 + k:9 + k], scale=scale2[:, k:k + 1]).then_inc(done, 1)

            act.wait_ge(h2m_ready, 1)
            for tt in range(TT + 1):
                if tt < TT:
                    t, free = filled(act, ("mix", tt, 0))
                    if tt >= 2:
                        filled(act, ("out", tt - 2, 1))
                    nc.scalar.copy(mixT[:, tt % 2, 0:4, :], t[:, :].rearrange("p (c n) -> p c n", c=4)).then_inc(mixT_ready[0], 1)
                    act.wait_ge(mixT_ready[0], tt + 1)
                    act.sem_inc(free, 1)
                if tt:
                    t, free = filled(act, ("x2", tt - 1, 1))
                    if tt >= 3:
                        filled(act, ("lg", tt - 3), "G")
                    for q in range(4):
                        shifted(h2T[:, (tt - 1) % 2, 4 + q, :], t[:, q * P:(q + 1) * P], 4 + q, h2T_ready[1])
                    act.wait_ge(h2T_ready[1], 4 * tt)
                    act.sem_inc(free, 1)
                if tt < TT:
                    rms_of(tt)
            act.wait_ge(ge_in, 1)
            nc.scalar.activation(gp[:, :, 0:GROUPS], gp[:, :, 0:GROUPS], ACT.Exp)
            nc.scalar.activation(rt[:, 4, :], rt[:, 3, :], ACT.Exp).then_inc(ge_out, 1)

            def pair(j, b, back, stores):
                act.wait_ge(bank["T1"].full, moe_base["T1"] + j + 1)
                act.wait_ge(bank["G"].full, moe_base["G"] + back)
                for q in range(4):
                    shifted(h2g[:, b, 4 + q, :], ps["T1"][:, q * P:(q + 1) * P], 4 + q, h2g_ready[1])
                act.wait_ge(h2g_ready[1], 4 * j + 4)
                act.sem_inc(bank["T1"].free, 1)
                act.wait_ge(bank["G"].full, moe_base["G"] + j + 1)
                nc.scalar.activation(gact[:, b, :], ps["G"][:, 0:DE], ACT.Silu).then_inc(silu_ready, 1)
                act.wait_ge(bank["O"].full, moe_base["O"] + j + 1)
                act.wait_ge(bank["A1"].full, moe_base["A1"] + back)
                nc.scalar.copy(actT[:, b, :, :], ps["O"][:, 0:DE].rearrange("p (k n) -> p k n", k=2)).then_inc(actT_ready, 1)
                act.wait_ge(actT_ready, j + 1)
                act.sem_inc(bank["O"].free, 1)
                act.wait_ge(bank["A1"].full, moe_base["A1"] + j + 1)
                if stores is not None:
                    act.wait_ge(y_stored[b], 16 * stores)
                nc.scalar.copy(yb[:, b, 512:1024], ps["A1"][:, :]).then_inc(bank["A1"].free, 1)
                act.wait_ge(bank["A1"].free, moe_base["A1"] + j + 1)
                act.wait_ge(yb_ready, j + 1)
                act.dma_start(y_dram.rearrange("(j p) n -> j p n", p=P)[bass.ds(j, 1), :, :].rearrange("a p n -> p (a n)"), yb[:, b, :]).then_inc(y_stored[b], 16)

            pair(0, 0, 0, None)
            pair(1, 1, 0, None)
            with act.Fori(1, NPAIR // 2) as i:
                pair(2 * i, 0, 2 * i - 1, i)
                pair(2 * i + 1, 1, 2 * i, i)
            n_ov = act.value_load(ovi[0:1, NOV:NOV + 1], min_val=0, max_val=NOV // 2)
            with act.If(n_ov > 0):
                with act.Fori(0, n_ov) as v:
                    pair(NPAIR + v, 0, NPAIR + v, NPAIR // 2 + v)
            scratch2 = stage_mem[:, 0:D]
            for tt in range(TT):
                act.wait_ge(fss_ready, tt + 1)
                nc.scalar.activation(scratch2, yc[:, tt % 2, 0, :], ACT.Square, accum_out=st[:, 40:41]).then_inc(fms_ready, 1)
                act.wait_ge(fms_ready, tt + 1)
                act.wait_ge(fsq_in, tt + 1)
                nc.scalar.activation(st[:, 42:43], st[:, 41:42], ACT.Sqrt).then_inc(fsq_ready, 1)

        @block.vector
        def _(dve):
            dn = [0]

            def step(ins):
                dn[0] += 1
                ins.then_inc(dstep, 1)
                dve.wait_ge(dstep, dn[0])

            V = nc.vector

            def rsqrt_in(dst, src, n):
                return V.tensor_scalar(dst, src, 1.0 / n, EPS, ALU.mult, ALU.add)

            t, free = filled(dve, "vec")
            V.tensor_copy(vT[:, :], t[:, 0:42]).then_inc(vT_ready, 1)
            dve.wait_ge(vT_ready, 1)
            dve.sem_inc(free, 1)
            dve.wait_ge(ld_pos, 16)
            step(V.tensor_copy(posf[:, :], posi[:, :]))
            for j in range(HALF):
                freq = float(np.power(np.float32(THETA), np.float32(-j * 2.0 / ROT)))
                V.tensor_scalar(rope[:, 0, :, j], posf[:, :], freq, None, ALU.mult).then_inc(sin_in2, 1)
            dve.wait_ge(sin_in2, HALF)
            magic = 1.5 * 2 ** 23
            step(V.tensor_scalar(rope[:, 1, :, :], rope[:, 0, :, :], 1 / (2 * np.pi), magic, ALU.mult, ALU.add))
            step(V.tensor_scalar(rope[:, 1, :, :], rope[:, 1, :, :], magic, None, ALU.subtract))
            rest = 2 * np.pi
            for bits in (2 ** 8, 2 ** 18, None):
                part = round(rest * bits) / bits if bits else rest
                rest -= part
                step(V.scalar_tensor_tensor(rope[:, 0, :, :], rope[:, 1, :, :], -part, rope[:, 0, :, :], ALU.mult, ALU.add))
            V.tensor_scalar(rope[:, 0, :, :], rope[:, 0, :, :], 3.1415925, -3.1415925, ALU.min, ALU.max).then_inc(sin_in, 1)
            dve.wait_ge(ss_ready, TT)
            rsqrt_in(st[:, 4:8], st[:, 0:4], D).then_inc(rs_ready, 1)
            dve.wait_ge(ss_ready, TT + 1)
            step(V.reciprocal(st[:, 12:16], st[:, 8:12]))
            for tt in range(TT):
                V.tensor_scalar(x_in[:, tt, :], x_in[:, tt, :], st[:, 12 + tt:13 + tt], None, ALU.mult).then_inc(xn_ready, 1)
            dve.wait_ge(c_ready, 1)
            V.tensor_tensor(c32[:, :, :], vT[:, 34:42].unsqueeze(2).broadcast_to([P, KD, 32]), cs[:, :].unsqueeze(2).broadcast_to([P, KD, 32]), ALU.mult).then_inc(c32_ready, 1)
            dve.wait_ge(sin_out, 2)
            step(V.tensor_tensor(rope[:, 1, :, :], rope[:, 2, :, :], rope[:, 2, :, :], ALU.mult))
            step(V.tensor_scalar(rope[:, 2, :, :], rope[:, 1, :, :], -2.0, 1.0, ALU.mult, ALU.add))
            step(V.tensor_scalar(nsin[:, :, :], rope[:, 3, :, :], -1.0, None, ALU.mult))
            dve.sem_inc(rope_ready, 1)
            g, free = filled(dve, "rows", "G")
            V.tensor_copy(rowb[:, :], g[:, 0:228]).then_inc(rowb_ready, 1)
            dve.wait_ge(rowb_ready, 1)
            dve.sem_inc(free, 1)
            for k in range(1, KD, 2):
                t, free = filled(dve, ("x", k))
                step(V.tensor_copy(hT[:, k, :], t[:, :]))
                dve.sem_inc(free, 1)

            def mod_cols(grp):
                dve.wait_ge(ld_bada, 16)
                dve.wait_ge(m16_in, 16 * (grp + 1))
                V.tensor_tensor(m16[:, grp, :], m16[:, grp, :], bada[:, grp, :], ALU.add).then_inc(m16_ready, 1)

            def mod_take(grp):
                t, free = filled(dve, ("mod", grp))
                step(V.tensor_copy(modT[:, grp, :], t[:, 0:16]))
                dve.sem_inc(free, 1)

            mod_cols(0)
            mod_take(0)
            step(V.scalar_tensor_tensor(scale1[:, :], modT[:, 0, 8:16], 1.0, vT[:, 0:8], ALU.add, ALU.mult))
            for k in range(KD):
                if k % 2 == 0:
                    dve.wait_ge(hraw, k // 2 + 1)
                V.tensor_scalar(hT[:, k, :], hT[:, k, :], scale1[:, k:k + 1], modT[:, 0, k:k + 1], ALU.mult, ALU.add).then_inc(h_ready, 1)

            dve.wait_ge(ikw_in, TT)
            ik = ikw[:, :, RANK:RANK + 64]
            step(V.tensor_reduce(st[:, 44:48], ik, AX.X, ALU.add))
            step(V.tensor_scalar(st[:, 44:48], st[:, 44:48], 1.0 / 64, None, ALU.mult))
            mu = st[:, 44:48].unsqueeze(2).broadcast_to([P, TT, 64])
            step(V.tensor_tensor(ik, ik, mu, ALU.subtract))
            step(V.tensor_tensor(kin[:, :, 0, :], ik, ik, ALU.mult))
            step(V.tensor_reduce(st[:, 48:52], kin[:, :, 0, :], AX.X, ALU.add))
            V.tensor_scalar(wi[:, :, :], ikw[:, :, RANK + 64:NS], 8 ** -0.5, None, ALU.mult).then_inc(wi_ready, 1)
            rsqrt_in(st[:, 52:56], st[:, 48:52], 64).then_inc(lnv_ready, 1)
            dve.wait_ge(lnq_ready, 1)
            step(V.reciprocal(st[:, 60:64], st[:, 56:60]))
            step(V.tensor_tensor(ik, ik, st[:, 60:64].unsqueeze(2).broadcast_to([P, TT, 64]), ALU.mult))
            step(V.tensor_tensor(kin[:, :, 0, :], ik, g_ki_b.unsqueeze(1).broadcast_to([P, TT, 64]), ALU.mult))
            ki = kin[:, :, 0, :]
            step(V.tensor_tensor(kin[:, :, 1, 0:HALF], ki[:, :, HALF:ROT], nsin[:, :, :], ALU.mult))
            step(V.tensor_tensor(kin[:, :, 1, HALF:ROT], ki[:, :, 0:HALF], rope[:, 3, :, :], ALU.mult))
            step(V.tensor_tensor(ki[:, :, 0:HALF], ki[:, :, 0:HALF], rope[:, 2, :, :], ALU.mult))
            step(V.tensor_tensor(ki[:, :, HALF:ROT], ki[:, :, HALF:ROT], rope[:, 2, :, :], ALU.mult))
            step(V.tensor_tensor(ki[:, :, 0:ROT], ki[:, :, 0:ROT], kin[:, :, 1, 0:ROT], ALU.add))
            V.tensor_copy(kin[:, :, 1, :], ki).then_inc(ki_ready, 1)

            queue = []

            def topk_round(tq, w):
                work = mask[:, tq - 1, 0:w]
                step(V.max(m8[:, :], work))
                step(V.match_replace(work, m8[:, :], work, TAKEN))

            def topk_end(tq, w):
                work = mask[:, tq - 1, 0:w]
                step(V.tensor_scalar(work, work, TAKEN * 0.7, HIDE, ALU.is_gt, ALU.mult))

            def some(n):
                for _ in range(n):
                    if queue:
                        queue.pop(0)()

            dve.wait_ge(const_ready, 3)
            dve.wait_ge(pstep_const, 1)
            for n in range(3 * PAIRS):
                tq, hp = 1 + n // PAIRS, n % PAIRS
                w = (tq + 1) * P
                acc = mask[:, tq - 1, 0:w]
                for hh in range(2):
                    h = 2 * hp + hh
                    dve.wait_ge(relu_ready, 2 * n + hh + 1)
                    if h == 0:
                        ins = V.tensor_scalar(acc, relu[:, hh, 0:w], wi[:, tq, 0:1], None, ALU.mult)
                    else:
                        ins = V.scalar_tensor_tensor(acc, relu[:, hh, 0:w], wi[:, tq, h:h + 1], acc, ALU.mult, ALU.add)
                    ins.then_inc(relu_used, 1)
                    dve.wait_ge(relu_used, 2 * n + hh + 1)
                if hp == PAIRS - 1:
                    step(V.tensor_tensor(mask[:, tq - 1, tq * P:w], mask[:, tq - 1, tq * P:w], causal0[:, :], ALU.add))
                some(4)
                if hp == PAIRS - 1:
                    assert not queue
                    queue += [lambda tq=tq, w=w: topk_round(tq, w)] * (TOPK // 8 - 1)
                    queue.append(lambda tq=tq, w=w: (topk_round(tq, w), topk_end(tq, w)))
                if n == 5:
                    for r, name in enumerate(("G", "O")):
                        z, free = filled(dve, ("z", r), name)
                        step(V.tensor_scalar(zz[:, 0, r, :], z[:, :], vT[:, 32 + r:33 + r], None, ALU.add))
                        dve.sem_inc(free, 1)
                    V.scalar_tensor_tensor(zz[:, 1, :, :], zz[:, 0, :, :], -1.0, zz[:, 0, :, :], ALU.mult, ALU.min).then_inc(z_in, 1)
                if n == 8:
                    dve.wait_ge(zexp_ready, 2)
                    for r in range(2):
                        step(V.scalar_tensor_tensor(zz[:, 3, r, :], zz[:, 0, r, :], 0.0, zz[:, 2, r, :], ALU.min, ALU.subtract))
                        for ch in range(TT):
                            cut = slice(ch * P, (ch + 1) * P)
                            V.tensor_tensor_scan(bT[:, r, cut], ones[:, :], zz[:, 3, r, cut], 0.0, ALU.mult, ALU.add).then_inc(b_ready, 1)

            for u in range(TT * PAIRS + 1):
                tq, hp = u // PAIRS, u % PAIRS
                w = (tq + 1) * P
                z = 4 * (u % 2)
                if u < TT * PAIRS:
                    for hh in range(2):
                        s, free = filled(dve, ("att", u), f"S{hh}")
                        if u >= 2:
                            filled(dve, ("p", u - 2, hh))
                        hidden = causal0[:, :] if tq == 0 else mask[:, tq - 1, 0:w]
                        step(V.tensor_tensor_reduce(out=prob[:, u % 2, hh, 0:w], in0=s[:, 0:w], in1=hidden, scale=1.0, scalar=-3e38,
                                                    op0=ALU.add, op1=ALU.max, accum_out=sm[:, hh, z:z + 1]))
                        dve.sem_inc(free, 1)
                        V.tensor_scalar(sm[:, hh, z + 1:z + 2], sm[:, hh, z:z + 1], -HD ** -0.5, None, ALU.mult).then_inc(s_masked, 1)
                    some(4)
                    for hh in range(2):
                        dve.wait_ge(p_exp, 2 * u + hh + 1)
                        step(V.reciprocal(sm[:, hh, z + 3:z + 4], sm[:, hh, z + 2:z + 3]))
                        V.tensor_scalar(prob[:, u % 2, hh, 0:w], prob[:, u % 2, hh, 0:w], sm[:, hh, z + 3:z + 4], None, ALU.mult).then_inc(p_ready, 1)
                if u in (13, 14):
                    mod_cols(u - 12)
                    mod_take(u - 12)
                if u:
                    v = u - 1
                    m = (v // PAIRS + 1) * P
                    t, free = filled(dve, ("p", v, 1))
                    if v >= 2:
                        filled(dve, ("att", v - 2), "O")
                    V.tensor_copy(probT[:, v % 2, 1, 0:m], t[:, 0:m]).then_inc(pT_ready[1], 1)
                    dve.wait_ge(pT_ready[1], v + 1)
                    dve.sem_inc(free, 1)
            step(V.scalar_tensor_tensor(scale2[:, :], modT[:, 2, 0:8], 1.0, vT[:, 8:16], ALU.add, ALU.mult))
            step(V.tensor_tensor(gatev[:, 0, :], modT[:, 1, 0:8], vT[:, 16:24], ALU.mult))
            step(V.tensor_tensor(gatev[:, 1, :], modT[:, 2, 8:16], vT[:, 24:32], ALU.mult))
            dve.sem_inc(h2m_ready, 1)

            dve.wait_ge(gs_in, TT + 1)
            gsv = gs.rearrange("p t (h n) -> p (t h) n", h=GLA_H)
            step(V.tensor_tensor(gsv, gsv, g_out_b.unsqueeze(1).broadcast_to([P, TT * GLA_H, P]), ALU.mult))
            dve.wait_ge(gqk_ready, 4)
            dve.wait_ge(b_ready, 2 * TT)

            def gla_factors(ch):
                if ch:
                    filled(dve, ("o", ch - 1), "G")
                    filled(dve, ("o", ch - 1), "O")
                for r in range(2):
                    b = bT[:, r, ch * P:(ch + 1) * P]
                    b3 = b.rearrange("p (i t) -> p i t", i=NB)
                    ref = b3[:, :, BLK // 2 - 1:BLK // 2]
                    V.tensor_tensor(expo[:, r, 0:512].rearrange("p (i s) -> p i s", i=NB), ref.broadcast_to([P, NB, P]),
                                    b.unsqueeze(1).broadcast_to([P, NB, P]), ALU.subtract)
                    V.tensor_tensor(expo[:, r, 512:640].rearrange("p (i t) -> p i t", i=NB), b3, ref.broadcast_to([P, NB, BLK]), ALU.subtract)
                    V.tensor_copy(expo[:, r, 640:768], b)
                    step(V.tensor_scalar(expo[:, r, 768:896], b, -1.0, b[:, P - 1:P], ALU.mult, ALU.add))
                V.tensor_scalar(expo[:, :, :], expo[:, :, :], CLAMP * TAU, None, ALU.min).then_inc(ex_in, 1)
                dve.wait_ge(ex_exp, ch + 1)
                step(V.tensor_copy(dec[:, :], expo[:, :, 767]))
                for r in range(2):
                    q, k = gqk[:, r, ch * P:(ch + 1) * P], gqk[:, 2 + r, ch * P:(ch + 1) * P]
                    for lo, n, f in ((0, NB, k), (512, 2, q), (768, 1, k)):
                        e = expo[:, r, lo:lo + n * P].rearrange("p (i s) -> p i s", i=n)
                        ins = V.tensor_tensor(e, e, f.unsqueeze(1).broadcast_to([P, n, P]), ALU.mult)
                        step(ins)
                dve.sem_inc(ex_ready, 1)

            for ch in range(TT):
                gla_factors(ch)
                for hh in range(2):
                    sc, free = filled(dve, ("sc", ch), "GO"[hh])
                    V.tensor_tensor(scT.rearrange("p (r a) n -> p r a n", a=2)[:, :, hh, :], sc[:, 0:256].rearrange("p (r n) -> p r n", r=2),
                                    upto[:, :].unsqueeze(1).broadcast_to([P, 2, P]), ALU.mult).then_inc(sc_ready, 1)
                    dve.wait_ge(sc_ready, 2 * ch + hh + 1)
                    dve.sem_inc(free, 1)
                dve.wait_ge(oss_ready, 4 * ch + 4)
                rsqrt_in(st[:, 20:24], st[:, 16:20], GLA_DV).then_inc(oms_ready, 1)
                if ch < TT - 1:
                    t, free = filled(dve, ("state", ch))
                    for r in range(2):
                        if ch == 0:
                            V.tensor_copy(state[:, r, :], t[:, r * P:(r + 1) * P]).then_inc(state_ready, 1)
                        else:
                            V.scalar_tensor_tensor(state[:, r, :], state[:, r, :], dec[:, r:r + 1], t[:, r * P:(r + 1) * P], ALU.mult, ALU.add).then_inc(state_ready, 1)
                    dve.wait_ge(state_ready, 2 * ch + 2)
                    dve.sem_inc(free, 1)
                dve.wait_ge(osq_ready, ch + 1)
                step(V.reciprocal(st[:, 36:40], st[:, 24:28]))
                if ch:
                    filled(dve, ("oa", ch - 1))
                for h in range(GLA_H):
                    name, r = "GO"[h % 2], h // 2
                    V.scalar_tensor_tensor(oan[:, h * P:(h + 1) * P], ps[name][:, r * P:(r + 1) * P], st[:, 36 + h:37 + h],
                                           gs[:, ch, h * P:(h + 1) * P], ALU.mult, ALU.mult).then_inc(oan_ready, 1)
                dve.wait_ge(oan_ready, 4 * ch + 4)
                for name in ("G", "O"):
                    dve.sem_inc(bank[name].free, 1)
                t, free = filled(dve, ("oa", ch))
                V.tensor_copy(gqk[:, :, ch * P:(ch + 1) * P], t[:, :].rearrange("p (c n) -> p c n", c=4)).then_inc(oa_ready, 1)
                dve.wait_ge(oa_ready, ch + 1)
                dve.sem_inc(free, 1)

            def diagonal(which):
                V.tensor_tensor(diag[:, which, :].rearrange("p (k n) -> p k n", k=KD), ident[:, :].unsqueeze(1).broadcast_to([P, KD, P]),
                                gatev[:, which, :].unsqueeze(2).broadcast_to([P, KD, P]), ALU.mult).then_inc(gd_ready, 1)

            def gate_take(tag, dst):
                for n, name in enumerate(("G", "O")):
                    g, free = filled(dve, (tag, n), name)
                    step(V.tensor_copy(dst[:, n * 512:(n + 1) * 512], g[:, :]))
                    dve.sem_inc(free, 1)

            filled(dve, ("dq", TT - 1))
            diagonal(0)
            gate_take("gm", gmb)

            def mixing(n, tt):
                for ab in range(2):
                    dve.wait_ge(sig_ready, n * 2 * TT + ab * TT + tt + 1)
                    a, free = filled(dve, ("y", n, tt, ab))
                    step(V.tensor_tensor(sig[:, ab, tt, :], a[:, :], sig[:, ab, tt, :], ALU.mult))
                    dve.sem_inc(free, 1)
                if n == 0 and tt == 0:
                    filled(dve, ("att", TT * PAIRS - 1), "O")
                V.tensor_tensor(mix[:, tt, n * 512:(n + 1) * 512], sig[:, 0, tt, :], sig[:, 1, tt, :], ALU.add).then_inc(mix_ready, 1)

            for n in range(2):
                for tt in range(TT):
                    mixing(n, tt)
            dve.wait_ge(mix_ready, 2 * TT)

            def shifted(dst, src, k, done):
                return V.tensor_scalar(dst, src, scale2[:, k:k + 1], modT[:, 1, 8 + k:9 + k], ALU.mult, ALU.add).then_inc(done, 1)

            def residual(tt):
                dve.wait_ge(rss_ready, 2 * tt + 2)
                step(V.tensor_tensor(st[:, 28:29], st[:, 28:29], st[:, 29:30], ALU.add))
                rsqrt_in(st[:, 30:31], st[:, 28:29], D).then_inc(rms_ready, 1)
                dve.wait_ge(rsq_ready, tt + 1)
                step(V.reciprocal(st[:, 32:33], st[:, 31:32]))
                for n in range(2):
                    a, free = filled(dve, ("out", tt, n))
                    step(V.scalar_tensor_tensor(x1[:, tt, n * 512:(n + 1) * 512], a[:, :], st[:, 32:33], gmb[:, n * 512:(n + 1) * 512], ALU.mult, ALU.mult))
                    dve.sem_inc(free, 1)
                dve.wait_ge(ld_xr[tt % 2], 16 * (tt // 2 + 1))
                V.tensor_tensor(x1[:, tt, :], x1[:, tt, :], xres[:, tt % 2, :], ALU.add).then_inc(x1_ready, 1)
                dve.wait_ge(xss_ready, tt + 1)
                rsqrt_in(st[:, 34:35], st[:, 33:34], D).then_inc(xms_ready, 1)
                dve.wait_ge(xsq_ready, tt + 1)
                step(V.reciprocal(st[:, 43:44], st[:, 35:36]))
                if tt >= 2:
                    dve.wait_ge(xn2_stored[tt % 2], 16)
                    filled(dve, ("x2", tt - 2, 1))
                V.tensor_scalar(xn2[:, tt % 2, :], x1[:, tt, :], st[:, 43:44], None, ALU.mult).then_inc(xn2_ready, 1)

            for tt in range(TT + 1):
                if tt < TT:
                    t, free = filled(dve, ("mix", tt, 1))
                    if tt >= 2:
                        filled(dve, ("out", tt - 2, 1))
                    V.tensor_copy(mixT[:, tt % 2, 4:8, :], t[:, :].rearrange("p (c n) -> p c n", c=4)).then_inc(mixT_ready[1], 1)
                    dve.wait_ge(mixT_ready[1], tt + 1)
                    dve.sem_inc(free, 1)
                if tt:
                    t, free = filled(dve, ("x2", tt - 1, 0))
                    if tt >= 3:
                        filled(dve, ("lg", tt - 3), "G")
                    for q in range(4):
                        shifted(h2T[:, (tt - 1) % 2, q, :], t[:, q * P:(q + 1) * P], q, h2T_ready[0])
                    dve.wait_ge(h2T_ready[0], 4 * tt)
                    dve.sem_inc(free, 1)
                if tt < TT:
                    residual(tt)
                if tt:
                    g, free = filled(dve, ("lg", tt - 1), "G")
                    step(V.tensor_tensor(lg[:, tt - 1, :], g[:, 0:GROUPS + NE], b_rt_b, ALU.add))
                    dve.sem_inc(free, 1)

            step(V.tensor_copy(gp[:, :, 0:GROUPS], lg[:, :, 0:GROUPS]))
            step(V.tensor_copy(iotaf[:, :], iota[:, :]))
            for tt in range(TT):
                step(V.max(top[:, tt, :], gp[:, tt, :]))
                step(V.max_index(topi[:, tt, :], top[:, tt, :], gp[:, tt, :]))
            step(V.tensor_copy(rt[:, 0, :], topi[:, :, 0]))
            step(V.tensor_tensor(ohg[:, :, 0, :], iotaf[:, 0:GROUPS].unsqueeze(1).broadcast_to([P, TT, GROUPS]),
                                 rt[:, 0, :].unsqueeze(2).broadcast_to([P, TT, GROUPS]), ALU.is_equal))
            step(V.tensor_scalar(ohg[:, :, 1, :], ohg[:, :, 0, :], -HIDE, HIDE, ALU.mult, ALU.add))
            for a, op in ((0, ALU.mult), (1, ALU.add)):
                src = (lg[:, :, GROUPS:] if a == 0 else el[:, :, :]).rearrange("p t (g e) -> p t g e", g=GROUPS)
                for tt in range(TT):
                    step(V.tensor_tensor(el[:, tt, :].rearrange("p (g e) -> p g e", g=GROUPS), src[:, tt, :, :],
                                         ohg[:, tt, a, :].unsqueeze(2).broadcast_to([P, GROUPS, PER_GROUP]), op))
            for tt in range(TT):
                step(V.max(etop[:, tt, :], el[:, tt, :]))
                step(V.max_index(etopi[:, tt, :], etop[:, tt, :], el[:, tt, :]))
            for w, dst in enumerate((e1, e2)):
                step(V.tensor_copy(rt[:, 1 + w, :], etopi[:, :, w]))
                step(V.tensor_tensor(dst[:, :, :], iotaf[:, :].unsqueeze(1).broadcast_to([P, TT, NE]),
                                     rt[:, 1 + w, :].unsqueeze(2).broadcast_to([P, TT, NE]), ALU.is_equal))
            V.tensor_tensor(em[:, :, :], e1[:, :, :], e2[:, :, :], ALU.add).then_inc(em_ready, 1)
            step(V.tensor_tensor(gp[:, :, 0:GROUPS], gp[:, :, 0:GROUPS], top[:, :, 0:1].broadcast_to([P, TT, GROUPS]), ALU.subtract))
            step(V.tensor_tensor(rt[:, 3, :], etop[:, :, 1], etop[:, :, 0], ALU.subtract))
            dve.sem_inc(ge_in, 1)
            o, free = filled(dve, "count", "O")
            n_e, x_e, cum, base_d, base_e = (cnt[:, n, :] for n in range(5))
            step(V.tensor_copy(n_e, o[:, 0:NE]))
            dve.sem_inc(free, 1)
            step(V.tensor_scalar(x_e, n_e, float(SLOT), None, ALU.is_gt))
            for m in range(2, SEQ // SLOT):
                step(V.scalar_tensor_tensor(x_e, n_e, float(SLOT * m), x_e, ALU.is_gt, ALU.add))
            step(V.tensor_tensor_scan(cum, ones[:, 0:NE], x_e, 0.0, ALU.mult, ALU.add))
            step(V.tensor_tensor(base_d, cum, x_e, ALU.subtract))
            step(V.tensor_scalar(base_e, iotaf[:, :], float(SLOT), None, ALU.mult))
            step(V.tensor_scalar(base_d, base_d, float(SLOT), float(SLOT * (NE - 1)), ALU.mult, ALU.add))
            step(V.tensor_tensor(base_d, base_d, base_e, ALU.subtract))
            g, free = filled(dve, "rank", "G")
            step(V.tensor_copy(rpos[:, :, :], g[:, 0:TT * NE].rearrange("p (t e) -> p t e", t=TT)))
            dve.sem_inc(free, 1)
            step(V.tensor_scalar(rtmp3[:, :, :], rpos[:, :, :], float(SLOT), None, ALU.is_ge))
            step(V.tensor_tensor(rtmp3[:, :, :], rtmp3[:, :, :], base_d.unsqueeze(1).broadcast_to([P, TT, NE]), ALU.mult))
            step(V.tensor_tensor(rpos[:, :, :], rpos[:, :, :], rtmp3[:, :, :], ALU.add))
            step(V.tensor_tensor(rpos[:, :, :], rpos[:, :, :], base_e.unsqueeze(1).broadcast_to([P, TT, NE]), ALU.add))
            for w, oh in enumerate((e1, e2)):
                step(V.tensor_tensor(rtmp3[:, :, :], rpos[:, :, :], oh[:, :, :], ALU.mult))
                step(V.tensor_reduce(rt[:, 5 + w, :], rtmp3[:, :, :], AX.X, ALU.add))
                step(V.tensor_copy(slotpos[:, :, w], rt[:, 5 + w, :]))
            dve.sem_inc(pos_ready, 1)
            step(V.tensor_tensor(ovc[:, :, :], iotaf[:, 0:NOV].unsqueeze(2).broadcast_to([P, NOV, NE]), cum.unsqueeze(1).broadcast_to([P, NOV, NE]), ALU.is_ge))
            step(V.tensor_reduce(ovf[:, 0:NOV], ovc[:, :, :], AX.X, ALU.add))
            step(V.tensor_scalar(ovf[:, 0:NOV], ovf[:, 0:NOV], float(NE - 1), None, ALU.min))
            step(V.tensor_scalar(cnt[:, 5, 0:NOV // 2], iotaf[:, 0:NOV // 2], 2.0, None, ALU.mult))
            step(V.tensor_tensor(cnt[:, 6, 0:NOV // 2], cnt[:, 5, 0:NOV // 2], cum[:, NE - 1:NE].broadcast_to([P, NOV // 2]), ALU.is_lt))
            step(V.tensor_reduce(ovf[:, NOV:NOV + 1], cnt[:, 6, 0:NOV // 2], AX.X, ALU.add))
            step(V.tensor_copy(ovi[:, 0:NOV + 1], ovf[:, 0:NOV + 1]))
            dve.sem_inc(route_ready, 1)
            dve.wait_ge(ge_out, 1)
            step(V.tensor_reduce(rt[:, 7, :], gp[:, :, 0:GROUPS], AX.X, ALU.add))
            step(V.tensor_scalar(rt[:, 8, :], rt[:, 4, :], 1.0, None, ALU.add))
            step(V.tensor_tensor(rt[:, 7, :], rt[:, 7, :], rt[:, 8, :], ALU.mult))
            step(V.reciprocal(rt[:, 9, :], rt[:, 7, :]))
            step(V.tensor_tensor(rt[:, 10, :], rt[:, 9, :], rt[:, 4, :], ALU.mult))
            filled(dve, ("out", TT - 1, 1))
            diagonal(1)
            gate_take("gf", gfb)
            dve.wait_ge(slot_in, 16)
            V.tensor_copy(slot_f[:, :], slot_r[:, :]).then_inc(slot_cast, 1)
            g, free = filled(dve, "slots", "G")
            V.tensor_copy(slot_i[:, :], g[:, 0:NPALL]).then_inc(slot_ready, 1)
            dve.wait_ge(slot_ready, 1)
            dve.sem_inc(free, 1)

            def pair(j, b, back, stores):
                dve.wait_ge(bank["T0"].full, moe_base["T0"] + j + 1)
                dve.wait_ge(bank["G"].full, moe_base["G"] + back)
                for q in range(4):
                    shifted(h2g[:, b, q, :], ps["T0"][:, q * P:(q + 1) * P], q, h2g_ready[0])
                dve.wait_ge(h2g_ready[0], 4 * j + 4)
                dve.sem_inc(bank["T0"].free, 1)
                dve.wait_ge(silu_ready, j + 1)
                V.tensor_tensor(aact[:, b, :], gact[:, b, :], ps["G"][:, DE:2 * DE], ALU.mult).then_inc(act_ready, 1)
                dve.wait_ge(act_ready, j + 1)
                dve.sem_inc(bank["G"].free, 1)
                dve.wait_ge(bank["A0"].full, moe_base["A0"] + j + 1)
                if stores is not None:
                    dve.wait_ge(y_stored[b], 16 * stores)
                V.tensor_copy(yb[:, b, 0:512], ps["A0"][:, :]).then_inc(yb_ready, 1)
                dve.wait_ge(yb_ready, j + 1)
                dve.sem_inc(bank["A0"].free, 1)

            pair(0, 0, 0, None)
            pair(1, 1, 0, None)
            with dve.Fori(1, NPAIR // 2) as i:
                pair(2 * i, 0, 2 * i - 1, i)
                pair(2 * i + 1, 1, 2 * i, i)
            n_ov = dve.value_load(ovi[0:1, NOV:NOV + 1], min_val=0, max_val=NOV // 2)
            with dve.If(n_ov > 0):
                with dve.Fori(0, n_ov) as v:
                    pair(NPAIR + v, 0, NPAIR + v, NPAIR // 2 + v)
            for tt in range(TT):
                dve.wait_ge(yc_in[tt % 2], 32 * (tt // 2 + 1))
                y = yc[:, tt % 2, :, :]
                step(V.tensor_scalar(y[:, 0, :], y[:, 0, :], rt[:, 9, tt:tt + 1], None, ALU.mult))
                V.scalar_tensor_tensor(y[:, 0, :], y[:, 1, :], rt[:, 10, tt:tt + 1], y[:, 0, :], ALU.mult, ALU.add).then_inc(fss_ready, 1)
                dve.wait_ge(fms_ready, tt + 1)
                rsqrt_in(st[:, 41:42], st[:, 40:41], D).then_inc(fsq_in, 1)
                dve.wait_ge(fsq_ready, tt + 1)
                step(V.reciprocal(st[:, 43:44], st[:, 42:43]))
                step(V.scalar_tensor_tensor(y[:, 0, :], y[:, 0, :], st[:, 43:44], gfb, ALU.mult, ALU.mult))
                V.tensor_tensor(x1[:, tt, :], x1[:, tt, :], y[:, 0, :], ALU.add).then_inc(fin_ready, 1)
                dve.wait_ge(fin_ready, tt + 1)
                dve.sem_inc(fin_y, 1)


_INS = ["x", "c", "positions", "w_ada", "b_ada", "g_pre_mix", "g_post_mix", "g_pre_ffn", "g_post_ffn", "w_in", "w_gla_a2", "b_gla_a",
        "g_gla_out", "g_idx_k", "w_proj_gla", "w_proj_dsa", "w_out", "w_router_g", "b_router_g", "w_router_e", "b_router_e",
        "w_e_gate", "w_e_up", "w_e_down"]
_OUTS = [((1, SEQ, D), "float32")]


def kernel(**inputs):
    import numpy as _np
    import concourse.bacc as _bacc
    from concourse import mybir as _mybir
    from concourse.bass_utils import run_bass_kernel_spmd as _run

    nc = _bacc.Bacc("TRN2", target_bir_lowering=False, num_devices=1)
    arrays, args = {}, []
    for name in _INS:
        a = _np.ascontiguousarray(inputs[name])
        arrays[f"in_{name}_dram"] = a
        args.append(nc.dram_tensor(f"in_{name}_dram", a.shape, _mybir.dt.from_np(a.dtype), kind="ExternalInput").ap())
    for i, (shape, dtype) in enumerate(_OUTS):
        dt = _mybir.dt.from_np(_np.dtype(dtype))
        args.append(nc.dram_tensor(f"out_{i}_dram", shape, dt, kind="ExternalOutput").ap())
    layer(nc, *args)
    r = _run(nc, [arrays], core_ids=[0])
    got = tuple(r.results[0][f"out_{i}_dram"] for i in range(len(_OUTS)))
    return got[0]
```

```python
from contextlib import ExitStack

import numpy as np

import concourse.bass as bass
from concourse import mybir

ALU = mybir.AluOpType
ACT = mybir.ActivationFunctionType
F32 = mybir.dt.float32
F32R = mybir.dt.float32r
I32 = mybir.dt.int32
U32 = mybir.dt.uint32
AX = mybir.AxisListType

P = 128
D = 1024
SEQ = 512
TT = SEQ // P
KD = D // P
EPS = 1e-6
GLA_H, GLA_DK, GLA_DV, RANK = 4, 64, 128, 16
TAU = 16.0
HEADS, HD = 8, 64
TOPK = min(256, SEQ // 4)
ROT = HD // 4
HALF = ROT // 2
THETA = 500000.0
GROUPS, PER_GROUP = 4, 8
NE = GROUPS * PER_GROUP
DE = D // 4
PAIRS = HEADS // 2
SIZES = (256, 256, 512, 512, RANK, 512, 512, 512, 512, 64, 8, 2 * D)
OFF = [0] + [int(v) for v in np.cumsum(SIZES)]
(O_GQ, O_GK, O_GV, O_GG, O_GA, O_DQ, O_DK, O_DV, O_IQ, O_IK, O_IW, O_BG) = OFF[:12]
NS = RANK + 64 + 8
BLK = 32
NB = P // BLK
CLAMP = 40.0
HIDE = -1e30
TAKEN = -3e38
SLOT = 64
NPAIR = NE // 2
NOV = 16
NPALL = NPAIR + NOV // 2
NONE = 4096.0
NU = TT * PAIRS
GLA_AT = 8
WELEM = 3 * D * DE // P


class Bank:

    def __init__(self, full, free):
        self.full, self.free, self.at = full, free, {}

    def turn(self, name):
        assert name not in self.at, name
        self.at[name] = len(self.at)
        return self.at[name]


def layer(nc, x, c, positions, w_ada, b_ada, g_pre_mix, g_post_mix, g_pre_ffn, g_post_ffn, w_in,
          w_gla_a2, b_gla_a, g_gla_out, g_idx_k, w_proj_gla, w_proj_dsa, w_out, w_router_g,
          b_router_g, w_router_e, b_router_e, w_e_gate, w_e_up, w_e_down, out):
    xn_dram = nc.dram_tensor("xn_dram", (SEQ, D), F32, kind="Internal").ap()
    y_dram = nc.dram_tensor("y_dram", (2 * SEQ, D), F32, kind="Internal").ap()

    x_v = x[0].rearrange("(t p) d -> p t d", p=P)
    out_v = out[0].rearrange("(t p) d -> p t d", p=P)
    win_v = w_in[0].rearrange("(k p) n -> p k n", p=P)
    ada_v = w_ada[0].rearrange("(k p) n -> p k n", p=P)
    pg_v = w_proj_gla[0].rearrange("(k p) n -> p k n", p=P)
    pd_v = w_proj_dsa[0].rearrange("(k p) n -> p k n", p=P)
    wo_v = w_out[0].rearrange("(k p) n -> p k n", p=P)
    weg_v = w_e_gate[0].rearrange("e (k p) f -> e p k f", p=P)
    weu_v = w_e_up[0].rearrange("e (k p) f -> e p k f", p=P)
    wed_v = w_e_down[0].rearrange("e (k p) n -> e p k n", p=P)

    with ExitStack() as ctx:
        place = {}

        def sb(name, shape, dt=F32):
            place[name] = (nc.sbuf_base + 31) // 32 * 32
            return ctx.enter_context(nc.sbuf_tensor(name, shape, dt))

        def rounded(name, n):
            return nc.alloc_sbuf_tensor_at(name + "_r", [P, n], F32R, offset=place[name])

        def sem(name):
            return ctx.enter_context(nc.semaphore(name))

        arena = sb("arena", [P, 4 * WELEM])
        ring = arena[:, 0:4 * 4096].rearrange("p (s n) -> p s n", s=4)
        hT = arena[:, 16384:20480].rearrange("p (k n) -> p k n", k=KD)
        prob = arena[:, 20480:22528].rearrange("p (b h n) -> p b h n", b=2, h=2)
        probT = arena[:, 22528:24576].rearrange("p (b h n) -> p b h n", b=2, h=2)
        adab = arena[:, 20480:24576].rearrange("p (b n) -> p b n", b=2)
        yc = arena[:, 0:8192].rearrange("p (t w n) -> p t w n", t=TT, w=2)
        wexp = arena[:, :].rearrange("p (s n) -> p s n", s=4)

        qi_mem = sb("qi_mem", [P, 2048])
        qiT = qi_mem[:, :].rearrange("p (c n) -> p c n", c=4)
        expo = qi_mem[:, 0:1792].rearrange("p (r n) -> p r n", r=2)
        kiT = sb("kiT", [P, SEQ])
        qT = sb("qT", [P, PAIRS, SEQ])
        kv = sb("kv", [P, 4096])
        kT = kv[:, 0:2048].rearrange("p (c n) -> p c n", c=PAIRS)
        val = kv[:, 2048:4096].rearrange("p (t n) -> p t n", t=TT)
        mix = kv[:, :].rearrange("p (t n) -> p t n", t=TT)
        xg = kv[:, 0:2048].rearrange("p (b n) -> p b n", b=2)
        h2g = kv[:, 2048:4096].rearrange("p (b k n) -> p b k n", b=2, k=KD)
        gqk = sb("gqk", [P, 4, SEQ])
        relu = gqk[:, 0:2, :]
        gvs = sb("gvs", [P, 4096])
        gv = gvs[:, 0:2048].rearrange("p (t n) -> p t n", t=TT)
        gs = gvs[:, 2048:4096].rearrange("p (t n) -> p t n", t=TT)
        mask = sb("mask", [P, TT - 1, SEQ])
        sig_mem = sb("sig_mem", [P, 4096])
        x_in = sig_mem[:, :].rearrange("p (t n) -> p t n", t=TT)
        zz = sig_mem[:, :].rearrange("p (w r n) -> p w r n", w=4, r=2)
        sig = sig_mem[:, :].rearrange("p (a t n) -> p a t n", a=2, t=TT)
        xn2 = sig_mem[:, 0:2048].rearrange("p (b n) -> p b n", b=2)
        h2T = sig_mem[:, 2048:4096].rearrange("p (b k n) -> p b k n", b=2, k=KD)
        yb = sig_mem[:, 0:2048].rearrange("p (b n) -> p b n", b=2)
        gact = sig_mem[:, 2048:2560].rearrange("p (b n) -> p b n", b=2)
        aact = sig_mem[:, 2560:3072].rearrange("p (b n) -> p b n", b=2)
        actT = sig_mem[:, 3072:3584].rearrange("p (b k n) -> p b k n", b=2, k=2)
        stage_mem = sb("stage_mem", [P, 2048])
        stage = stage_mem[:, :].rearrange("p (s n) -> p s n", s=4)
        xres = stage_mem[:, :].rearrange("p (b n) -> p b n", b=2)
        diag = stage_mem[:, :].rearrange("p (w n) -> p w n", w=2)
        gla_mem = sb("gla_mem", [P, 2560])
        bT = gla_mem[:, 0:1024].rearrange("p (r n) -> p r n", r=2)
        scT = gla_mem[:, 1024:1536].rearrange("p (h n) -> p h n", h=4)
        kN = gla_mem[:, 1536:1792]
        state = gla_mem[:, 1792:2048].rearrange("p (r n) -> p r n", r=2)
        oan = gla_mem[:, 2048:2560]
        gmb = gla_mem[:, 1024:2048]
        gfb = gmb
        w_small = gvs[:, 0:KD * NS].rearrange("p (k n) -> p k n", k=KD)
        ikw = gvs[:, KD * NS:(KD + TT) * NS].rearrange("p (t n) -> p t n", t=TT)
        kin = sig_mem[:, 3072:3584].rearrange("p (t a n) -> p t a n", t=TT, a=2)
        w_rt = sb("w_rt", [P, KD, GROUPS + NE])
        ident = sb("ident", [P, P])
        ones = sb("ones", [P, P])
        before = sb("before", [P, P])
        upto = sb("upto", [P, P])
        causal0 = sb("causal0", [P, P])
        vrows = gla_mem[0:42, 1536:1664]
        vT = sb("vT", [P, 42])
        rows = gla_mem[0:1, 1664:1892]
        rowb = sb("rowb", [P, 228])
        g_out_b, g_ki_b, b_rt_b = rowb[:, 0:128], rowb[:, 128:192], rowb[:, 192:228]
        bada = sb("bada", [16, 3, P])
        mrow = gla_mem[:, 1024:1536]
        m16 = sb("m16", [16, 3, P])
        modT = sb("modT", [P, 3, 16])
        cs = sb("cs", [P, KD])
        c32 = sb("c32", [P, KD, 32])
        scale1 = sb("scale1", [P, KD])
        scale2 = sb("scale2", [P, KD])
        gatev = sb("gatev", [P, 2, KD])
        posi = sb("posi", [P, TT], I32)
        posf = sb("posf", [P, TT])
        rope = sb("rope", [P, 4, TT, HALF])
        nsin = sb("nsin", [P, TT, HALF])
        rtmp_mem = sb("rtmp_mem", [P, HEADS * ROT])
        rtmp = rtmp_mem[:, :].rearrange("p (h r) -> p h r", h=HEADS)
        st = sb("st", [P, 64])
        wi = sb("wi", [P, TT, 8])
        m8 = sb("m8", [P, 8])
        sm = sb("sm", [P, 2, 8])
        dec = sb("dec", [P, 2])
        bend = sb("bend", [P, 2])
        a2 = gvs[0:RANK, (KD + TT) * NS:(KD + TT) * NS + 256]
        gaT = sig_mem[0:RANK, 3584:4096]
        mask_f = mask[:, :, :].rearrange("p a n -> p (a n)")
        lg = sb("lg", [P, TT, GROUPS + NE])
        gp = sb("gp", [P, TT, 8])
        top = sb("top", [P, TT, 8])
        topi = sb("topi", [P, TT, 8], U32)
        etop = sb("etop", [P, TT, 8])
        etopi = sb("etopi", [P, TT, 8], U32)
        rt = rtmp_mem[:, 0:64].rearrange("p (a t) -> p a t", t=TT)
        ohg = sb("ohg", [P, TT, 2, GROUPS])
        el = mask_f[:, 0:128].rearrange("p (t e) -> p t e", t=TT)
        e1 = mask_f[:, 128:256].rearrange("p (t e) -> p t e", t=TT)
        e2 = mask_f[:, 256:384].rearrange("p (t e) -> p t e", t=TT)
        em = mask_f[:, 384:512].rearrange("p (t e) -> p t e", t=TT)
        rpos = mask_f[:, 512:640].rearrange("p (t e) -> p t e", t=TT)
        rtmp3 = mask_f[:, 640:768].rearrange("p (t e) -> p t e", t=TT)
        cnt = mask_f[:, 768:1024].rearrange("p (a e) -> p a e", a=8)
        ovc = mask_f[:, 1024:1536].rearrange("p (a e) -> p a e", a=NOV)
        ovi = sb("ovi", [P, NOV + 2], I32)
        ovf = sb("ovf", [P, NOV + 2])
        iota = sb("iota", [P, NE], I32)
        iotaf = sb("iotaf", [P, NE])
        arena_r, gvs_r, gqk_r, qT_r, qi_r, stage_r, mask_r, kiT_r = (rounded(name, n) for name, n in (
            ("arena", 4 * WELEM), ("gvs", 4096), ("gqk", 2048), ("qT", 2048), ("qi_mem", 2048), ("stage_mem", 2048), ("mask", 1536), ("kiT", SEQ)))
        spots = {0: 0, 1: 4096, 2: 8192, 3: 12288, "H": 16384, "B": 20480}
        area = {key: arena[:, n:n + 4096] for key, n in spots.items()}
        area_r = {key: arena_r[:, n:n + 4096] for key, n in spots.items()}
        area_r["G"] = gvs_r[:, :]
        g_all, q_all = (v[:, :, :].rearrange("p a n -> p (a n)") for v in (gqk, qT))
        splits = {key: (area[raw], area_r[lo], area_r[hi]) for key, raw, lo, hi in (
            ("h", "H", "G", "B"), (("proj", 0), 1, 1, 3), (("in", O_BG + 512), 2, 2, "H"), (("in", O_BG + D + 512), 0, 0, 3),
            (("proj", 1), 1, 1, 2), (("out", 0), "H", "H", "B"), (("out", 1), 3, 3, "G"))}
        splits["g"], splits["q"] = (g_all, gqk_r[:, :], qi_r[:, :]), (q_all, qT_r[:, :], stage_r[:, :])
        split_at = {key: n for n, key in enumerate(["h", ("proj", 0), "g", "q", ("in", O_BG + 512), ("in", O_BG + D + 512),
                                                    ("proj", 1), ("out", 0), ("out", 1)])}

        def parts(key, k):
            return [v.rearrange("p (k n) -> p k n", k=k) for v in (splits[key][2], splits[key][1])]

        def mixT(b, part, n, size):
            if b:
                return qi_r[:, 1024 * part + n:1024 * part + n + size]
            if part and n >= 512:
                return kiT_r[:, n - 512:n - 512 + size]
            return mask_r[:, 1024 * part + n:1024 * part + n + size]

        def x1(tt):
            return (g_all if tt < 2 else q_all)[:, D * (tt % 2):D * (tt % 2 + 1)]

        lo_hot = gla_mem[:, 0:1024].rearrange("p (c n) -> p c n", c=2 * TT)
        hi_ge = stage_mem[:, 0:2 * TT * (NPALL + 1)].rearrange("p (c n) -> p c n", c=2 * TT)
        hi_hot = stage_mem[:, 256:256 + 2 * TT * NPALL].rearrange("p (c n) -> p c n", c=2 * TT)
        slot_f = sb("slot_f", [P, 2, NPALL])
        dst_i = sb("dst_i", [P, NPALL], U32)
        src_i = sb("src_i", [P, NPALL], U32)
        idx_c = sb("idx_c", [P, 2, 2], U32)
        spos = sb("spos", [P, TT, 2])
        iota_hi = sb("iota_hi", [P, NPALL + 1])
        iota_lo = sb("iota_lo", [P, P])
        hi_n, lo_n = cnt[:, 5, 0:2 * TT], cnt[:, 6, 0:2 * TT]
        rowid = sb("rowid", [P, TT, 2])

        names = ["A0", "A1", "S0", "S1", "T0", "T1", "O", "G"]
        ps, bank = {}, {}
        for n in names:
            ps[n] = ctx.enter_context(nc.psum_tensor("ps" + n, [P, 512], F32))
            bank[n] = Bank(sem(n + "_full"), sem(n + "_free"))

        ld_x = [sem(f"ld_x{t}") for t in range(TT)]
        ld_vec, ld_rows, ld_pos, ld_bada = (sem(n) for n in ("ld_vec", "ld_rows", "ld_pos", "ld_bada"))
        ld_small, ld_a2, ld_rt = sem("ld_small"), sem("ld_a2"), sem("ld_rt")
        ring_in = [sem(f"ring_in{i}") for i in range(4)]
        ring_out = sem("ring_out")
        const_ready = sem("const_ready")
        vT_ready, rowb_ready, c_ready = sem("vT_ready"), sem("rowb_ready"), sem("c_ready")
        ss_ready, rs_ready, xn_ready = sem("ss_ready"), sem("rs_ready"), sem("xn_ready")
        hraw, h_ready = sem("hraw"), sem("h_ready")
        mrow_ready, m16_in, m16_ready, mod_ready = (sem(n) for n in ("mrow_ready", "m16_in", "m16_ready", "mod_ready"))
        sin_in, sin_out, rope_ready = sem("sin_in"), sem("sin_out"), sem("rope_ready")
        stage_in, stage_roped = sem("stage_in"), sem("stage_roped")
        ikw_in, ki_ready, wi_ready = sem("ikw_in"), sem("ki_ready"), sem("wi_ready")
        qiT_ready, kiT_ready, qT_ready, kT_ready, val_ready = (sem(n) for n in ("qiT_ready", "kiT_ready", "qT_ready", "kT_ready", "val_ready"))
        gaT_ready, z_in, zexp_ready, b_ready = (sem(n) for n in ("gaT_ready", "z_in", "zexp_ready", "b_ready"))
        relu_ready, relu_used, mask_ready, causal_ready = (sem(n) for n in ("relu_ready", "relu_used", "mask_ready", "causal_ready"))
        s_masked, p_exp, p_ready, p_used = (sem(n) for n in ("s_masked", "p_exp", "p_ready", "p_used"))
        pT_ready, ob_ready = [sem("pT_ready0"), sem("pT_ready1")], sem("ob_ready")
        gqk_ready, gv_ready, gs_in, gs_ready = (sem(n) for n in ("gqk_ready", "gv_ready", "gs_in", "gs_ready"))
        ex_in, ex_exp, ex_ready = (sem(n) for n in ("ex_in", "ex_exp", "ex_ready"))
        kN_ready, sc_ready, state_ready, oss_ready, oms_ready, osq_ready, oan_ready, oa_ready = (
            sem(n) for n in ("kN_ready", "sc_ready", "state_ready", "oss_ready", "oms_ready", "osq_ready", "oan_ready", "oa_ready"))
        sig_ready, mix_ready = sem("sig_ready"), sem("mix_ready")
        mixT_ready = [sem("mixT_act"), sem("mixT_dve")]
        h2T_ready = [sem("h2T_dve"), sem("h2T_act")]
        h2g_ready = [sem("h2g_dve"), sem("h2g_act")]
        gd_ready = sem("gd_ready")
        ld_xr = [sem("ld_xr0"), sem("ld_xr1")]
        rss_ready, rms_ready, rsq_ready, x1_ready, xss_ready, xms_ready, xsq_ready, xn2_ready = (
            sem(n) for n in ("rss_ready", "rms_ready", "rsq_ready", "x1_ready", "xss_ready", "xms_ready", "xsq_ready", "xn2_ready"))
        xn2_stored = [sem("xn2_stored0"), sem("xn2_stored1")]
        lg_ready, ge_in, ge_out, em_ready, pos_ready, route_ready = (
            sem(n) for n in ("lg_ready", "ge_in", "ge_out", "em_ready", "pos_ready", "route_ready"))
        slot_ready, ada_out = sem("slot_ready"), sem("ada_out")
        ada_in = [sem("ada_in0"), sem("ada_in1")]
        we_in, we_used = [sem("we_in0"), sem("we_in1")], sem("we_used")
        xg_in, idx_set, silu_ready, act_ready, actT_ready, yb_ready = (
            sem(n) for n in ("xg_in", "idx_set", "silu_ready", "act_ready", "actT_ready", "yb_ready"))
        y_stored, yb_act = [sem("y_stored0"), sem("y_stored1")], sem("yb_act")
        yc_in = [sem(f"yc_in{t}") for t in range(TT)]
        fw_ready, fss_ready, fms_ready, fsq_ready, fin_ready, out_done = (
            sem(n) for n in ("fw_ready", "fss_ready", "fms_ready", "fsq_ready", "fin_ready", "out_done"))
        dstep, pstep, h2m_ready, xg_clear = (sem(n) for n in ("dstep", "pstep", "h2m_ready", "xg_clear"))
        sin_in2, c32_ready, lnv_ready, lnq_ready, pstep_const = (sem(n) for n in ("sin_in2", "c32_ready", "lnv_ready", "lnq_ready", "pstep_const"))
        fsq_in, idx_seen, ex_sub = sem("fsq_in"), sem("idx_seen"), sem("ex_sub")
        hi_ready, lo_ready = sem("hi_ready"), sem("lo_ready")
        where, moe_base = {}, {}

        block = ctx.enter_context(nc.Block())

        items = [("ada", 0, q) for q in range(4)]
        items += [("in", O_IQ), ("in", O_DK), ("in", O_DQ), ("in", O_DV), ("in", O_GQ), ("in", O_GV), ("in", O_GG)]
        items += [("in", O_BG), ("in", O_BG + D), ("proj", 0), ("in", O_BG + 512), ("in", O_BG + D + 512), ("proj", 1)]
        items += [("out", 0), ("out", 1)]
        item_at = {it: n for n, it in enumerate(items)}

        def slot_of(it):
            if it in splits:
                return splits[it][0]
            return ring[:, item_at[it] % 4, :]

        def ring_wait(eng, it):
            n = item_at[it]
            extra = sum(1 for m, o in enumerate(items[:n + 1]) if m % 4 == n % 4 and o[0] == "proj")
            eng.wait_ge(ring_in[n % 4], 16 * (n // 4 + 1 + extra))

        def filled(eng, turn, name=None):
            name = name or where[turn]
            eng.wait_ge(bank[name].full, bank[name].at[turn] + 1)
            return ps[name], bank[name].free

        @block.tensor
        def _(pe):
            def take(name, turn):
                n = bank[name].turn(turn)
                if n:
                    pe.wait_ge(bank[name].free, n)
                return ps[name]

            flip = {"T": 0, "A": 0}

            def take_next(kind, turn):
                name = f"{kind}{flip[kind] % 2}"
                flip[kind] += 1
                where[turn] = name
                return take(name, turn), bank[name].full

            pe.wait_ge(const_ready, 1)
            pe.wait_ge(ld_vec, 16 * 6)
            t, full = take_next("T", "vec")
            nc.tensor.transpose(t[:, 0:42], vrows[:, :], ident[0:42, 0:42]).then_inc(full, 1)
            pe.wait_ge(const_ready, 2)
            pe.wait_ge(ld_rows, 16 * 4)
            g = take("G", "rows")
            nc.tensor.matmul(g[:, 0:228], ones[0:1, :], rows[:, :], start=True, stop=True).then_inc(bank["G"].full, 1)
            for k in range(KD):
                t, full = take_next("T", ("x", k))
                for tt in range(TT):
                    if k == 0:
                        pe.wait_ge(xn_ready, tt + 1)
                    last = nc.tensor.transpose(t[:, tt * P:(tt + 1) * P], x_in[:, tt, k * P:(k + 1) * P], ident[:, :])
                last.then_inc(full, 1)

            def ada(grp):
                if grp == 0:
                    pe.wait_ge(c32_ready, 1)
                a, full = take_next("A", ("ada", grp))
                for k in range(KD):
                    it = ("ada", grp, k // 2)
                    if k % 2 == 0:
                        ring_wait(pe, it)
                    w = slot_of(it).rearrange("p (k n) -> p k n", k=2)
                    for j in range(4):
                        last = nc.tensor.matmul(a[32 * j:32 * j + 32, :], c32[:, k, :], w[:, k % 2, j * 512:(j + 1) * 512],
                                                start=(k == 0), stop=(k == KD - 1))
                    if k % 2 == 1:
                        last.then_inc(ring_out, 1)
                pe.wait_ge(ring_out, item_at[("ada", grp, 3)] + 1)
                pe.sem_inc(full, 1)

            def ada_step(m):
                grp, k = 1 + m // KD, m % KD
                pe.wait_ge(ada_in[m % 2], 16 * (m // 2 + 1))
                if k == 0:
                    take("O", ("ada", grp))
                    where[("ada", grp)] = "O"
                o = ps["O"]
                for j in range(4):
                    last = nc.tensor.matmul(o[32 * j:32 * j + 32, :], c32[:, k, :], adab[:, m % 2, j * 512:(j + 1) * 512],
                                            start=(k == 0), stop=(k == KD - 1))
                last.then_inc(ada_out, 1)
                if k == KD - 1:
                    pe.wait_ge(ada_out, m + 1)
                    pe.sem_inc(bank["O"].full, 1)

            def ada_turn(grp):
                pe.wait_ge(m16_ready, grp + 1)
                t, full = take_next("T", ("mod", grp))
                nc.tensor.transpose(t[:, 0:16], m16[:, grp, :], ident[0:16, 0:16]).then_inc(full, 1)

            ada(0)
            ada_turn(0)

            def inproj(it, tt):
                if it in splits:
                    return inproj_split(it, tt)
                ring_wait(pe, it)
                a, full = take_next("A", (it, tt))
                w = slot_of(it).rearrange("p (k n) -> p k n", k=KD)
                for k in range(KD):
                    if tt == 0 and it == ("in", O_IQ):
                        pe.wait_ge(h_ready, k + 1)
                    last = nc.tensor.matmul(a[:, :], hT[:, k, tt * P:(tt + 1) * P], w[:, k, :], start=(k == 0), stop=(k == KD - 1))
                last.then_inc(full, 1)
                if tt == TT - 1:
                    pe.wait_ge(full, bank[where[(it, tt)]].at[(it, tt)] + 1)
                    pe.sem_inc(ring_out, 1)

            def split_matmul(acc, lhs, rhs, start, stop):
                nc.tensor.matmul(acc, lhs[0], rhs[0], start=start, stop=False)
                nc.tensor.matmul(acc, lhs[0], rhs[1], start=False, stop=False)
                return nc.tensor.matmul(acc, lhs[1], rhs[0], start=False, stop=stop)

            def split_wait(key):
                pe.wait_ge(hi_ready, split_at[key] + 1)
                pe.wait_ge(lo_ready, split_at[key] + 1)

            def inproj_split(it, tt):
                split_wait("h")
                split_wait(it)
                h, w = parts("h", KD), parts(it, KD)
                a, full = take_next("A", (it, tt))
                for k in range(KD):
                    last = split_matmul(a[:, :], [v[:, k, tt * P:(tt + 1) * P] for v in h], [v[:, k, :] for v in w], k == 0, k == KD - 1)
                last.then_inc(full, 1)
                if tt == TT - 1:
                    pe.wait_ge(full, bank[where[(it, tt)]].at[(it, tt)] + 1)
                    pe.sem_inc(ring_out, 1)

            def inproj_T(it, cb):
                ring_wait(pe, it)
                a, full = take_next("A", (it, cb))
                w = slot_of(it).rearrange("p (k n) -> p k n", k=KD)
                for k in range(KD):
                    last = nc.tensor.matmul(a[:, :], w[:, k, cb * P:(cb + 1) * P], hT[:, k, :], start=(k == 0), stop=(k == KD - 1))
                last.then_inc(full, 1)
                if cb == 3:
                    pe.wait_ge(full, bank[where[(it, cb)]].at[(it, cb)] + 1)
                    pe.sem_inc(ring_out, 1)

            nstage = [0]

            def turn_stage(what, tt):
                pe.wait_ge(stage_roped, nstage[0] + 1)
                t, full = take_next("T", (what, tt))
                for cb in range(4):
                    last = nc.tensor.transpose(t[:, cb * P:(cb + 1) * P], stage[:, nstage[0] % 4, cb * P:(cb + 1) * P], ident[:, :])
                last.then_inc(full, 1)
                nstage[0] += 1

            for tt in range(TT):
                inproj(("in", O_IQ), tt)
            pe.wait_ge(ld_small, 32)
            for tt in range(TT):
                a, full = take_next("A", ("small", tt))
                for k in range(KD):
                    last = nc.tensor.matmul(a[:, 0:NS], hT[:, k, tt * P:(tt + 1) * P], w_small[:, k, :], start=(k == 0), stop=(k == KD - 1))
                last.then_inc(full, 1)
            for tt in range(TT):
                inproj(("in", O_DK), tt)
                turn_stage("iq", tt)
            pe.wait_ge(ki_ready, 1)
            t, full = take_next("T", "ki")
            for tt in range(TT):
                last = nc.tensor.transpose(t[:, tt * P:(tt + 1) * P], kin[:, tt, :, :].rearrange("p a n -> p (a n)"), ident[:, :])
            last.then_inc(full, 1)
            t, full = take_next("T", "ga")
            for tt in range(TT):
                last = nc.tensor.transpose(t[0:RANK, tt * P:(tt + 1) * P], ikw[:, tt, 0:RANK], ident[:, :])
            last.then_inc(full, 1)

            def index_scores(tq, hp):
                n = (tq + 1) * P
                if (tq, hp) == (1, 0):
                    pe.wait_ge(kiT_ready, 1)
                    pe.wait_ge(qiT_ready, TT)
                for hh in range(2):
                    s = take(f"S{hh}", ("idx", tq, hp))
                    nc.tensor.matmul(s[:, 0:n], qiT[64 * hh:64 * hh + 64, hp, tq * P:(tq + 1) * P], kiT[64 * hh:64 * hh + 64, 0:n],
                                     start=True, stop=True).then_inc(bank[f"S{hh}"].full, 1)

            fill = [lambda tt=tt: (inproj(("in", O_DQ), tt), turn_stage("dk", tt)) for tt in range(TT)]
            fill += [lambda tt=tt: (inproj(("in", O_DV), tt), turn_stage("dq", tt)) for tt in range(TT)]
            for n in range(3 * PAIRS):
                index_scores(1 + n // PAIRS, n % PAIRS)
                if n in (1, 3):
                    r = n // 2
                    pe.wait_ge(gaT_ready, 1)
                    pe.wait_ge(ld_a2, 16)
                    z = take("G", ("z", r))
                    nc.tensor.matmul(z[:, :], a2[:, r * P:(r + 1) * P], gaT[:, :], start=True, stop=True).then_inc(bank["G"].full, 1)
                if n < KD:
                    ada_step(2 * n)
                    ada_step(2 * n + 1)
                if n in (6, 10):
                    ada_turn(1 + n // 10)
                if n % 3 != 1:
                    fill.pop(0)()

            def attn_scores(u):
                tq, hp = u // PAIRS, u % PAIRS
                n = (tq + 1) * P
                if u == 0:
                    pe.wait_ge(kT_ready, TT)
                    pe.wait_ge(qT_ready, TT)
                for hh in range(2):
                    s = take(f"S{hh}", ("att", u))
                    nc.tensor.matmul(s[:, 0:n], qT[64 * hh:64 * hh + 64, hp, tq * P:(tq + 1) * P], kT[64 * hh:64 * hh + 64, hp, 0:n],
                                     start=True, stop=True).then_inc(bank[f"S{hh}"].full, 1)

            def attn_out(u):
                tq, hp = u // PAIRS, u % PAIRS
                for hh in range(2):
                    pe.wait_ge(p_ready, 2 * u + hh + 1)
                    t, full = take_next("T", ("p", u, hh))
                    for kb in range(tq + 1):
                        last = nc.tensor.transpose(t[:, kb * P:(kb + 1) * P], prob[:, u % 2, hh, kb * P:(kb + 1) * P], ident[:, :])
                    last.then_inc(full, 1)
                if u == 0:
                    pe.wait_ge(val_ready, TT)
                o = take("O", ("att", u))
                for kb in range(tq + 1):
                    for hh in range(2):
                        if kb == 0:
                            pe.wait_ge(pT_ready[hh], u + 1)
                        last = nc.tensor.matmul(o[64 * hh:64 * hh + 64, 0:P], val[:, kb, (2 * hp + hh) * HD:(2 * hp + hh + 1) * HD],
                                                probT[:, u % 2, hh, kb * P:(kb + 1) * P], start=(kb == 0), stop=(kb == tq))
                last.then_inc(bank["O"].full, 1)

            def gla_scores(ch):
                pe.wait_ge(ex_ready, 6 * ch + 6)
                t, full = take_next("T", ("kN", ch))
                for r in range(2):
                    last = nc.tensor.transpose(t[:, r * P:(r + 1) * P], expo[:, r, 768:896], ident[:, :])
                last.then_inc(full, 1)
                sc = [take(n, ("sc", ch)) for n in ("G", "O")]
                for r in range(2):
                    for i in range(NB):
                        for hh in range(2):
                            lo = 64 * hh
                            last = nc.tensor.matmul(sc[hh][:, r * P + i * BLK:r * P + (i + 1) * BLK], expo[lo:lo + 64, r, i * P:(i + 1) * P],
                                                    expo[lo:lo + 64, r, 512 + i * BLK:512 + (i + 1) * BLK], start=True, stop=True)
                            if r == 1 and i == NB - 1:
                                last.then_inc(bank["GO"[hh]].full, 1)

            def gla_out(ch):
                pe.wait_ge(sc_ready, 2 * ch + 2)
                pe.wait_ge(gv_ready, TT)
                o = [take(n, ("o", ch)) for n in ("G", "O")]
                if ch:
                    pe.wait_ge(state_ready, 2 * ch)
                for r in range(2):
                    for hh in range(2):
                        h, lo = 2 * r + hh, 64 * hh
                        if ch:
                            nc.tensor.matmul(o[hh][:, r * P:(r + 1) * P], expo[lo:lo + 64, r, 640:768], state[lo:lo + 64, r, :], start=True, stop=False)
                        last = nc.tensor.matmul(o[hh][:, r * P:(r + 1) * P], scT[:, h, :], gv[:, ch, h * P:(h + 1) * P], start=(ch == 0), stop=True)
                        if r == 1:
                            last.then_inc(bank["GO"[hh]].full, 1)
                if ch < TT - 1:
                    pe.wait_ge(kN_ready, ch + 1)
                    t, full = take_next("T", ("state", ch))
                    for r in range(2):
                        for hh in range(2):
                            h = 2 * r + hh
                            last = nc.tensor.matmul(t[64 * hh:64 * hh + 64, r * P:(r + 1) * P], kN[:, r * P + 64 * hh:r * P + 64 * hh + 64],
                                                    gv[:, ch, h * P:(h + 1) * P], start=True, stop=True)
                    last.then_inc(full, 1)

            def gla_turn(ch):
                pe.wait_ge(oan_ready, 4 * (ch + 1))
                t, full = take_next("T", ("oa", ch))
                for h in range(GLA_H):
                    last = nc.tensor.transpose(t[:, h * P:(h + 1) * P], oan[:, h * P:(h + 1) * P], ident[:, :])
                last.then_inc(full, 1)

            fill = [lambda cb=cb: inproj_T(("in", O_GQ), cb) for cb in range(4)]
            fill += [lambda tt=tt: inproj(("in", O_GV), tt) for tt in range(TT)]
            fill += [lambda tt=tt: inproj(("in", O_GG), tt) for tt in range(TT)]
            fill += [lambda tt=tt: inproj(("in", O_BG), tt) for tt in range(TT)]
            for u in range(NU + 1):
                ch, odd = (u - GLA_AT) // 2, (u - GLA_AT) % 2
                if u < NU:
                    attn_scores(u)
                if odd and 0 <= ch < TT:
                    gla_out(ch)
                if fill:
                    fill.pop(0)()
                if not odd and 0 < ch <= TT:
                    gla_turn(ch - 1)
                if u:
                    attn_out(u - 1)
                if not odd and 0 <= ch < TT:
                    gla_scores(ch)

            def gate_rows(which, tag):
                pe.wait_ge(gd_ready, which + 1)
                for n, name in enumerate(("G", "O")):
                    g = take(name, (tag, n))
                    nc.tensor.matmul(g[:, :], ones[:, :], diag[:, which, n * 512:(n + 1) * 512], start=True, stop=True).then_inc(bank[name].full, 1)

            gate_rows(0, "gm")

            def branches(n, tt):
                split_wait(("proj", n))
                w = parts(("proj", n), KD)
                for b, key in enumerate(("g", "q")):
                    split_wait(key)
                    src = parts(key, 4)
                    a, full = take_next("A", ("y", n, tt, b))
                    for k in range(4):
                        last = split_matmul(a[:, :], [v[:, k, tt * P:(tt + 1) * P] for v in src], [v[:, 4 * b + k, :] for v in w], k == 0, k == 3)
                    last.then_inc(full, 1)
                if tt == TT - 1:
                    pe.wait_ge(full, bank[where[("y", n, tt, 1)]].at[("y", n, tt, 1)] + 1)
                    pe.sem_inc(ring_out, 1)

            for tt in range(TT):
                inproj(("in", O_BG + D), tt)
            for tt in range(TT):
                branches(0, tt)
            for ab in range(2):
                for tt in range(TT):
                    inproj(("in", O_BG + ab * D + 512), tt)
            for tt in range(TT):
                branches(1, tt)

            def mix_turn(tt):
                pe.wait_ge(mix_ready, TT + tt + 1)
                for half in range(2):
                    t, full = take_next("T", ("mix", tt, half))
                    for q in range(4):
                        k = 4 * half + q
                        last = nc.tensor.transpose(t[:, q * P:(q + 1) * P], mix[:, tt, k * P:(k + 1) * P], ident[:, :])
                    last.then_inc(full, 1)

            def out_proj(tt):
                for n in range(2):
                    split_wait(("out", n))
                    w = parts(("out", n), KD)
                    a, full = take_next("A", ("out", tt, n))
                    for k in range(KD):
                        if n == 0 and k == 0:
                            pe.wait_ge(mixT_ready[0], 2 * tt + 2)
                            pe.wait_ge(mixT_ready[1], 2 * tt + 2)
                        last = split_matmul(a[:, :], [mixT(tt % 2, part, P * k, P) for part in range(2)], [v[:, k, :] for v in w], k == 0, k == KD - 1)
                    last.then_inc(full, 1)
                if tt == TT - 1:
                    pe.wait_ge(full, bank[where[("out", tt, 1)]].at[("out", tt, 1)] + 1)
                    pe.sem_inc(ring_out, 2)

            def router(tt):
                pe.wait_ge(xn2_ready, tt + 1)
                for half in range(2):
                    t, full = take_next("T", ("x2", tt, half))
                    for q in range(4):
                        k = 4 * half + q
                        last = nc.tensor.transpose(t[:, q * P:(q + 1) * P], xn2[:, tt % 2, k * P:(k + 1) * P], ident[:, :])
                    last.then_inc(full, 1)
                for half in range(2):
                    pe.wait_ge(h2T_ready[half], 4 * (tt + 1))
                pe.wait_ge(ld_rt, 32)
                g = take("G", ("lg", tt))
                for k in range(KD):
                    last = nc.tensor.matmul(g[:, 0:GROUPS + NE], h2T[:, tt % 2, k, :], w_rt[:, k, :], start=(k == 0), stop=(k == KD - 1))
                last.then_inc(bank["G"].full, 1)

            mix_turn(0)
            for tt in range(TT + 1):
                if tt < TT - 1:
                    mix_turn(tt + 1)
                if tt < TT:
                    out_proj(tt)
                if tt:
                    router(tt - 1)

            pe.wait_ge(em_ready, 1)
            g = take("G", "rank")
            for tt in range(TT):
                for i in range(tt + 1):
                    last = nc.tensor.matmul(g[:, tt * NE:(tt + 1) * NE], (before if i == tt else ones)[:, :], em[:, i, :], start=(i == 0), stop=(i == tt))
            last.then_inc(bank["G"].full, 1)
            o = take("O", "count")
            for i in range(TT):
                last = nc.tensor.matmul(o[:, 0:NE], ones[:, :], em[:, i, :], start=(i == 0), stop=(i == TT - 1))
            last.then_inc(bank["O"].full, 1)
            pe.wait_ge(pos_ready, 1)
            g = take("G", "slots")
            for n in range(2 * TT):
                last = nc.tensor.matmul(g[:, 0:NPALL], lo_hot[:, n, :], hi_hot[:, n, :], start=(n == 0), stop=(n == 2 * TT - 1))
            last.then_inc(bank["G"].full, 1)
            gate_rows(1, "gf")

            base = {n: len(b.at) for n, b in bank.items()}
            moe_base.update(base)

            def pair(j, b, i):
                w0, w1 = (wexp[:, 2 * b + q, :] for q in range(2))
                pe.wait_ge(xg_in, 16 * (j + 1))
                for half in range(2):
                    name = f"T{half}"
                    pe.wait_ge(bank[name].free, base[name] + j)
                    for q in range(4):
                        k = 4 * half + q
                        last = nc.tensor.transpose(ps[name][:, q * P:(q + 1) * P], xg[:, b, k * P:(k + 1) * P], ident[:, :])
                    last.then_inc(bank[name].full, 1)
                pe.wait_ge(bank["G"].free, base["G"] + j)
                pe.wait_ge(we_in[b], 96 * (i + 1))
                for half in range(2):
                    pe.wait_ge(h2g_ready[half], 4 * j + 4)
                for k in range(KD):
                    for q, w in enumerate((w0, w1)):
                        gu = w[:, 0:4096].rearrange("p (g k f) -> p g k f", g=2, k=KD)[:, :, k, :]
                        last = nc.tensor.matmul(ps["G"][64 * q:64 * q + 64, :].rearrange("p (g f) -> p g f", g=2), h2g[:, b, k, 64 * q:64 * q + 64], gu,
                                                start=(k == 0), stop=(k == KD - 1))
                last.then_inc(bank["G"].full, 1)
                pe.wait_ge(act_ready, j + 1)
                pe.wait_ge(bank["O"].free, base["O"] + j)
                for q in range(2):
                    last = nc.tensor.transpose(ps["O"][:, q * P:(q + 1) * P], aact[:, b, q * P:(q + 1) * P], ident[:, :])
                last.then_inc(bank["O"].full, 1)
                pe.wait_ge(actT_ready, j + 1)
                for n in range(2):
                    name = f"A{n}"
                    pe.wait_ge(bank[name].free, base[name] + j)
                    for kf in range(2):
                        for q, w in enumerate((w0, w1)):
                            wd = w[:, 4096:6144].rearrange("p (k n) -> p k n", k=2)
                            last = nc.tensor.matmul(ps[name][64 * q:64 * q + 64, :], actT[:, b, kf, 64 * q:64 * q + 64],
                                                    wd[:, kf, n * 512:(n + 1) * 512], start=(kf == 0), stop=(kf == 1))
                    last.then_inc(bank[name].full, 1)
                pe.wait_ge(bank["A1"].full, base["A1"] + j + 1)
                pe.sem_inc(we_used, 1)

            with pe.Fori(0, NPAIR // 2) as i:
                pair(2 * i, 0, i)
                pair(2 * i + 1, 1, i)
            pe.wait_ge(route_ready, 1)
            n_ov = pe.value_load(ovi[0:1, NOV:NOV + 1], min_val=0, max_val=NOV // 2)
            with pe.If(n_ov > 0):
                with pe.Fori(0, n_ov) as v:
                    pair(NPAIR + v, 0, NPAIR // 2 + v)

        @block.sync
        def _(sp):
            for tt in range(TT):
                sp.dma_start(x_in[:, tt, :], x_v[:, tt, :]).then_inc(ld_x[tt], 16)
            vecs = (g_pre_mix, g_pre_ffn, g_post_mix, g_post_ffn)
            for n, v in enumerate(vecs):
                sp.dma_start(vrows[8 * n:8 * n + 8, :], v[0].rearrange("(k p) -> k p", p=P)).then_inc(ld_vec, 16)
            sp.dma_start(vrows[32:34, :], b_gla_a[0].rearrange("(k p) -> k p", p=P)).then_inc(ld_vec, 16)
            sp.dma_start(vrows[34:42, :], c[0].rearrange("(k p) -> k p", p=P)).then_inc(ld_vec, 16)

            def load(n):
                it = items[n]
                if n >= 4:
                    sp.wait_ge(ring_out, {15: 13, 16: 14, 17: 15, 18: 16}.get(n, n - 3))
                dst, s = slot_of(it), ring_in[n % 4]
                if it[0] == "ada":
                    grp, q = it[1:]
                    sp.dma_start(dst.rearrange("p (k n) -> p k n", k=2), ada_v[:, 2 * q:2 * q + 2, grp * 2048:(grp + 1) * 2048]).then_inc(s, 16)
                elif it[0] == "in":
                    sp.dma_start(dst.rearrange("p (k n) -> p k n", k=KD), win_v[:, :, it[1]:it[1] + 512]).then_inc(s, 16)
                elif it[0] == "proj":
                    w = dst.rearrange("p (b k n) -> p b k n", b=2, k=4)
                    for b, src in enumerate((pg_v, pd_v)):
                        sp.dma_start(w[:, b, :, :], src[:, :, it[1] * 512:(it[1] + 1) * 512]).then_inc(s, 16)
                else:
                    sp.dma_start(dst.rearrange("p (k n) -> p k n", k=KD), wo_v[:, :, it[1] * 512:(it[1] + 1) * 512]).then_inc(s, 16)

            for n in range(4):
                load(n)
            load(4)
            load(5)
            sp.dma_start(w_small[:, :, 0:RANK], win_v[:, :, O_GA:O_GA + RANK]).then_inc(ld_small, 16)
            sp.dma_start(w_small[:, :, RANK:NS], win_v[:, :, O_IK:O_IK + 72]).then_inc(ld_small, 16)
            sp.dma_start(a2[:, :], w_gla_a2[0]).then_inc(ld_a2, 16)
            for n in range(6, len(items)):
                load(n)
                if n == 8:
                    sp.dma_start(w_rt[:, :, 0:GROUPS], w_router_g[0].rearrange("(k p) n -> p k n", p=P)).then_inc(ld_rt, 16)
                    sp.dma_start(w_rt[:, :, GROUPS:], w_router_e[0].rearrange("(k p) n -> p k n", p=P)).then_inc(ld_rt, 16)

            def experts(b, e0, e1_):
                for q, e in enumerate((e0, e1_)):
                    w = wexp[:, 2 * b + q, :]
                    for dst, src, kk in ((w[:, 0:2048], weg_v, KD), (w[:, 2048:4096], weu_v, KD), (w[:, 4096:6144], wed_v, 2)):
                        sp.dma_start(dst.rearrange("p (k f) -> p k f", k=kk), src[bass.ds(e, 1), :, :, :].rearrange("a p k f -> p (a k) f")).then_inc(we_in[b], 16)

            sp.wait_ge(ring_out, item_at[("proj", 1)] + 1)
            experts(0, 0, 1)
            sp.wait_ge(ring_out, len(items))
            experts(1, 2, 3)
            with sp.Fori(1, NPAIR // 2) as i:
                sp.wait_ge(we_used, 2 * i - 1)
                experts(0, 4 * i, 4 * i + 1)
                sp.wait_ge(we_used, 2 * i)
                experts(1, 4 * i + 2, 4 * i + 3)
            sp.wait_ge(route_ready, 1)
            n_ov = sp.value_load(ovi[0:1, NOV:NOV + 1], min_val=0, max_val=NOV // 2)
            with sp.If(n_ov > 0):
                with sp.Fori(0, n_ov) as v:
                    e_a = sp.value_load(ovi[0:1, bass.ds(2 * v, 1)], min_val=0, max_val=NE - 1)
                    e_b = sp.value_load(ovi[0:1, bass.ds(2 * v + 1, 1)], min_val=0, max_val=NE - 1)
                    sp.wait_ge(we_used, NPAIR + v)
                    experts(0, e_a, e_b)
            sp.wait_ge(y_stored[1], 16 * NPAIR // 2)
            sp.wait_ge(y_stored[0], 16 * (NPAIR // 2 + n_ov))
            for tt in range(TT):
                sp.dma_start(yc[:, tt, :, :], y_dram.rearrange("(w t p) n -> t p w n", w=2, p=P)[tt]).then_inc(yc_in[tt], 16)
            for tt in range(TT):
                sp.wait_ge(fin_ready, tt + 1)
                sp.dma_start(out_v[:, tt, :], x1(tt)).then_inc(out_done, 16)
            sp.wait_ge(out_done, 16 * TT)

        @block.gpsimd
        def _(pool):
            def step(ins):
                pstep_n[0] += 1
                ins.then_inc(pstep, 1)
                pool.wait_ge(pstep, pstep_n[0])

            pstep_n = [0]
            pool.dma_start(posi[:, :], positions[0].rearrange("(t p) -> p t", p=P), allow_slow_non_contiguous=True).then_inc(ld_pos, 16)
            pool.dma_start(rows[:, 0:128], g_gla_out).then_inc(ld_rows, 16)
            pool.dma_start(rows[:, 128:192], g_idx_k).then_inc(ld_rows, 16)
            pool.dma_start(rows[:, 192:196], b_router_g).then_inc(ld_rows, 16)
            pool.dma_start(rows[:, 196:228], b_router_e).then_inc(ld_rows, 16)
            pool.dma_start(bada[:, :, :], b_ada[0].rearrange("(g r p) -> r g p", r=16, p=P)).then_inc(ld_bada, 16)
            step(pool.memset(ident[:, :], 0.0))
            pool.affine_select(out=ident[:, :], in_=ident[:, :], compare_op=ALU.not_equal, fill=1.0, base=0,
                               pattern=[[-1, P]], channel_multiplier=1).then_inc(const_ready, 1)
            pool.memset(ones[:, :], 1.0).then_inc(const_ready, 1)
            pool.wait_ge(const_ready, 2)
            step(pool.affine_select(out=before[:, :], in_=ones[:, :], compare_op=ALU.is_gt, fill=0.0, base=0,
                                    pattern=[[1, P]], channel_multiplier=-1))
            step(pool.affine_select(out=upto[:, :], in_=ones[:, :], compare_op=ALU.is_ge, fill=0.0, base=0,
                                    pattern=[[1, P]], channel_multiplier=-1))
            step(pool.memset(causal0[:, :], 0.0))
            step(pool.affine_select(out=causal0[:, :], in_=causal0[:, :], compare_op=ALU.is_ge, fill=HIDE, base=0,
                                    pattern=[[-1, P]], channel_multiplier=1))
            step(pool.iota(iota[:, :], pattern=[[1, NE]], base=0, channel_multiplier=0))
            step(pool.iota(rowid[:, :, :], pattern=[[P, TT], [SEQ, 2]], base=1, channel_multiplier=1, allow_small_or_imprecise_dtypes=True))
            step(pool.iota(iota_hi[:, :], pattern=[[P, NPALL + 1]], base=0, channel_multiplier=0, allow_small_or_imprecise_dtypes=True))
            step(pool.iota(iota_lo[:, :], pattern=[[1, P]], base=0, channel_multiplier=0, allow_small_or_imprecise_dtypes=True))
            pool.memset(gp[:, :, :], HIDE).then_inc(const_ready, 1)
            pool.sem_inc(pstep_const, 1)

            def rotate(xv, cosv, sinv, nsinv, tmp):
                step(pool.tensor_tensor(tmp[..., 0:HALF], xv[..., HALF:ROT], nsinv, ALU.mult))
                step(pool.tensor_tensor(tmp[..., HALF:ROT], xv[..., 0:HALF], sinv, ALU.mult))
                step(pool.tensor_tensor(xv[..., 0:HALF], xv[..., 0:HALF], cosv, ALU.mult))
                step(pool.tensor_tensor(xv[..., HALF:ROT], xv[..., HALF:ROT], cosv, ALU.mult))
                return pool.tensor_tensor(xv[..., 0:ROT], xv[..., 0:ROT], tmp[..., 0:ROT], ALU.add)

            pool.wait_ge(rope_ready, 1)

            def rope_stage(n):
                pool.wait_ge(stage_in, n + 1)
                if n:
                    pool.wait_ge(stage_roped, n)
                tt = n % TT
                xv = stage[:, n % 4, :].rearrange("p (h d) -> p h d", h=HEADS)
                cs_, sn_, ns_ = (v.unsqueeze(1).broadcast_to([P, HEADS, HALF]) for v in (rope[:, 2, tt, :], rope[:, 3, tt, :], nsin[:, tt, :]))
                rotate(xv, cs_, sn_, ns_, rtmp[:, :, :]).then_inc(stage_roped, 1)

            for n in range(3 * TT):
                rope_stage(n)

            def gla_exponents(ch):
                if ch:
                    filled(pool, ("o", ch - 1), "G")
                    filled(pool, ("o", ch - 1), "O")
                for r in range(2):
                    b = bT[:, r, ch * P:(ch + 1) * P]
                    b3 = b.rearrange("p (i t) -> p i t", i=NB)
                    ref = b3[:, :, BLK // 2 - 1:BLK // 2]
                    pool.tensor_tensor(expo[:, r, 0:512].rearrange("p (i s) -> p i s", i=NB), ref.broadcast_to([P, NB, P]),
                                       b.unsqueeze(1).broadcast_to([P, NB, P]), ALU.subtract).then_inc(ex_sub, 1)
                    pool.tensor_tensor(expo[:, r, 512:640].rearrange("p (i t) -> p i t", i=NB), b3, ref.broadcast_to([P, NB, BLK]),
                                       ALU.subtract).then_inc(ex_sub, 1)

            pool.wait_ge(b_ready, 2 * TT)
            filled(pool, ("idx", TT - 1, PAIRS - 1), "S1")
            pool.wait_ge(rowb_ready, 1)
            for tt in range(TT):
                gla_exponents(tt)
                pool.wait_ge(gs_in, tt + 1)
                g3 = gs[:, tt, :].rearrange("p (h n) -> p h n", h=GLA_H)
                pool.tensor_tensor(g3, g3, g_out_b.unsqueeze(1).broadcast_to([P, GLA_H, P]), ALU.mult).then_inc(gs_ready, 1)
            pool.wait_ge(mixT_ready[1], 2 * TT)
            filled(pool, ("mix", TT - 1, 0))
            filled(pool, ("mix", TT - 1, 1))
            pool.memset(xg[:, :, :], 0.0).then_inc(xg_clear, 1)
            pool.wait_ge(xg_clear, 1)
            pool.wait_ge(slot_ready, 1)
            for b in range(2):
                pool.wait_ge(xn2_stored[b], 32)

            def index(table, which, b, j, count):
                pool.tensor_copy(idx_c[:, which, b:b + 1], table[:, bass.ds(j, 1)]).then_inc(idx_set, 1)
                pool.wait_ge(idx_set, count)
                pool.sem_inc(idx_seen, 1)

            def gather(j, b, count):
                index(src_i, 0, b, j, count)
                pool.indirect_dma_start(out=xg[:, b, :], out_offset=None, in_=xn_dram, in_offset=bass.IndirectOffsetOnAxis(ap=idx_c[:, 0, b:b + 1], axis=0),
                                        bounds_check=SEQ - 1, oob_is_err=False).then_inc(xg_in, 16)

            def gather2(j, b, count):
                pool.wait_ge(bank["T1"].full, moe_base["T1"] + j - 1)
                pool.wait_ge(xg_in, 16 * j)
                gather(j, b, count)

            def scatter(j, b, count, before):
                pool.wait_ge(yb_ready, j + 1)
                pool.wait_ge(yb_act, j + 1)
                if before is not None:
                    pool.wait_ge(y_stored[b], 16 * before)
                index(dst_i, 1, b, j, count)
                pool.indirect_dma_start(out=y_dram, out_offset=bass.IndirectOffsetOnAxis(ap=idx_c[:, 1, b:b + 1], axis=0), in_=yb[:, b, :], in_offset=None,
                                        bounds_check=2 * SEQ - 1, oob_is_err=False).then_inc(y_stored[b], 16)

            gather(0, 0, 1)
            pool.wait_ge(xg_in, 16)
            gather(1, 1, 2)
            pool.wait_ge(xg_in, 32)
            scatter(0, 0, 3, None)
            gather2(2, 0, 4)
            scatter(1, 1, 5, None)
            gather2(3, 1, 6)
            with pool.Fori(1, NPAIR // 2 - 1) as i:
                scatter(2 * i, 0, 4 * i + 3, i)
                gather2(2 * i + 2, 0, 4 * i + 4)
                scatter(2 * i + 1, 1, 4 * i + 5, i)
                gather2(2 * i + 3, 1, 4 * i + 6)
            for b in range(2):
                scatter(NPAIR - 2 + b, b, 2 * NPAIR - 1 + b, NPAIR // 2 - 1)
            n_ov = pool.value_load(ovi[0:1, NOV:NOV + 1], min_val=0, max_val=NOV // 2)
            with pool.If(n_ov > 0):
                with pool.Fori(0, n_ov) as v:
                    gather2(NPAIR + v, 0, 2 * NPAIR + 1 + 2 * v)
                    scatter(NPAIR + v, 0, 2 * NPAIR + 2 + 2 * v, NPAIR // 2 + v)

        @block.scalar
        def _(act):
            scratch = kv[:, 0:D]
            for tt in range(TT):
                act.wait_ge(ld_x[tt], 16)
                nc.scalar.activation(scratch[:, 0:D], x_in[:, tt, :], ACT.Square, accum_out=st[:, tt:tt + 1]).then_inc(ss_ready, 1)
                act.wait_ge(ss_ready, tt + 1)
            act.wait_ge(rs_ready, 1)
            nc.scalar.activation(st[:, 8:12], st[:, 4:8], ACT.Sqrt).then_inc(ss_ready, 1)
            act.wait_ge(vT_ready, 1)
            nc.scalar.activation(cs[:, :], vT[:, 34:42], ACT.Sigmoid).then_inc(c_ready, 1)
            act.wait_ge(sin_in, 1)
            nc.scalar.activation(rope[:, 3, :, :], rope[:, 0, :, :], ACT.Sin).then_inc(sin_out, 1)
            nc.scalar.activation(rope[:, 2, :, :], rope[:, 0, :, :], ACT.Sin, scale=0.5).then_inc(sin_out, 1)
            for k in range(0, KD, 2):
                t, free = filled(act, ("x", k))
                nc.scalar.copy(hT[:, k, :], t[:, :]).then_inc(free, 1)
                act.wait_ge(free, bank[where[("x", k)]].at[("x", k)] + 1)
                act.sem_inc(hraw, 1)

            def mod_row(grp):
                a, free = filled(act, ("ada", grp))
                if grp:
                    act.wait_ge(m16_in, 16 * grp)
                nc.scalar.copy(mrow[:, :], a[:, :]).then_inc(free, 1)
                act.wait_ge(free, bank[where[("ada", grp)]].at[("ada", grp)] + 1)
                act.dma_start(m16[:, grp, :], mrow[0:P:32, :]).then_inc(m16_in, 16)

            mod_row(0)

            nst = [0]

            def to_stage(turn):
                a, free = filled(act, turn)
                n = nst[0]
                if n >= 4:
                    filled(act, stage_turns[n - 4])
                nc.scalar.copy(stage[:, n % 4, :], a[:, :]).then_inc(stage_in, 1)
                act.wait_ge(stage_in, n + 1)
                act.sem_inc(free, 1)
                nst[0] += 1

            stage_turns = [("iq", t) for t in range(TT)] + [("dk", t) for t in range(TT)] + [("dq", t) for t in range(TT)]

            def spread(turn, dst, done):
                t, free = filled(act, turn)
                nc.scalar.copy(dst, t[:, :].rearrange("p (c n) -> p c n", c=4)).then_inc(done, 1)
                act.wait_ge(done, spread_n.setdefault(done.name, 0) + 1)
                spread_n[done.name] += 1
                act.sem_inc(free, 1)

            spread_n = {}
            def ada_load(m):
                act.dma_start(adab[:, m % 2, :], ada_v[:, m % KD, (1 + m // KD) * 2048:(2 + m // KD) * 2048]).then_inc(ada_in[m % 2], 16)

            for m in range(2):
                ada_load(m)
            for tt in range(TT):
                to_stage((("in", O_IQ), tt))
            for tt in range(TT):
                a, free = filled(act, ("small", tt))
                nc.scalar.copy(ikw[:, tt, :], a[:, 0:NS]).then_inc(ikw_in, 1)
                act.wait_ge(ikw_in, tt + 1)
                act.sem_inc(free, 1)
            act.wait_ge(lnv_ready, 1)
            nc.scalar.activation(st[:, 56:60], st[:, 52:56], ACT.Sqrt).then_inc(lnq_ready, 1)
            for tt in range(TT):
                spread(("iq", tt), qiT[:, :, tt * P:(tt + 1) * P], qiT_ready)
                to_stage((("in", O_DK), tt))
            t, free = filled(act, "ki")
            nc.scalar.copy(kiT[:, :], t[:, :]).then_inc(kiT_ready, 1)
            act.wait_ge(kiT_ready, 1)
            act.sem_inc(free, 1)
            t, free = filled(act, "ga")
            nc.scalar.copy(gaT[:, :], t[0:RANK, :]).then_inc(gaT_ready, 1)
            act.wait_ge(gaT_ready, 1)
            act.sem_inc(free, 1)

            def do_dq(tt):
                spread(("dk", tt), kT[:, :, tt * P:(tt + 1) * P], kT_ready)
                to_stage((("in", O_DQ), tt))

            def do_dv(tt):
                spread(("dq", tt), qT[:, :, tt * P:(tt + 1) * P], qT_ready)
                a, free = filled(act, (("in", O_DV), tt))
                nc.scalar.copy(val[:, tt, :], a[:, :]).then_inc(val_ready, 1)
                act.wait_ge(val_ready, tt + 1)
                act.sem_inc(free, 1)

            fill = [lambda tt=tt: do_dq(tt) for tt in range(TT)] + [lambda tt=tt: do_dv(tt) for tt in range(TT)]
            for n in range(3 * PAIRS):
                tq, hp = 1 + n // PAIRS, n % PAIRS
                w = (tq + 1) * P
                if n in (4, 8):
                    mod_row(n // 4)
                for hh in range(2):
                    s, free = filled(act, ("idx", tq, hp), f"S{hh}")
                    if n:
                        act.wait_ge(relu_used, 2 * (n - 1) + hh + 1)
                    nc.scalar.activation(relu[:, hh, 0:w], s[:, 0:w], ACT.Relu, scale=64 ** -0.5).then_inc(relu_ready, 1)
                    act.wait_ge(relu_ready, 2 * n + hh + 1)
                    act.sem_inc(free, 1)
                if n == 6:
                    act.wait_ge(z_in, 1)
                    nc.scalar.activation(zz[:, 1, :, :], zz[:, 1, :, :], ACT.Exp).then_inc(zexp_ready, 1)
                    act.wait_ge(zexp_ready, 1)
                    nc.scalar.activation(zz[:, 2, :, :], zz[:, 1, :, :], ACT.Ln, bias=1.0).then_inc(zexp_ready, 1)
                for m in range(2 * n + 2, min(2 * n + 4, 2 * KD)):
                    act.wait_ge(ada_out, m - 1)
                    ada_load(m)
                if n % 3 != 1:
                    fill.pop(0)()

            def simple(turn, dst, done, count, **kw):
                a, free = filled(act, turn)
                nc.scalar.activation(dst, a[:, :], kw.get("func", ACT.Copy), scale=kw.get("scale", 1.0)).then_inc(done, 1)
                act.wait_ge(done, count)
                act.sem_inc(free, 1)

            fill = [lambda cb=cb: simple((("in", O_GQ), cb), gqk[:, cb, :], gqk_ready, cb + 1, scale=GLA_DK ** -0.5 if cb < 2 else 1.0) for cb in range(4)]
            fill += [lambda tt=tt: simple((("in", O_GV), tt), gv[:, tt, :], gv_ready, tt + 1) for tt in range(TT)]
            fill += [lambda tt=tt: simple((("in", O_GG), tt), gs[:, tt, :], gs_in, tt + 1, func=ACT.Silu) for tt in range(TT)]

            def sigmoid(half, ab, tt):
                turn = (("in", O_BG + ab * D + 512 * half), tt)
                if half:
                    act.wait_ge(mix_ready, tt + 1)
                simple(turn, sig[:, ab, tt, :], sig_ready, half * 2 * TT + ab * TT + tt + 1, func=ACT.Sigmoid)

            fill += [lambda tt=tt: sigmoid(0, 0, tt) for tt in range(TT)]

            def gla_exp(ch):
                act.wait_ge(ex_in, ch + 1)
                nc.scalar.activation(expo[:, :, 0:640], expo[:, :, 0:640], ACT.Exp, scale=1.0 / TAU).then_inc(ex_exp, 1)
                b = bT[:, :, ch * P:(ch + 1) * P]
                nc.scalar.activation(expo[:, :, 640:768], b, ACT.Exp, scale=1.0 / TAU).then_inc(ex_exp, 1)
                for r in range(2):
                    nc.scalar.activation(expo[:, r, 768:896], b[:, r, :], ACT.Exp, bias=bend[:, r:r + 1], scale=-1.0 / TAU).then_inc(ex_exp, 1)

            gscr = stage_mem[:, 0:P]

            def gla_squares(ch):
                for h in range(GLA_H):
                    o, _ = filled(act, ("o", ch), "GO"[h % 2])
                    r = h // 2
                    nc.scalar.activation(gscr, o[:, r * P:(r + 1) * P], ACT.Square, accum_out=st[:, 16 + h:17 + h]).then_inc(oss_ready, 1)
                    act.wait_ge(oss_ready, 4 * ch + h + 1)
                act.wait_ge(oms_ready, ch + 1)
                nc.scalar.activation(st[:, 24:28], st[:, 20:24], ACT.Sqrt).then_inc(osq_ready, 1)

            for u in range(NU + 1):
                tq, hp = u // PAIRS, u % PAIRS
                n = (tq + 1) * P
                ch, odd = (u - GLA_AT) // 2, (u - GLA_AT) % 2
                if u < NU:
                    for hh in range(2):
                        act.wait_ge(s_masked, 2 * u + hh + 1)
                        z = 4 * (u % 2)
                        nc.scalar.activation(prob[:, u % 2, hh, 0:n], prob[:, u % 2, hh, 0:n], ACT.Exp, bias=sm[:, hh, z + 1:z + 2],
                                             scale=HD ** -0.5, accum_out=sm[:, hh, z + 2:z + 3]).then_inc(p_exp, 1)
                if not odd and 0 <= ch < TT:
                    gla_exp(ch)
                if odd and 0 <= ch < TT:
                    gla_squares(ch)
                if fill:
                    fill.pop(0)()
                if u:
                    v = u - 1
                    vq, vp = v // PAIRS, v % PAIRS
                    m = (vq + 1) * P
                    t, free = filled(act, ("p", v, 0))
                    if v >= 2:
                        filled(act, ("att", v - 2), "O")
                    nc.scalar.copy(probT[:, v % 2, 0, 0:m], t[:, 0:m]).then_inc(pT_ready[0], 1)
                    act.wait_ge(pT_ready[0], v + 1)
                    act.sem_inc(free, 1)
                    o, free = filled(act, ("att", v), "O")
                    nc.scalar.copy(qT[:, vp, vq * P:(vq + 1) * P], o[:, 0:P]).then_inc(ob_ready, 1)
                    act.wait_ge(ob_ready, v + 1)
                    act.sem_inc(free, 1)
                if not odd and 0 <= ch < TT:
                    t, free = filled(act, ("kN", ch))
                    if ch:
                        filled(act, ("state", ch - 1))
                    nc.scalar.copy(kN[:, :], t[:, 0:256]).then_inc(kN_ready, 1)
                    act.wait_ge(kN_ready, ch + 1)
                    act.sem_inc(free, 1)
            scratch = gla_mem[:, 0:D]

            def split_hi(key):
                src, _, hi = splits[key]
                nc.scalar.copy(hi, src).then_inc(hi_ready, 1)

            split_hi("h")
            sigmoid(0, 1, 0)
            act.wait_ge(ring_out, item_at[("in", O_BG)] + 1)
            ring_wait(act, ("proj", 0))
            split_hi(("proj", 0))
            sigmoid(0, 1, 1)
            act.wait_ge(oa_ready, TT)
            filled(act, ("gm", 0), "G")
            filled(act, ("gm", 1), "O")
            split_hi("g")
            split_hi("q")
            sigmoid(0, 1, 2)
            sigmoid(0, 1, 3)
            act.wait_ge(ring_out, item_at[("in", O_BG + D)] + 1)
            act.wait_ge(lo_ready, split_at["h"] + 1)
            ring_wait(act, ("in", O_BG + 512))
            split_hi(("in", O_BG + 512))
            for ab, (used, key) in enumerate(((("proj", 0), ("in", O_BG + D + 512)), (("in", O_BG + 512), ("proj", 1)))):
                sigmoid(1, ab, 0)
                act.wait_ge(ring_out, item_at[used] + 1)
                ring_wait(act, key)
                split_hi(key)
                for tt in range(1, TT):
                    sigmoid(1, ab, tt)
            act.wait_ge(ring_out, item_at[("in", O_BG + D + 512)] + 1)
            for n in range(2):
                ring_wait(act, ("out", n))
                split_hi(("out", n))

            def rms_of(tt):
                for n in range(2):
                    a, _ = filled(act, ("out", tt, n))
                    nc.scalar.activation(scratch[:, 0:512], a[:, :], ACT.Square, accum_out=st[:, 28 + n:29 + n]).then_inc(rss_ready, 1)
                    act.wait_ge(rss_ready, 2 * tt + n + 1)
                act.wait_ge(rms_ready, tt + 1)
                nc.scalar.activation(st[:, 31:32], st[:, 30:31], ACT.Sqrt).then_inc(rsq_ready, 1)
                act.wait_ge(x1_ready, tt + 1)
                if tt + 2 < TT:
                    act.dma_start(xres[:, tt % 2, :], x_v[:, tt + 2, :]).then_inc(ld_xr[tt % 2], 16)
                nc.scalar.activation(scratch[:, 0:D], x1(tt), ACT.Square, accum_out=st[:, 33:34]).then_inc(xss_ready, 1)
                act.wait_ge(xss_ready, tt + 1)
                act.wait_ge(xms_ready, tt + 1)
                nc.scalar.activation(st[:, 35:36], st[:, 34:35], ACT.Sqrt).then_inc(xsq_ready, 1)
                act.wait_ge(xn2_ready, tt + 1)
                act.dma_start(xn_dram[tt * P:(tt + 1) * P, :], xn2[:, tt % 2, :]).then_inc(xn2_stored[tt % 2], 16)

            def shifted(dst, src, k, done):
                return nc.scalar.activation(dst, src, ACT.Identity, bias=modT[:, 1, 8 + k:9 + k], scale=scale2[:, k:k + 1]).then_inc(done, 1)

            act.wait_ge(h2m_ready, 1)
            def mix_copy(tt):
                if tt == 1:
                    act.wait_ge(ring_out, item_at[("proj", 1)] + 1)
                if tt >= 2:
                    filled(act, ("out", tt - 2, 1))
                for half in range(2):
                    t, _ = filled(act, ("mix", tt, half))
                    nc.scalar.copy(mixT(tt % 2, 0, 512 * half, 512), t[:, :]).then_inc(mixT_ready[0], 1)

            mix_copy(0)
            act.wait_ge(ring_out, item_at[("proj", 1)] + 1)
            for tt in range(2):
                act.dma_start(xres[:, tt, :], x_v[:, tt, :]).then_inc(ld_xr[tt], 16)
            for tt in range(TT + 1):
                if tt < TT - 1:
                    mix_copy(tt + 1)
                if tt:
                    t, free = filled(act, ("x2", tt - 1, 1))
                    if tt >= 3:
                        filled(act, ("lg", tt - 3), "G")
                    for q in range(4):
                        shifted(h2T[:, (tt - 1) % 2, 4 + q, :], t[:, q * P:(q + 1) * P], 4 + q, h2T_ready[1])
                    act.wait_ge(h2T_ready[1], 4 * tt)
                    act.sem_inc(free, 1)
                if tt < TT:
                    rms_of(tt)
            act.wait_ge(ge_in, 1)
            nc.scalar.activation(gp[:, :, 0:GROUPS], gp[:, :, 0:GROUPS], ACT.Exp)
            nc.scalar.activation(rt[:, 4, :], rt[:, 3, :], ACT.Exp).then_inc(ge_out, 1)

            def pair(j, b, back, stores):
                act.wait_ge(bank["T1"].full, moe_base["T1"] + j + 1)
                act.wait_ge(bank["G"].full, moe_base["G"] + back)
                for q in range(4):
                    shifted(h2g[:, b, 4 + q, :], ps["T1"][:, q * P:(q + 1) * P], 4 + q, h2g_ready[1])
                act.wait_ge(h2g_ready[1], 4 * j + 4)
                act.sem_inc(bank["T1"].free, 1)
                act.wait_ge(bank["G"].full, moe_base["G"] + j + 1)
                nc.scalar.activation(gact[:, b, :], ps["G"][:, 0:DE], ACT.Silu).then_inc(silu_ready, 1)
                act.wait_ge(bank["O"].full, moe_base["O"] + j + 1)
                act.wait_ge(bank["A1"].full, moe_base["A1"] + back)
                nc.scalar.copy(actT[:, b, :, :], ps["O"][:, 0:DE].rearrange("p (k n) -> p k n", k=2)).then_inc(actT_ready, 1)
                act.wait_ge(actT_ready, j + 1)
                act.sem_inc(bank["O"].free, 1)
                act.wait_ge(bank["A1"].full, moe_base["A1"] + j + 1)
                if stores is not None:
                    act.wait_ge(y_stored[b], 16 * stores)
                nc.scalar.copy(yb[:, b, 512:1024], ps["A1"][:, :]).then_inc(yb_act, 1)
                act.wait_ge(yb_act, j + 1)
                act.sem_inc(bank["A1"].free, 1)

            pair(0, 0, 0, None)
            pair(1, 1, 0, None)
            with act.Fori(1, NPAIR // 2) as i:
                pair(2 * i, 0, 2 * i - 1, i)
                pair(2 * i + 1, 1, 2 * i, i)
            n_ov = act.value_load(ovi[0:1, NOV:NOV + 1], min_val=0, max_val=NOV // 2)
            with act.If(n_ov > 0):
                with act.Fori(0, n_ov) as v:
                    pair(NPAIR + v, 0, NPAIR + v, NPAIR // 2 + v)
            scratch2 = stage_mem[:, 0:D]
            for tt in range(TT):
                act.wait_ge(yc_in[tt], 16)
                nc.scalar.activation(yc[:, tt, 0, :], yc[:, tt, 0, :], ACT.Copy, scale=rt[:, 9, tt:tt + 1]).then_inc(fw_ready, 1)
            for tt in range(TT):
                act.wait_ge(fss_ready, tt + 1)
                nc.scalar.activation(scratch2, yc[:, tt, 0, :], ACT.Square, accum_out=st[:, 40:41]).then_inc(fms_ready, 1)
                act.wait_ge(fms_ready, tt + 1)
                act.wait_ge(fsq_in, tt + 1)
                nc.scalar.activation(st[:, 42:43], st[:, 41:42], ACT.Sqrt).then_inc(fsq_ready, 1)

        @block.vector
        def _(dve):
            dn = [0]

            def step(ins):
                dn[0] += 1
                ins.then_inc(dstep, 1)
                dve.wait_ge(dstep, dn[0])

            V = nc.vector

            def rsqrt_in(dst, src, n):
                return V.tensor_scalar(dst, src, 1.0 / n, EPS, ALU.mult, ALU.add)

            t, free = filled(dve, "vec")
            V.tensor_copy(vT[:, :], t[:, 0:42]).then_inc(vT_ready, 1)
            dve.wait_ge(vT_ready, 1)
            dve.sem_inc(free, 1)
            dve.wait_ge(ld_pos, 16)
            step(V.tensor_copy(posf[:, :], posi[:, :]))
            for j in range(HALF):
                freq = float(np.power(np.float32(THETA), np.float32(-j * 2.0 / ROT)))
                V.tensor_scalar(rope[:, 0, :, j], posf[:, :], freq, None, ALU.mult).then_inc(sin_in2, 1)
            dve.wait_ge(sin_in2, HALF)
            magic = 1.5 * 2 ** 23
            step(V.tensor_scalar(rope[:, 1, :, :], rope[:, 0, :, :], 1 / (2 * np.pi), magic, ALU.mult, ALU.add))
            step(V.tensor_scalar(rope[:, 1, :, :], rope[:, 1, :, :], magic, None, ALU.subtract))
            rest = 2 * np.pi
            for bits in (2 ** 8, 2 ** 18, None):
                part = round(rest * bits) / bits if bits else rest
                rest -= part
                step(V.scalar_tensor_tensor(rope[:, 0, :, :], rope[:, 1, :, :], -part, rope[:, 0, :, :], ALU.mult, ALU.add))
            V.tensor_scalar(rope[:, 0, :, :], rope[:, 0, :, :], 3.1415925, -3.1415925, ALU.min, ALU.max).then_inc(sin_in, 1)
            dve.wait_ge(ss_ready, TT)
            rsqrt_in(st[:, 4:8], st[:, 0:4], D).then_inc(rs_ready, 1)
            dve.wait_ge(ss_ready, TT + 1)
            step(V.reciprocal(st[:, 12:16], st[:, 8:12]))
            for tt in range(TT):
                V.tensor_scalar(x_in[:, tt, :], x_in[:, tt, :], st[:, 12 + tt:13 + tt], None, ALU.mult).then_inc(xn_ready, 1)
            dve.wait_ge(c_ready, 1)
            V.tensor_tensor(c32[:, :, :], vT[:, 34:42].unsqueeze(2).broadcast_to([P, KD, 32]), cs[:, :].unsqueeze(2).broadcast_to([P, KD, 32]), ALU.mult).then_inc(c32_ready, 1)
            dve.wait_ge(sin_out, 2)
            step(V.tensor_tensor(rope[:, 1, :, :], rope[:, 2, :, :], rope[:, 2, :, :], ALU.mult))
            step(V.tensor_scalar(rope[:, 2, :, :], rope[:, 1, :, :], -2.0, 1.0, ALU.mult, ALU.add))
            step(V.tensor_scalar(nsin[:, :, :], rope[:, 3, :, :], -1.0, None, ALU.mult))
            dve.sem_inc(rope_ready, 1)
            g, free = filled(dve, "rows", "G")
            V.tensor_copy(rowb[:, :], g[:, 0:228]).then_inc(rowb_ready, 1)
            dve.wait_ge(rowb_ready, 1)
            dve.sem_inc(free, 1)
            for k in range(1, KD, 2):
                t, free = filled(dve, ("x", k))
                step(V.tensor_copy(hT[:, k, :], t[:, :]))
                dve.sem_inc(free, 1)

            def mod_cols(grp):
                dve.wait_ge(ld_bada, 16)
                dve.wait_ge(m16_in, 16 * (grp + 1))
                V.tensor_tensor(m16[:, grp, :], m16[:, grp, :], bada[:, grp, :], ALU.add).then_inc(m16_ready, 1)

            def mod_take(grp):
                t, free = filled(dve, ("mod", grp))
                step(V.tensor_copy(modT[:, grp, :], t[:, 0:16]))
                dve.sem_inc(free, 1)

            mod_cols(0)
            mod_take(0)
            step(V.scalar_tensor_tensor(scale1[:, :], modT[:, 0, 8:16], 1.0, vT[:, 0:8], ALU.add, ALU.mult))
            for k in range(KD):
                if k % 2 == 0:
                    dve.wait_ge(hraw, k // 2 + 1)
                V.tensor_scalar(hT[:, k, :], hT[:, k, :], scale1[:, k:k + 1], modT[:, 0, k:k + 1], ALU.mult, ALU.add).then_inc(h_ready, 1)

            dve.wait_ge(ikw_in, TT)
            ik = ikw[:, :, RANK:RANK + 64]
            step(V.tensor_reduce(st[:, 44:48], ik, AX.X, ALU.add))
            step(V.tensor_scalar(st[:, 44:48], st[:, 44:48], 1.0 / 64, None, ALU.mult))
            mu = st[:, 44:48].unsqueeze(2).broadcast_to([P, TT, 64])
            step(V.tensor_tensor(ik, ik, mu, ALU.subtract))
            step(V.tensor_tensor(kin[:, :, 0, :], ik, ik, ALU.mult))
            step(V.tensor_reduce(st[:, 48:52], kin[:, :, 0, :], AX.X, ALU.add))
            V.tensor_scalar(wi[:, :, :], ikw[:, :, RANK + 64:NS], 8 ** -0.5, None, ALU.mult).then_inc(wi_ready, 1)
            rsqrt_in(st[:, 52:56], st[:, 48:52], 64).then_inc(lnv_ready, 1)
            dve.wait_ge(lnq_ready, 1)
            step(V.reciprocal(st[:, 60:64], st[:, 56:60]))
            step(V.tensor_tensor(ik, ik, st[:, 60:64].unsqueeze(2).broadcast_to([P, TT, 64]), ALU.mult))
            step(V.tensor_tensor(kin[:, :, 0, :], ik, g_ki_b.unsqueeze(1).broadcast_to([P, TT, 64]), ALU.mult))
            ki = kin[:, :, 0, :]
            step(V.tensor_tensor(kin[:, :, 1, 0:HALF], ki[:, :, HALF:ROT], nsin[:, :, :], ALU.mult))
            step(V.tensor_tensor(kin[:, :, 1, HALF:ROT], ki[:, :, 0:HALF], rope[:, 3, :, :], ALU.mult))
            step(V.tensor_tensor(ki[:, :, 0:HALF], ki[:, :, 0:HALF], rope[:, 2, :, :], ALU.mult))
            step(V.tensor_tensor(ki[:, :, HALF:ROT], ki[:, :, HALF:ROT], rope[:, 2, :, :], ALU.mult))
            step(V.tensor_tensor(ki[:, :, 0:ROT], ki[:, :, 0:ROT], kin[:, :, 1, 0:ROT], ALU.add))
            V.tensor_copy(kin[:, :, 1, :], ki).then_inc(ki_ready, 1)

            queue = []

            def topk_round(tq, w):
                work = mask[:, tq - 1, 0:w]
                step(V.max(m8[:, :], work))
                step(V.match_replace(work, m8[:, :], work, TAKEN))

            def topk_end(tq, w):
                work = mask[:, tq - 1, 0:w]
                step(V.tensor_scalar(work, work, TAKEN * 0.7, HIDE, ALU.is_gt, ALU.mult))

            def some(n):
                for _ in range(n):
                    if queue:
                        queue.pop(0)()

            dve.wait_ge(const_ready, 3)
            dve.wait_ge(pstep_const, 1)
            for n in range(3 * PAIRS):
                tq, hp = 1 + n // PAIRS, n % PAIRS
                w = (tq + 1) * P
                acc = mask[:, tq - 1, 0:w]
                for hh in range(2):
                    h = 2 * hp + hh
                    dve.wait_ge(relu_ready, 2 * n + hh + 1)
                    if h == 0:
                        ins = V.tensor_scalar(acc, relu[:, hh, 0:w], wi[:, tq, 0:1], None, ALU.mult)
                    else:
                        ins = V.scalar_tensor_tensor(acc, relu[:, hh, 0:w], wi[:, tq, h:h + 1], acc, ALU.mult, ALU.add)
                    ins.then_inc(relu_used, 1)
                    dve.wait_ge(relu_used, 2 * n + hh + 1)
                if hp == PAIRS - 1:
                    step(V.tensor_tensor(mask[:, tq - 1, tq * P:w], mask[:, tq - 1, tq * P:w], causal0[:, :], ALU.add))
                some(4)
                if hp == PAIRS - 1:
                    assert not queue
                    queue += [lambda tq=tq, w=w: topk_round(tq, w)] * (TOPK // 8 - 1)
                    queue.append(lambda tq=tq, w=w: (topk_round(tq, w), topk_end(tq, w)))
                if n in (2, 5):
                    r = n // 5
                    z, free = filled(dve, ("z", r), "G")
                    step(V.tensor_scalar(zz[:, 0, r, :], z[:, :], vT[:, 32 + r:33 + r], None, ALU.add))
                    dve.sem_inc(free, 1)
                if n == 5:
                    V.scalar_tensor_tensor(zz[:, 1, :, :], zz[:, 0, :, :], -1.0, zz[:, 0, :, :], ALU.mult, ALU.min).then_inc(z_in, 1)
                if n == 8:
                    dve.wait_ge(zexp_ready, 2)
                    for r in range(2):
                        step(V.scalar_tensor_tensor(zz[:, 3, r, :], zz[:, 0, r, :], 0.0, zz[:, 2, r, :], ALU.min, ALU.subtract))
                        for ch in range(TT):
                            cut = slice(ch * P, (ch + 1) * P)
                            V.tensor_tensor_scan(bT[:, r, cut], ones[:, :], zz[:, 3, r, cut], 0.0, ALU.mult, ALU.add).then_inc(b_ready, 1)

                if n in (5, 9):
                    mod_cols(1 + n // 9)
                if n in (6, 10):
                    mod_take(1 + n // 10)
            step(V.scalar_tensor_tensor(scale2[:, :], modT[:, 2, 0:8], 1.0, vT[:, 8:16], ALU.add, ALU.mult))
            step(V.tensor_tensor(gatev[:, 0, :], modT[:, 1, 0:8], vT[:, 16:24], ALU.mult))
            step(V.tensor_tensor(gatev[:, 1, :], modT[:, 2, 8:16], vT[:, 24:32], ALU.mult))
            dve.sem_inc(h2m_ready, 1)

            def gla_clamp(ch):
                dve.wait_ge(ex_sub, 4 * ch + 4)
                step(V.tensor_scalar(bend[:, :], bT[:, :, ch * P + P - 1], 1.0 / TAU, None, ALU.mult))
                V.tensor_scalar(expo[:, :, 0:640], expo[:, :, 0:640], CLAMP * TAU, None, ALU.min).then_inc(ex_in, 1)

            def gla_factors(ch):
                dve.wait_ge(gqk_ready, 4)
                dve.wait_ge(ex_exp, 4 * ch + 4)
                step(V.tensor_copy(dec[:, :], expo[:, :, 767]))
                for r in range(2):
                    q, k = gqk[:, r, ch * P:(ch + 1) * P], gqk[:, 2 + r, ch * P:(ch + 1) * P]
                    for lo, n, f in ((0, NB, k), (512, 2, q), (768, 1, k)):
                        e = expo[:, r, lo:lo + n * P].rearrange("p (i s) -> p i s", i=n)
                        V.tensor_tensor(e, e, f.unsqueeze(1).broadcast_to([P, n, P]), ALU.mult).then_inc(ex_ready, 1)

            def gla_mask(ch):
                for hh in range(2):
                    sc, free = filled(dve, ("sc", ch), "GO"[hh])
                    V.tensor_tensor(scT.rearrange("p (r a) n -> p r a n", a=2)[:, :, hh, :], sc[:, 0:256].rearrange("p (r n) -> p r n", r=2),
                                    upto[:, :].unsqueeze(1).broadcast_to([P, 2, P]), ALU.mult).then_inc(sc_ready, 1)
                    dve.wait_ge(sc_ready, 2 * ch + hh + 1)
                    dve.sem_inc(free, 1)

            def gla_state(ch):
                if ch == TT - 1:
                    return
                t, free = filled(dve, ("state", ch))
                for r in range(2):
                    if ch == 0:
                        V.tensor_copy(state[:, r, :], t[:, r * P:(r + 1) * P]).then_inc(state_ready, 1)
                    else:
                        V.scalar_tensor_tensor(state[:, r, :], state[:, r, :], dec[:, r:r + 1], t[:, r * P:(r + 1) * P], ALU.mult, ALU.add).then_inc(state_ready, 1)
                dve.wait_ge(state_ready, 2 * ch + 2)
                dve.sem_inc(free, 1)

            def gla_norm(ch):
                dve.wait_ge(oss_ready, 4 * ch + 4)
                rsqrt_in(st[:, 20:24], st[:, 16:20], GLA_DV).then_inc(oms_ready, 1)
                dve.wait_ge(osq_ready, ch + 1)
                step(V.reciprocal(st[:, 36:40], st[:, 24:28]))
                dve.wait_ge(gs_ready, ch + 1)
                if ch:
                    filled(dve, ("oa", ch - 1))
                for h in range(GLA_H):
                    name, r = "GO"[h % 2], h // 2
                    V.scalar_tensor_tensor(oan[:, h * P:(h + 1) * P], ps[name][:, r * P:(r + 1) * P], st[:, 36 + h:37 + h],
                                           gs[:, ch, h * P:(h + 1) * P], ALU.mult, ALU.mult).then_inc(oan_ready, 1)
                dve.wait_ge(oan_ready, 4 * ch + 4)
                for name in ("G", "O"):
                    dve.sem_inc(bank[name].free, 1)

            def gla_take(ch):
                t, free = filled(dve, ("oa", ch))
                V.tensor_copy(gqk[:, :, ch * P:(ch + 1) * P], t[:, :].rearrange("p (c n) -> p c n", c=4)).then_inc(oa_ready, 1)
                dve.wait_ge(oa_ready, ch + 1)
                dve.sem_inc(free, 1)

            for u in range(NU + 1):
                tq, hp = u // PAIRS, u % PAIRS
                w = (tq + 1) * P
                z = 4 * (u % 2)
                ch, odd = (u - GLA_AT) // 2, (u - GLA_AT) % 2
                if u < TT * PAIRS:
                    for hh in range(2):
                        s, free = filled(dve, ("att", u), f"S{hh}")
                        if u >= 2:
                            filled(dve, ("p", u - 2, hh))
                        hidden = causal0[:, :] if tq == 0 else mask[:, tq - 1, 0:w]
                        step(V.tensor_tensor_reduce(out=prob[:, u % 2, hh, 0:w], in0=s[:, 0:w], in1=hidden, scale=1.0, scalar=-3e38,
                                                    op0=ALU.add, op1=ALU.max, accum_out=sm[:, hh, z:z + 1]))
                        dve.sem_inc(free, 1)
                        V.tensor_scalar(sm[:, hh, z + 1:z + 2], sm[:, hh, z:z + 1], -HD ** -0.5, None, ALU.mult).then_inc(s_masked, 1)
                    if not odd and 0 <= ch < TT:
                        gla_clamp(ch)
                    some(4)
                    for hh in range(2):
                        dve.wait_ge(p_exp, 2 * u + hh + 1)
                        step(V.reciprocal(sm[:, hh, z + 3:z + 4], sm[:, hh, z + 2:z + 3]))
                        V.tensor_scalar(prob[:, u % 2, hh, 0:w], prob[:, u % 2, hh, 0:w], sm[:, hh, z + 3:z + 4], None, ALU.mult).then_inc(p_ready, 1)
                if not odd and 0 <= ch < TT:
                    gla_factors(ch)
                if odd and 0 <= ch < TT:
                    gla_state(ch)
                    gla_norm(ch)
                if not odd and 0 < ch <= TT:
                    gla_take(ch - 1)
                if u:
                    v = u - 1
                    m = (v // PAIRS + 1) * P
                    t, free = filled(dve, ("p", v, 1))
                    if v >= 2:
                        filled(dve, ("att", v - 2), "O")
                    V.tensor_copy(probT[:, v % 2, 1, 0:m], t[:, 0:m]).then_inc(pT_ready[1], 1)
                    dve.wait_ge(pT_ready[1], v + 1)
                    dve.sem_inc(free, 1)
                if not odd and 0 <= ch < TT:
                    gla_mask(ch)

            def split_h_lo():
                dve.wait_ge(hi_ready, 1)
                filled(dve, ("o", TT - 1), "O")
                src, lo, hi = splits["h"]
                V.tensor_tensor(lo, src, hi, ALU.subtract).then_inc(lo_ready, 1)

            def diagonal(which):
                V.tensor_tensor(diag[:, which, :].rearrange("p (k n) -> p k n", k=KD), ident[:, :].unsqueeze(1).broadcast_to([P, KD, P]),
                                gatev[:, which, :].unsqueeze(2).broadcast_to([P, KD, P]), ALU.mult).then_inc(gd_ready, 1)

            def gate_take(tag, dst):
                for n, name in enumerate(("G", "O")):
                    g, free = filled(dve, (tag, n), name)
                    step(V.tensor_copy(dst[:, n * 512:(n + 1) * 512], g[:, :]))
                    dve.sem_inc(free, 1)

            filled(dve, ("dq", TT - 1))
            diagonal(0)
            split_h_lo()
            gate_take("gm", gmb)

            def mixing(n, tt):
                for ab in range(2):
                    dve.wait_ge(sig_ready, n * 2 * TT + ab * TT + tt + 1)
                    a, free = filled(dve, ("y", n, tt, ab))
                    step(V.tensor_tensor(sig[:, ab, tt, :], a[:, :], sig[:, ab, tt, :], ALU.mult))
                    dve.sem_inc(free, 1)
                if n == 0 and tt == 0:
                    filled(dve, ("att", TT * PAIRS - 1), "O")
                V.tensor_tensor(mix[:, tt, n * 512:(n + 1) * 512], sig[:, 0, tt, :], sig[:, 1, tt, :], ALU.add).then_inc(mix_ready, 1)

            def split_lo(key):
                src, lo, hi = splits[key]
                dve.wait_ge(hi_ready, split_at[key] + 1)
                V.tensor_tensor(lo, src, hi, ALU.subtract).then_inc(lo_ready, 1)

            split_lo(("proj", 0))
            split_lo("g")
            split_lo("q")
            after = {(0, 0): ("in", O_BG + 512), (0, 3): ("in", O_BG + D + 512), (1, 1): ("out", 0), (1, 2): ("out", 1)}
            for n in range(2):
                for tt in range(TT):
                    mixing(n, tt)
                    if (n, tt) in after:
                        split_lo(after[n, tt])
                if n == 0:
                    split_lo(("proj", 1))
            dve.wait_ge(mix_ready, 2 * TT)

            def shifted(dst, src, k, done):
                return V.tensor_scalar(dst, src, scale2[:, k:k + 1], modT[:, 1, 8 + k:9 + k], ALU.mult, ALU.add).then_inc(done, 1)

            def residual(tt):
                dve.wait_ge(rss_ready, 2 * tt + 2)
                step(V.tensor_tensor(st[:, 28:29], st[:, 28:29], st[:, 29:30], ALU.add))
                rsqrt_in(st[:, 30:31], st[:, 28:29], D).then_inc(rms_ready, 1)
                dve.wait_ge(rsq_ready, tt + 1)
                step(V.reciprocal(st[:, 32:33], st[:, 31:32]))
                for n in range(2):
                    a, free = filled(dve, ("out", tt, n))
                    step(V.scalar_tensor_tensor(x1(tt)[:, n * 512:(n + 1) * 512], a[:, :], st[:, 32:33], gmb[:, n * 512:(n + 1) * 512], ALU.mult, ALU.mult))
                    dve.sem_inc(free, 1)
                dve.wait_ge(ld_xr[tt % 2], 16 * (tt // 2 + 1))
                V.tensor_tensor(x1(tt), x1(tt), xres[:, tt % 2, :], ALU.add).then_inc(x1_ready, 1)
                dve.wait_ge(xss_ready, tt + 1)
                rsqrt_in(st[:, 34:35], st[:, 33:34], D).then_inc(xms_ready, 1)
                dve.wait_ge(xsq_ready, tt + 1)
                step(V.reciprocal(st[:, 43:44], st[:, 35:36]))
                if tt >= 2:
                    dve.wait_ge(xn2_stored[tt % 2], 16)
                    filled(dve, ("x2", tt - 2, 1))
                V.tensor_scalar(xn2[:, tt % 2, :], x1(tt), st[:, 43:44], None, ALU.mult).then_inc(xn2_ready, 1)

            def mix_copy(tt):
                if tt >= 2:
                    filled(dve, ("out", tt - 2, 1))
                for half in range(2):
                    t, free = filled(dve, ("mix", tt, half))
                    dve.wait_ge(mixT_ready[0], 2 * tt + half + 1)
                    V.tensor_tensor(mixT(tt % 2, 1, 512 * half, 512), t[:, :], mixT(tt % 2, 0, 512 * half, 512), ALU.subtract).then_inc(mixT_ready[1], 1)
                    dve.wait_ge(mixT_ready[1], 2 * tt + half + 1)
                    dve.sem_inc(free, 1)

            mix_copy(0)
            for tt in range(TT + 1):
                if tt < TT - 1:
                    mix_copy(tt + 1)
                if tt:
                    t, free = filled(dve, ("x2", tt - 1, 0))
                    if tt >= 3:
                        filled(dve, ("lg", tt - 3), "G")
                    for q in range(4):
                        shifted(h2T[:, (tt - 1) % 2, q, :], t[:, q * P:(q + 1) * P], q, h2T_ready[0])
                    dve.wait_ge(h2T_ready[0], 4 * tt)
                    dve.sem_inc(free, 1)
                if tt < TT:
                    residual(tt)
                if tt:
                    g, free = filled(dve, ("lg", tt - 1), "G")
                    step(V.tensor_tensor(lg[:, tt - 1, :], g[:, 0:GROUPS + NE], b_rt_b, ALU.add))
                    dve.sem_inc(free, 1)

            step(V.tensor_copy(gp[:, :, 0:GROUPS], lg[:, :, 0:GROUPS]))
            step(V.tensor_copy(iotaf[:, :], iota[:, :]))
            for tt in range(TT):
                step(V.max(top[:, tt, :], gp[:, tt, :]))
                step(V.max_index(topi[:, tt, :], top[:, tt, :], gp[:, tt, :]))
            step(V.tensor_copy(rt[:, 0, :], topi[:, :, 0]))
            step(V.tensor_tensor(ohg[:, :, 0, :], iotaf[:, 0:GROUPS].unsqueeze(1).broadcast_to([P, TT, GROUPS]),
                                 rt[:, 0, :].unsqueeze(2).broadcast_to([P, TT, GROUPS]), ALU.is_equal))
            step(V.tensor_scalar(ohg[:, :, 1, :], ohg[:, :, 0, :], -HIDE, HIDE, ALU.mult, ALU.add))
            for a, op in ((0, ALU.mult), (1, ALU.add)):
                src = (lg[:, :, GROUPS:] if a == 0 else el[:, :, :]).rearrange("p t (g e) -> p t g e", g=GROUPS)
                for tt in range(TT):
                    step(V.tensor_tensor(el[:, tt, :].rearrange("p (g e) -> p g e", g=GROUPS), src[:, tt, :, :],
                                         ohg[:, tt, a, :].unsqueeze(2).broadcast_to([P, GROUPS, PER_GROUP]), op))
            for tt in range(TT):
                step(V.max(etop[:, tt, :], el[:, tt, :]))
                step(V.max_index(etopi[:, tt, :], etop[:, tt, :], el[:, tt, :]))
            for w, dst in enumerate((e1, e2)):
                step(V.tensor_copy(rt[:, 1 + w, :], etopi[:, :, w]))
                step(V.tensor_tensor(dst[:, :, :], iotaf[:, :].unsqueeze(1).broadcast_to([P, TT, NE]),
                                     rt[:, 1 + w, :].unsqueeze(2).broadcast_to([P, TT, NE]), ALU.is_equal))
            V.tensor_tensor(em[:, :, :], e1[:, :, :], e2[:, :, :], ALU.add).then_inc(em_ready, 1)
            step(V.tensor_tensor(gp[:, :, 0:GROUPS], gp[:, :, 0:GROUPS], top[:, :, 0:1].broadcast_to([P, TT, GROUPS]), ALU.subtract))
            step(V.tensor_tensor(rt[:, 3, :], etop[:, :, 1], etop[:, :, 0], ALU.subtract))
            dve.sem_inc(ge_in, 1)
            o, free = filled(dve, "count", "O")
            n_e, x_e, cum, base_d, base_e = (cnt[:, n, :] for n in range(5))
            step(V.tensor_copy(n_e, o[:, 0:NE]))
            dve.sem_inc(free, 1)
            step(V.tensor_scalar(x_e, n_e, float(SLOT), None, ALU.is_gt))
            for m in range(2, SEQ // SLOT):
                step(V.scalar_tensor_tensor(x_e, n_e, float(SLOT * m), x_e, ALU.is_gt, ALU.add))
            step(V.tensor_tensor_scan(cum, ones[:, 0:NE], x_e, 0.0, ALU.mult, ALU.add))
            step(V.tensor_tensor(base_d, cum, x_e, ALU.subtract))
            step(V.tensor_scalar(base_e, iotaf[:, :], float(SLOT), None, ALU.mult))
            step(V.tensor_scalar(base_d, base_d, float(SLOT), float(SLOT * (NE - 1)), ALU.mult, ALU.add))
            step(V.tensor_tensor(base_d, base_d, base_e, ALU.subtract))
            g, free = filled(dve, "rank", "G")
            step(V.tensor_copy(rpos[:, :, :], g[:, 0:TT * NE].rearrange("p (t e) -> p t e", t=TT)))
            dve.sem_inc(free, 1)
            step(V.tensor_scalar(rtmp3[:, :, :], rpos[:, :, :], float(SLOT), None, ALU.is_ge))
            step(V.tensor_tensor(rtmp3[:, :, :], rtmp3[:, :, :], base_d.unsqueeze(1).broadcast_to([P, TT, NE]), ALU.mult))
            step(V.tensor_tensor(rpos[:, :, :], rpos[:, :, :], rtmp3[:, :, :], ALU.add))
            step(V.tensor_tensor(rpos[:, :, :], rpos[:, :, :], base_e.unsqueeze(1).broadcast_to([P, TT, NE]), ALU.add))
            for w, oh in enumerate((e1, e2)):
                step(V.tensor_tensor(rtmp3[:, :, :], rpos[:, :, :], oh[:, :, :], ALU.mult))
                step(V.tensor_reduce(spos[:, :, w], rtmp3[:, :, :], AX.X, ALU.add))
            pos = spos[:, :, :].rearrange("p t w -> p (t w)")
            name = rowid[:, :, :].rearrange("p t w -> p (t w)")
            nn = 2 * TT
            step(V.tensor_tensor(hi_ge[:, :, :], pos.unsqueeze(2).broadcast_to([P, nn, NPALL + 1]), iota_hi[:, :].unsqueeze(1).broadcast_to([P, nn, NPALL + 1]), ALU.is_ge))
            step(V.tensor_reduce(hi_n, hi_ge[:, :, :], AX.X, ALU.add))
            step(V.tensor_tensor(hi_hot[:, :, :], hi_ge[:, :, 0:NPALL], hi_ge[:, :, 1:NPALL + 1], ALU.subtract))
            step(V.tensor_tensor(hi_hot[:, :, :], hi_hot[:, :, :], name.unsqueeze(2).broadcast_to([P, nn, NPALL]), ALU.mult))
            step(V.scalar_tensor_tensor(lo_n, hi_n, -float(P), pos, ALU.mult, ALU.add))
            step(V.tensor_scalar(lo_n, lo_n, float(P), None, ALU.add))
            step(V.tensor_tensor(lo_hot[:, :, :], lo_n.unsqueeze(2).broadcast_to([P, nn, P]), iota_lo[:, :].unsqueeze(1).broadcast_to([P, nn, P]), ALU.is_equal))
            dve.sem_inc(pos_ready, 1)
            g, free = filled(dve, "slots", "G")
            table, late = slot_f[:, 0, :], slot_f[:, 1, :]
            step(V.tensor_scalar(table, g[:, 0:NPALL], -1.0, None, ALU.add))
            dve.sem_inc(free, 1)
            step(V.tensor_scalar(late, table, 0.0, NONE + SEQ, ALU.is_lt, ALU.mult))
            step(V.tensor_tensor(table, table, late, ALU.add))
            step(V.tensor_copy(dst_i[:, :], table))
            step(V.tensor_scalar(late, table, float(SEQ), -float(SEQ), ALU.is_ge, ALU.mult))
            step(V.tensor_tensor(table, table, late, ALU.add))
            V.tensor_copy(src_i[:, :], table).then_inc(slot_ready, 1)
            step(V.tensor_tensor(ovc[:, :, :], iotaf[:, 0:NOV].unsqueeze(2).broadcast_to([P, NOV, NE]), cum.unsqueeze(1).broadcast_to([P, NOV, NE]), ALU.is_ge))
            step(V.tensor_reduce(ovf[:, 0:NOV], ovc[:, :, :], AX.X, ALU.add))
            step(V.tensor_scalar(ovf[:, 0:NOV], ovf[:, 0:NOV], float(NE - 1), None, ALU.min))
            step(V.tensor_scalar(cnt[:, 5, 0:NOV // 2], iotaf[:, 0:NOV // 2], 2.0, None, ALU.mult))
            step(V.tensor_tensor(cnt[:, 6, 0:NOV // 2], cnt[:, 5, 0:NOV // 2], cum[:, NE - 1:NE].broadcast_to([P, NOV // 2]), ALU.is_lt))
            step(V.tensor_reduce(ovf[:, NOV:NOV + 1], cnt[:, 6, 0:NOV // 2], AX.X, ALU.add))
            step(V.tensor_copy(ovi[:, 0:NOV + 1], ovf[:, 0:NOV + 1]))
            dve.sem_inc(route_ready, 1)
            dve.wait_ge(ge_out, 1)
            step(V.tensor_reduce(rt[:, 7, :], gp[:, :, 0:GROUPS], AX.X, ALU.add))
            step(V.tensor_scalar(rt[:, 8, :], rt[:, 4, :], 1.0, None, ALU.add))
            step(V.tensor_tensor(rt[:, 7, :], rt[:, 7, :], rt[:, 8, :], ALU.mult))
            step(V.reciprocal(rt[:, 9, :], rt[:, 7, :]))
            step(V.tensor_tensor(rt[:, 10, :], rt[:, 9, :], rt[:, 4, :], ALU.mult))
            filled(dve, "slots", "G")
            diagonal(1)
            gate_take("gf", gfb)

            def pair(j, b, back, stores):
                dve.wait_ge(bank["T0"].full, moe_base["T0"] + j + 1)
                dve.wait_ge(bank["G"].full, moe_base["G"] + back)
                for q in range(4):
                    shifted(h2g[:, b, q, :], ps["T0"][:, q * P:(q + 1) * P], q, h2g_ready[0])
                dve.wait_ge(h2g_ready[0], 4 * j + 4)
                dve.sem_inc(bank["T0"].free, 1)
                dve.wait_ge(silu_ready, j + 1)
                V.tensor_tensor(aact[:, b, :], gact[:, b, :], ps["G"][:, DE:2 * DE], ALU.mult).then_inc(act_ready, 1)
                dve.wait_ge(act_ready, j + 1)
                dve.sem_inc(bank["G"].free, 1)
                dve.wait_ge(bank["A0"].full, moe_base["A0"] + j + 1)
                if stores is not None:
                    dve.wait_ge(y_stored[b], 16 * stores)
                V.tensor_copy(yb[:, b, 0:512], ps["A0"][:, :]).then_inc(yb_ready, 1)
                dve.wait_ge(yb_ready, j + 1)
                dve.sem_inc(bank["A0"].free, 1)

            pair(0, 0, 0, None)
            pair(1, 1, 0, None)
            with dve.Fori(1, NPAIR // 2) as i:
                pair(2 * i, 0, 2 * i - 1, i)
                pair(2 * i + 1, 1, 2 * i, i)
            n_ov = dve.value_load(ovi[0:1, NOV:NOV + 1], min_val=0, max_val=NOV // 2)
            with dve.If(n_ov > 0):
                with dve.Fori(0, n_ov) as v:
                    pair(NPAIR + v, 0, NPAIR + v, NPAIR // 2 + v)
            for tt in range(TT):
                y = yc[:, tt, :, :]
                dve.wait_ge(fw_ready, tt + 1)
                V.scalar_tensor_tensor(y[:, 0, :], y[:, 1, :], rt[:, 10, tt:tt + 1], y[:, 0, :], ALU.mult, ALU.add).then_inc(fss_ready, 1)
                dve.wait_ge(fss_ready, tt + 1)
                step(V.tensor_tensor(y[:, 1, :], y[:, 0, :], gfb, ALU.mult))
                dve.wait_ge(fms_ready, tt + 1)
                rsqrt_in(st[:, 41:42], st[:, 40:41], D).then_inc(fsq_in, 1)
                dve.wait_ge(fsq_ready, tt + 1)
                step(V.reciprocal(st[:, 43:44], st[:, 42:43]))
                V.scalar_tensor_tensor(x1(tt), y[:, 1, :], st[:, 43:44], x1(tt), ALU.mult, ALU.add).then_inc(fin_ready, 1)
                dve.wait_ge(fin_ready, tt + 1)


_INS = ["x", "c", "positions", "w_ada", "b_ada", "g_pre_mix", "g_post_mix", "g_pre_ffn", "g_post_ffn", "w_in", "w_gla_a2", "b_gla_a",
        "g_gla_out", "g_idx_k", "w_proj_gla", "w_proj_dsa", "w_out", "w_router_g", "b_router_g", "w_router_e", "b_router_e",
        "w_e_gate", "w_e_up", "w_e_down"]
_OUTS = [((1, SEQ, D), "float32")]


def kernel(**inputs):
    import numpy as _np
    import concourse.bacc as _bacc
    from concourse import mybir as _mybir
    from concourse.bass_utils import run_bass_kernel_spmd as _run

    nc = _bacc.Bacc("TRN2", target_bir_lowering=False, num_devices=1)
    arrays, args = {}, []
    for name in _INS:
        a = _np.ascontiguousarray(inputs[name])
        arrays[f"in_{name}_dram"] = a
        args.append(nc.dram_tensor(f"in_{name}_dram", a.shape, _mybir.dt.from_np(a.dtype), kind="ExternalInput").ap())
    for i, (shape, dtype) in enumerate(_OUTS):
        dt = _mybir.dt.from_np(_np.dtype(dtype))
        args.append(nc.dram_tensor(f"out_{i}_dram", shape, dt, kind="ExternalOutput").ap())
    layer(nc, *args)
    r = _run(nc, [arrays], core_ids=[0])
    got = tuple(r.results[0][f"out_{i}_dram"] for i in range(len(_OUTS)))
    return got[0]
```

```python
from contextlib import ExitStack

import numpy as np

import concourse.bass as bass
from concourse import mybir

ALU = mybir.AluOpType
ACT = mybir.ActivationFunctionType
F32 = mybir.dt.float32
F32R = mybir.dt.float32r
BF16 = mybir.dt.bfloat16
I32 = mybir.dt.int32
U32 = mybir.dt.uint32
AX = mybir.AxisListType

P = 128
D = 1024
SEQ = 512
TT = SEQ // P
KD = D // P
EPS = 1e-6
GLA_H, GLA_DK, GLA_DV, RANK = 4, 64, 128, 16
TAU = 16.0
HEADS, HD = 8, 64
TOPK = min(256, SEQ // 4)
ROT = HD // 4
HALF = ROT // 2
THETA = 500000.0
GROUPS, PER_GROUP = 4, 8
NE = GROUPS * PER_GROUP
DE = D // 4
PAIRS = HEADS // 2
SIZES = (256, 256, 512, 512, RANK, 512, 512, 512, 512, 64, 8, 2 * D)
OFF = [0] + [int(v) for v in np.cumsum(SIZES)]
(O_GQ, O_GK, O_GV, O_GG, O_GA, O_DQ, O_DK, O_DV, O_IQ, O_IK, O_IW, O_BG) = OFF[:12]
NS = RANK + 64 + 8
BLK = 32
NB = P // BLK
CLAMP = 40.0
HIDE = -1e30
TAKEN = -3e38
SLOT = 64
NPAIR = NE // 2
NOV = 16
NPALL = NPAIR + NOV // 2
NONE = 2048.0
NU = TT * PAIRS
GLA_AT = 8
WELEM = 3 * D * DE // P


class Bank:

    def __init__(self, full, free):
        self.full, self.free, self.at = full, free, {}

    def turn(self, name):
        assert name not in self.at, name
        self.at[name] = len(self.at)
        return self.at[name]


def layer(nc, x, c, positions, w_ada, b_ada, g_pre_mix, g_post_mix, g_pre_ffn, g_post_ffn, w_in,
          w_gla_a2, b_gla_a, g_gla_out, g_idx_k, w_proj_gla, w_proj_dsa, w_out, w_router_g,
          b_router_g, w_router_e, b_router_e, w_e_gate, w_e_up, w_e_down, out):
    xn_dram = nc.dram_tensor("xn_dram", (SEQ, D), F32, kind="Internal").ap()
    y_dram = nc.dram_tensor("y_dram", (2 * SEQ, D), F32, kind="Internal").ap()

    x_v = x[0].rearrange("(t p) d -> p t d", p=P)
    out_v = out[0].rearrange("(t p) d -> p t d", p=P)
    win_v = w_in[0].rearrange("(k p) n -> p k n", p=P)
    ada_v = w_ada[0].rearrange("(k p) n -> p k n", p=P)
    pg_v = w_proj_gla[0].rearrange("(k p) n -> p k n", p=P)
    pd_v = w_proj_dsa[0].rearrange("(k p) n -> p k n", p=P)
    wo_v = w_out[0].rearrange("(k p) n -> p k n", p=P)
    weg_v = w_e_gate[0].rearrange("e (k p) f -> e p k f", p=P)
    weu_v = w_e_up[0].rearrange("e (k p) f -> e p k f", p=P)
    wed_v = w_e_down[0].rearrange("e (k p) n -> e p k n", p=P)

    with ExitStack() as ctx:
        place = {}

        def sb(name, shape, dt=F32):
            place[name] = (nc.sbuf_base + 31) // 32 * 32
            return ctx.enter_context(nc.sbuf_tensor(name, shape, dt))

        def rounded(name, n):
            return nc.alloc_sbuf_tensor_at(name + "_r", [P, n], F32R, offset=place[name])

        def sem(name):
            return ctx.enter_context(nc.semaphore(name))

        arena = sb("arena", [P, 4 * WELEM])
        ring = arena[:, 0:4 * 4096].rearrange("p (s n) -> p s n", s=4)
        hT = arena[:, 16384:20480].rearrange("p (k n) -> p k n", k=KD)
        prob = arena[:, 20480:22528].rearrange("p (b h n) -> p b h n", b=2, h=2)
        probT = arena[:, 22528:24576].rearrange("p (b h n) -> p b h n", b=2, h=2)
        adab = arena[:, 20480:24576].rearrange("p (b n) -> p b n", b=2)
        yc = arena[:, 0:8192].rearrange("p (t w n) -> p t w n", t=TT, w=2)
        wexp = arena[:, :].rearrange("p (s n) -> p s n", s=4)

        qs_mem = sb("qs_mem", [P, 4096])
        qi_mem, stage_mem = qs_mem[:, 0:2048], qs_mem[:, 2048:4096]
        qiT = qi_mem.rearrange("p (c n) -> p c n", c=4)
        expo = qi_mem[:, 0:1792].rearrange("p (r n) -> p r n", r=2)
        qT = sb("qT", [P, PAIRS, SEQ])
        kv = sb("kv", [P, 4096])
        kT = kv[:, 0:2048].rearrange("p (c n) -> p c n", c=PAIRS)
        val = kv[:, 2048:4096].rearrange("p (t n) -> p t n", t=TT)
        mix = kv[:, :].rearrange("p (t n) -> p t n", t=TT)
        xg = kv[:, 0:2048].rearrange("p (b n) -> p b n", b=2)
        h2g = kv[:, 2048:4096].rearrange("p (b k n) -> p b k n", b=2, k=KD)
        gqk = sb("gqk", [P, 4, SEQ])
        relu = gqk[:, 0:2, :]
        gvs = sb("gvs", [P, 4096])
        gv = gvs[:, 0:2048].rearrange("p (t n) -> p t n", t=TT)
        gs = gvs[:, 2048:4096].rearrange("p (t n) -> p t n", t=TT)
        mk_mem = sb("mk_mem", [P, TT * SEQ])
        mask = mk_mem[:, 0:(TT - 1) * SEQ].rearrange("p (t n) -> p t n", n=SEQ)
        kiT = mk_mem[:, (TT - 1) * SEQ:]
        sig_mem = sb("sig_mem", [P, 4096])
        x_in = sig_mem[:, :].rearrange("p (t n) -> p t n", t=TT)
        zz = sig_mem[:, :].rearrange("p (w r n) -> p w r n", w=4, r=2)
        sig = sig_mem[:, :].rearrange("p (a t n) -> p a t n", a=2, t=TT)
        xn2 = sig_mem[:, 0:2048].rearrange("p (b n) -> p b n", b=2)
        h2T = sig_mem[:, 2048:4096].rearrange("p (b k n) -> p b k n", b=2, k=KD)
        yb = sig_mem[:, 0:2048].rearrange("p (b n) -> p b n", b=2)
        gact = sig_mem[:, 2048:2560].rearrange("p (b n) -> p b n", b=2)
        aact = sig_mem[:, 2560:3072].rearrange("p (b n) -> p b n", b=2)
        actT = sig_mem[:, 3072:3584].rearrange("p (b k n) -> p b k n", b=2, k=2)
        stage = stage_mem.rearrange("p (s n) -> p s n", s=4)
        xres = stage_mem.rearrange("p (b n) -> p b n", b=2)
        diag = stage_mem[:, 0:D]
        gla_mem = sb("gla_mem", [P, 3072])
        bT = gla_mem[:, 0:1024].rearrange("p (r n) -> p r n", r=2)
        scT = gla_mem[:, 1024:1536].rearrange("p (h n) -> p h n", h=4)
        kN = gla_mem[:, 1536:1792]
        state = gla_mem[:, 1792:2048].rearrange("p (r n) -> p r n", r=2)
        oan = gla_mem[:, 2048:2560]
        gmb = gla_mem[:, 1024:2048]
        gfb = gmb
        w_small = gvs[:, 0:KD * NS].rearrange("p (k n) -> p k n", k=KD)
        ikw = gvs[:, KD * NS:(KD + TT) * NS].rearrange("p (t n) -> p t n", t=TT)
        kin = sig_mem[:, 3072:3584].rearrange("p (t a n) -> p t a n", t=TT, a=2)
        w_rt = sb("w_rt", [P, KD, GROUPS + NE])
        ident = sb("ident", [P, P])
        ones = sb("ones", [P, P])
        ones_b = sb("ones_b", [P, P], BF16)
        before = sb("before", [P, P], BF16)
        upto = sb("upto", [P, P])
        causal0 = sb("causal0", [P, P])
        vrows = gla_mem[0:90, 1536:1664]
        vT = sb("vT", [P, 90])
        rows = gla_mem[0:1, 1664:1892]
        rowb = sb("rowb", [P, 228])
        g_out_b, g_ki_b, b_rt_b = rowb[:, 0:128], rowb[:, 128:192], rowb[:, 192:228]
        mrow = gla_mem[:, 1024:1536]
        modT = sb("modT", [P, 3, 16])
        cs = sb("cs", [P, KD])
        c32 = sb("c32", [P, KD, 32])
        scale1 = sb("scale1", [P, KD])
        scale2 = sb("scale2", [P, KD])
        gatev = sb("gatev", [P, 2, KD])
        posi = sb("posi", [P, TT], I32)
        posf = sb("posf", [P, TT])
        rope = sb("rope", [P, 4, TT, HALF])
        nsin = sb("nsin", [P, TT, HALF])
        rtmp_mem = sb("rtmp_mem", [P, HEADS * ROT])
        rtmp = rtmp_mem[:, :].rearrange("p (h r) -> p h r", h=HEADS)
        st = sb("st", [P, 64])
        wi = sb("wi", [P, TT, 8])
        m8 = sb("m8", [P, 8])
        sm = sb("sm", [P, 2, 8])
        dec = sb("dec", [P, 2])
        bend = sb("bend", [P, 2])
        a2 = gvs[0:RANK, (KD + TT) * NS:(KD + TT) * NS + 256]
        gaT = sig_mem[0:RANK, 3584:4096]
        mask_f = mask[:, :, :].rearrange("p a n -> p (a n)")
        lg = sb("lg", [P, NE])
        gp = sb("gp", [P, TT, 8])
        top = sb("top", [P, TT, 8])
        topi = sb("topi", [P, TT, 8], U32)
        etop = sb("etop", [P, TT, 8])
        etopi = sb("etopi", [P, TT, 8], U32)
        rt = rtmp_mem[:, 0:64].rearrange("p (a t) -> p a t", t=TT)
        el = sb("el", [P, NE])
        pen = sb("pen", [P, NE])
        e12 = sb("e12", [P, 2, TT, NE])
        em = sb("em", [P, TT, NE], BF16)
        rpos = mask_f[:, 512:640].rearrange("p (t e) -> p t e", t=TT)
        rtmp4 = mask_f[:, 0:256].rearrange("p (w t e) -> p w t e", w=2, t=TT)
        x_m = mask_f[:, 256:512].rearrange("p (e m) -> p e m", m=SEQ // SLOT)
        cnt = mask_f[:, 768:1024].rearrange("p (a e) -> p a e", a=8)
        ovc = mask_f[:, 1024:1536].rearrange("p (a e) -> p a e", a=NOV)
        ovi = sb("ovi", [P, NOV + 2], I32)
        ovf = sb("ovf", [P, NOV + 2])
        iotaf = sb("iotaf", [P, NE])
        giota = sb("giota", [P, NE])
        base_m = sb("base_m", [P, NE])
        thr = sb("thr", [P, SEQ // SLOT])
        arena_r, gvs_r, gqk_r, qT_r, qs_r, mk_r, gla_r = (rounded(name, n) for name, n in (
            ("arena", 4 * WELEM), ("gvs", 4096), ("gqk", 2048), ("qT", 2048), ("qs_mem", 4096), ("mk_mem", TT * SEQ), ("gla_mem", 1024)))
        qi_r, stage_r = qs_r[:, 0:2048], qs_r[:, 2048:4096]
        spots = {0: 0, 1: 4096, 2: 8192, 3: 12288, "H": 16384, "B": 20480}
        area = {key: arena[:, n:n + 4096] for key, n in spots.items()}
        area_r = {key: arena_r[:, n:n + 4096] for key, n in spots.items()}
        area_r["G"] = gvs_r[:, :]
        g_all, q_all = (v[:, :, :].rearrange("p a n -> p (a n)") for v in (gqk, qT))
        splits = {key: (area[raw], area_r[lo], area_r[hi]) for key, raw, lo, hi in (
            ("h", "H", "G", "B"), (("proj", 0), 1, 1, 3), (("in", O_BG + 512), 2, 2, "H"), (("in", O_BG + D + 512), 0, 0, 3),
            (("proj", 1), 1, 1, 2), (("out", 0), "H", "H", "B"), (("out", 1), 3, 3, "G"))}
        splits["g"], splits["q"] = (g_all, gqk_r[:, :], qi_r), (q_all, qT_r[:, :], stage_r)
        split_at = {key: n for n, key in enumerate(["h", ("proj", 0), "g", "q", ("in", O_BG + 512), ("in", O_BG + D + 512),
                                                    ("proj", 1), ("out", 0), ("out", 1)])}

        def parts(key, k):
            return [v.rearrange("p (k n) -> p k n", k=k) for v in (splits[key][2], splits[key][1])]

        def mixT(b, part, n, size):
            if b:
                return qi_r[:, 1024 * part + n:1024 * part + n + size]
            return mk_r[:, 1024 * part + n:1024 * part + n + size]

        def x1(tt):
            return (g_all if tt < 2 else q_all)[:, D * (tt % 2):D * (tt % 2 + 1)]

        gu_sets = [[wexp[:, 2 * z + q, 0:4096] for q in range(2)] for z in range(2)] + [[gvs[:, :], qs_mem[:, :]]]
        down_sets = [[[wexp[:, 2 * z + q, 4096 + D * k:4096 + D * (k + 1)] for k in range(2)] for q in range(2)] for z in range(2)]
        down_sets.append([[mk_mem[:, 0:D], mk_mem[:, D:2 * D]], [gla_mem[:, 0:D], gla_mem[:, 2048:3072]]])

        lo_hot = gla_r[:, 0:1024].rearrange("p (c n) -> p c n", c=2 * TT)
        hi_ge = qi_mem[:, 0:2 * TT * (NPALL + 1)].rearrange("p (c n) -> p c n", c=2 * TT)
        hi_d = qi_mem[:, 256:256 + 2 * TT * NPALL].rearrange("p (c n) -> p c n", c=2 * TT)
        hi_hot = stage_r[:, 0:4 * TT * NPALL].rearrange("p (c w n) -> p c w n", c=2 * TT, w=2)
        tables = sb("tables", [P, 2, NPALL], U32)
        src_i, dst_i = tables[:, 0, :], tables[:, 1, :]
        idx_c = sb("idx_c", [P, 2, 2], U32)
        spos = sb("spos", [P, 2, TT])
        iota_hi = sb("iota_hi", [P, NPALL + 1])
        iota_lo = sb("iota_lo", [P, P])
        hi_n, lo_n = cnt[:, 5, 0:2 * TT], cnt[:, 6, 0:2 * TT]
        rowid = sb("rowid", [P, 2, TT, 2])
        diag_e = qi_mem[:, D:2 * D]

        names = ["A0", "A1", "S0", "S1", "T0", "T1", "O", "G"]
        ps, bank = {}, {}
        for n in names:
            ps[n] = ctx.enter_context(nc.psum_tensor("ps" + n, [P, 512], F32))
            bank[n] = Bank(sem(n + "_full"), sem(n + "_free"))

        ld_x = [sem(f"ld_x{t}") for t in range(TT)]
        ld_vec, ld_rows, ld_pos = (sem(n) for n in ("ld_vec", "ld_rows", "ld_pos"))
        ld_small, ld_a2, ld_rt = sem("ld_small"), sem("ld_a2"), sem("ld_rt")
        ring_in = [sem(f"ring_in{i}") for i in range(4)]
        ring_out = sem("ring_out")
        const_ready = sem("const_ready")
        vT_ready, rowb_ready, c_ready = sem("vT_ready"), sem("rowb_ready"), sem("c_ready")
        ss_ready, rs_ready, xn_ready = sem("ss_ready"), sem("rs_ready"), sem("xn_ready")
        hraw, h_ready = sem("hraw"), sem("h_ready")
        mrow_ready = sem("mrow_ready")
        sin_in, sin_out, rope_ready = sem("sin_in"), sem("sin_out"), sem("rope_ready")
        stage_in, stage_roped = sem("stage_in"), sem("stage_roped")
        ikw_in, ki_ready, wi_ready = sem("ikw_in"), sem("ki_ready"), sem("wi_ready")
        qiT_ready, kiT_ready, qT_ready, kT_ready, val_ready = (sem(n) for n in ("qiT_ready", "kiT_ready", "qT_ready", "kT_ready", "val_ready"))
        gaT_ready, z_in, zexp_ready, b_ready = (sem(n) for n in ("gaT_ready", "z_in", "zexp_ready", "b_ready"))
        relu_ready, relu_used, mask_ready, causal_ready = (sem(n) for n in ("relu_ready", "relu_used", "mask_ready", "causal_ready"))
        s_masked, p_exp, p_ready, p_used = (sem(n) for n in ("s_masked", "p_exp", "p_ready", "p_used"))
        pT_ready, ob_ready = [sem("pT_ready0"), sem("pT_ready1")], sem("ob_ready")
        gqk_ready, gv_ready, gs_in, gs_ready = (sem(n) for n in ("gqk_ready", "gv_ready", "gs_in", "gs_ready"))
        ex_in, ex_exp, ex_ready = (sem(n) for n in ("ex_in", "ex_exp", "ex_ready"))
        kN_ready, sc_ready, state_ready, oss_ready, oms_ready, osq_ready, oan_ready, oa_ready = (
            sem(n) for n in ("kN_ready", "sc_ready", "state_ready", "oss_ready", "oms_ready", "osq_ready", "oan_ready", "oa_ready"))
        sig_ready, mix_ready = sem("sig_ready"), sem("mix_ready")
        mixT_ready = [sem("mixT_act"), sem("mixT_dve")]
        h2T_ready = [sem("h2T_dve"), sem("h2T_act")]
        h2g_ready = [sem("h2g_dve"), sem("h2g_act")]
        gd_ready = sem("gd_ready")
        ld_xr = [sem("ld_xr0"), sem("ld_xr1")]
        rss_ready, rms_ready, rsq_ready, x1_ready, xss_ready, xms_ready, xsq_ready, xn2_ready = (
            sem(n) for n in ("rss_ready", "rms_ready", "rsq_ready", "x1_ready", "xss_ready", "xms_ready", "xsq_ready", "xn2_ready"))
        xn2_stored = [sem("xn2_stored0"), sem("xn2_stored1")]
        lg_ready, ge_in, ge_out, em_ready, pos_ready, route_ready = (
            sem(n) for n in ("lg_ready", "ge_in", "ge_out", "em_ready", "pos_ready", "route_ready"))
        slot_ready, ada_out, ge_diag = sem("slot_ready"), sem("ada_out"), sem("ge_diag")
        ada_in = [sem("ada_in0"), sem("ada_in1")]
        we_in, we_used = [sem(f"we_in{z}") for z in range(3)], sem("we_used")
        xg_in, idx_set, silu_ready, act_ready, actT_ready, yb_ready = (
            sem(n) for n in ("xg_in", "idx_set", "silu_ready", "act_ready", "actT_ready", "yb_ready"))
        y_stored, yb_act = [sem("y_stored0"), sem("y_stored1")], sem("yb_act")
        yc_in = [sem(f"yc_in{t}") for t in range(TT)]
        fw_ready, fss_ready, fms_ready, fsq_ready, fin_ready, out_done = (
            sem(n) for n in ("fw_ready", "fss_ready", "fms_ready", "fsq_ready", "fin_ready", "out_done"))
        dstep, pstep, h2m_ready, xg_clear = (sem(n) for n in ("dstep", "pstep", "h2m_ready", "xg_clear"))
        sin_in2, c32_ready, lnv_ready, lnq_ready, pstep_const = (sem(n) for n in ("sin_in2", "c32_ready", "lnv_ready", "lnq_ready", "pstep_const"))
        fsq_in, idx_seen, ex_sub = sem("fsq_in"), sem("idx_seen"), sem("ex_sub")
        hi_ready, lo_ready = sem("hi_ready"), sem("lo_ready")
        fsq_early, fg_ready = sem("fsq_early"), sem("fg_ready")
        where, moe_base = {}, {}

        block = ctx.enter_context(nc.Block())

        items = [("ada", 0, q) for q in range(4)]
        items += [("in", O_IQ), ("in", O_DK), ("in", O_DQ), ("in", O_DV), ("in", O_GQ), ("in", O_GV), ("in", O_GG)]
        items += [("in", O_BG), ("in", O_BG + D), ("proj", 0), ("in", O_BG + 512), ("in", O_BG + D + 512), ("proj", 1)]
        items += [("out", 0), ("out", 1)]
        item_at = {it: n for n, it in enumerate(items)}

        def slot_of(it):
            if it in splits:
                return splits[it][0]
            return ring[:, item_at[it] % 4, :]

        def ring_wait(eng, it):
            n = item_at[it]
            extra = sum(1 for m, o in enumerate(items[:n + 1]) if m % 4 == n % 4 and o[0] == "proj")
            eng.wait_ge(ring_in[n % 4], 16 * (n // 4 + 1 + extra))

        def filled(eng, turn, name=None):
            name = name or where[turn]
            eng.wait_ge(bank[name].full, bank[name].at[turn] + 1)
            return ps[name], bank[name].free

        @block.tensor
        def _(pe):
            def take(name, turn):
                n = bank[name].turn(turn)
                if n:
                    pe.wait_ge(bank[name].free, n)
                return ps[name]

            flip = {"T": 0, "A": 0}

            def take_next(kind, turn):
                name = f"{kind}{flip[kind] % 2}"
                flip[kind] += 1
                where[turn] = name
                return take(name, turn), bank[name].full

            pe.wait_ge(const_ready, 1)
            pe.wait_ge(ld_vec, 16 * 7)
            t, full = take_next("T", "vec")
            nc.tensor.transpose(t[:, 0:90], vrows[:, :], ident[0:90, 0:90]).then_inc(full, 1)
            pe.wait_ge(const_ready, 2)
            pe.wait_ge(ld_rows, 16 * 4)
            g = take("G", "rows")
            nc.tensor.matmul(g[:, 0:228], ones[0:1, :], rows[:, :], start=True, stop=True).then_inc(bank["G"].full, 1)
            for k in range(KD):
                t, full = take_next("T", ("x", k))
                for tt in range(TT):
                    if k == 0:
                        pe.wait_ge(xn_ready, tt + 1)
                    last = nc.tensor.transpose(t[:, tt * P:(tt + 1) * P], x_in[:, tt, k * P:(k + 1) * P], ident[:, :])
                last.then_inc(full, 1)

            def ada(grp):
                if grp == 0:
                    pe.wait_ge(c32_ready, 1)
                a, full = take_next("A", ("ada", grp))
                for k in range(KD):
                    it = ("ada", grp, k // 2)
                    if k % 2 == 0:
                        ring_wait(pe, it)
                    w = slot_of(it).rearrange("p (k n) -> p k n", k=2)
                    for j in range(4):
                        last = nc.tensor.matmul(a[32 * j:32 * j + 32, :], c32[:, k, :], w[:, k % 2, j * 512:(j + 1) * 512],
                                                start=(k == 0), stop=(k == KD - 1))
                    if k % 2 == 1:
                        last.then_inc(ring_out, 1)
                pe.wait_ge(ring_out, item_at[("ada", grp, 3)] + 1)
                pe.sem_inc(full, 1)

            def ada_step(m):
                grp, k = 1 + m // KD, m % KD
                pe.wait_ge(ada_in[m % 2], 16 * (m // 2 + 1))
                if k == 0:
                    take("O", ("ada", grp))
                    where[("ada", grp)] = "O"
                o = ps["O"]
                for j in range(4):
                    last = nc.tensor.matmul(o[32 * j:32 * j + 32, :], c32[:, k, :], adab[:, m % 2, j * 512:(j + 1) * 512],
                                            start=(k == 0), stop=(k == KD - 1))
                last.then_inc(ada_out, 1)
                if k == KD - 1:
                    pe.wait_ge(ada_out, m + 1)
                    pe.sem_inc(bank["O"].full, 1)

            def ada_turn(grp):
                pe.wait_ge(mrow_ready, grp + 1)
                t, full = take_next("T", ("mod", grp))
                for q in range(4):
                    last = nc.tensor.transpose(t[:, q * P:(q + 1) * P], mrow[:, q * P:(q + 1) * P], ident[:, :])
                last.then_inc(full, 1)

            ada(0)
            ada_turn(0)

            def inproj(it, tt):
                if it in splits:
                    return inproj_split(it, tt)
                ring_wait(pe, it)
                a, full = take_next("A", (it, tt))
                w = slot_of(it).rearrange("p (k n) -> p k n", k=KD)
                for k in range(KD):
                    if tt == 0 and it == ("in", O_IQ):
                        pe.wait_ge(h_ready, k + 1)
                    last = nc.tensor.matmul(a[:, :], hT[:, k, tt * P:(tt + 1) * P], w[:, k, :], start=(k == 0), stop=(k == KD - 1))
                last.then_inc(full, 1)
                if tt == TT - 1:
                    pe.wait_ge(full, bank[where[(it, tt)]].at[(it, tt)] + 1)
                    pe.sem_inc(ring_out, 1)

            def split_matmul(acc, lhs, rhs, start, stop):
                nc.tensor.matmul(acc, lhs[0], rhs[0], start=start, stop=False)
                nc.tensor.matmul(acc, lhs[0], rhs[1], start=False, stop=False)
                return nc.tensor.matmul(acc, lhs[1], rhs[0], start=False, stop=stop)

            def split_wait(key):
                pe.wait_ge(hi_ready, split_at[key] + 1)
                pe.wait_ge(lo_ready, split_at[key] + 1)

            def inproj_split(it, tt):
                split_wait("h")
                split_wait(it)
                h, w = parts("h", KD), parts(it, KD)
                a, full = take_next("A", (it, tt))
                for k in range(KD):
                    last = split_matmul(a[:, :], [v[:, k, tt * P:(tt + 1) * P] for v in h], [v[:, k, :] for v in w], k == 0, k == KD - 1)
                last.then_inc(full, 1)
                if tt == TT - 1:
                    pe.wait_ge(full, bank[where[(it, tt)]].at[(it, tt)] + 1)
                    pe.sem_inc(ring_out, 1)

            def inproj_T(it, cb):
                ring_wait(pe, it)
                a, full = take_next("A", (it, cb))
                w = slot_of(it).rearrange("p (k n) -> p k n", k=KD)
                for k in range(KD):
                    last = nc.tensor.matmul(a[:, :], w[:, k, cb * P:(cb + 1) * P], hT[:, k, :], start=(k == 0), stop=(k == KD - 1))
                last.then_inc(full, 1)
                if cb == 3:
                    pe.wait_ge(full, bank[where[(it, cb)]].at[(it, cb)] + 1)
                    pe.sem_inc(ring_out, 1)

            nstage = [0]

            def turn_stage(what, tt):
                pe.wait_ge(stage_roped, nstage[0] + 1)
                t, full = take_next("T", (what, tt))
                for cb in range(4):
                    last = nc.tensor.transpose(t[:, cb * P:(cb + 1) * P], stage[:, nstage[0] % 4, cb * P:(cb + 1) * P], ident[:, :])
                last.then_inc(full, 1)
                nstage[0] += 1

            for tt in range(TT):
                inproj(("in", O_IQ), tt)
            pe.wait_ge(ld_small, 32)
            for tt in range(TT):
                a, full = take_next("A", ("small", tt))
                for k in range(KD):
                    last = nc.tensor.matmul(a[:, 0:NS], hT[:, k, tt * P:(tt + 1) * P], w_small[:, k, :], start=(k == 0), stop=(k == KD - 1))
                last.then_inc(full, 1)
            for tt in range(TT):
                inproj(("in", O_DK), tt)
                turn_stage("iq", tt)
            pe.wait_ge(ki_ready, 1)
            t, full = take_next("T", "ki")
            for tt in range(TT):
                last = nc.tensor.transpose(t[:, tt * P:(tt + 1) * P], kin[:, tt, :, :].rearrange("p a n -> p (a n)"), ident[:, :])
            last.then_inc(full, 1)
            t, full = take_next("T", "ga")
            for tt in range(TT):
                last = nc.tensor.transpose(t[0:RANK, tt * P:(tt + 1) * P], ikw[:, tt, 0:RANK], ident[:, :])
            last.then_inc(full, 1)

            def index_scores(tq, hp):
                n = (tq + 1) * P
                if (tq, hp) == (1, 0):
                    pe.wait_ge(kiT_ready, 1)
                    pe.wait_ge(qiT_ready, TT)
                for hh in range(2):
                    s = take(f"S{hh}", ("idx", tq, hp))
                    nc.tensor.matmul(s[:, 0:n], qiT[64 * hh:64 * hh + 64, hp, tq * P:(tq + 1) * P], kiT[64 * hh:64 * hh + 64, 0:n],
                                     start=True, stop=True).then_inc(bank[f"S{hh}"].full, 1)

            fill = [lambda tt=tt: (inproj(("in", O_DQ), tt), turn_stage("dk", tt)) for tt in range(TT)]
            fill += [lambda tt=tt: (inproj(("in", O_DV), tt), turn_stage("dq", tt)) for tt in range(TT)]
            for n in range(3 * PAIRS):
                index_scores(1 + n // PAIRS, n % PAIRS)
                if n in (1, 3):
                    r = n // 2
                    pe.wait_ge(gaT_ready, 1)
                    pe.wait_ge(ld_a2, 16)
                    z = take("G", ("z", r))
                    nc.tensor.matmul(z[:, :], a2[:, r * P:(r + 1) * P], gaT[:, :], start=True, stop=True).then_inc(bank["G"].full, 1)
                if n < KD:
                    ada_step(2 * n)
                    ada_step(2 * n + 1)
                if n in (6, 10):
                    ada_turn(1 + n // 10)
                if n % 3 != 1:
                    fill.pop(0)()

            def attn_scores(u):
                tq, hp = u // PAIRS, u % PAIRS
                n = (tq + 1) * P
                if u == 0:
                    pe.wait_ge(kT_ready, TT)
                    pe.wait_ge(qT_ready, TT)
                for hh in range(2):
                    s = take(f"S{hh}", ("att", u))
                    nc.tensor.matmul(s[:, 0:n], qT[64 * hh:64 * hh + 64, hp, tq * P:(tq + 1) * P], kT[64 * hh:64 * hh + 64, hp, 0:n],
                                     start=True, stop=True).then_inc(bank[f"S{hh}"].full, 1)

            def attn_out(u):
                tq, hp = u // PAIRS, u % PAIRS
                for hh in range(2):
                    pe.wait_ge(p_ready, 2 * u + hh + 1)
                    t, full = take_next("T", ("p", u, hh))
                    for kb in range(tq + 1):
                        last = nc.tensor.transpose(t[:, kb * P:(kb + 1) * P], prob[:, u % 2, hh, kb * P:(kb + 1) * P], ident[:, :])
                    last.then_inc(full, 1)
                if u == 0:
                    pe.wait_ge(val_ready, TT)
                o = take("O", ("att", u))
                for kb in range(tq + 1):
                    for hh in range(2):
                        if kb == 0:
                            pe.wait_ge(pT_ready[hh], u + 1)
                        last = nc.tensor.matmul(o[64 * hh:64 * hh + 64, 0:P], val[:, kb, (2 * hp + hh) * HD:(2 * hp + hh + 1) * HD],
                                                probT[:, u % 2, hh, kb * P:(kb + 1) * P], start=(kb == 0), stop=(kb == tq))
                last.then_inc(bank["O"].full, 1)

            def gla_scores(ch):
                pe.wait_ge(ex_ready, 6 * ch + 6)
                t, full = take_next("T", ("kN", ch))
                for r in range(2):
                    last = nc.tensor.transpose(t[:, r * P:(r + 1) * P], expo[:, r, 768:896], ident[:, :])
                last.then_inc(full, 1)
                sc = [take(n, ("sc", ch)) for n in ("G", "O")]
                for r in range(2):
                    for i in range(NB):
                        for hh in range(2):
                            lo = 64 * hh
                            last = nc.tensor.matmul(sc[hh][:, r * P + i * BLK:r * P + (i + 1) * BLK], expo[lo:lo + 64, r, i * P:(i + 1) * P],
                                                    expo[lo:lo + 64, r, 512 + i * BLK:512 + (i + 1) * BLK], start=True, stop=True)
                            if r == 1 and i == NB - 1:
                                last.then_inc(bank["GO"[hh]].full, 1)

            def gla_out(ch):
                pe.wait_ge(sc_ready, 2 * ch + 2)
                pe.wait_ge(gv_ready, TT)
                o = [take(n, ("o", ch)) for n in ("G", "O")]
                if ch:
                    pe.wait_ge(state_ready, 2 * ch)
                for r in range(2):
                    for hh in range(2):
                        h, lo = 2 * r + hh, 64 * hh
                        if ch:
                            nc.tensor.matmul(o[hh][:, r * P:(r + 1) * P], expo[lo:lo + 64, r, 640:768], state[lo:lo + 64, r, :], start=True, stop=False)
                        last = nc.tensor.matmul(o[hh][:, r * P:(r + 1) * P], scT[:, h, :], gv[:, ch, h * P:(h + 1) * P], start=(ch == 0), stop=True)
                        if r == 1:
                            last.then_inc(bank["GO"[hh]].full, 1)
                if ch < TT - 1:
                    pe.wait_ge(kN_ready, ch + 1)
                    t, full = take_next("T", ("state", ch))
                    for r in range(2):
                        for hh in range(2):
                            h = 2 * r + hh
                            last = nc.tensor.matmul(t[64 * hh:64 * hh + 64, r * P:(r + 1) * P], kN[:, r * P + 64 * hh:r * P + 64 * hh + 64],
                                                    gv[:, ch, h * P:(h + 1) * P], start=True, stop=True)
                    last.then_inc(full, 1)

            def gla_turn(ch):
                pe.wait_ge(oan_ready, 4 * (ch + 1))
                t, full = take_next("T", ("oa", ch))
                for h in range(GLA_H):
                    last = nc.tensor.transpose(t[:, h * P:(h + 1) * P], oan[:, h * P:(h + 1) * P], ident[:, :])
                last.then_inc(full, 1)

            fill = [lambda cb=cb: inproj_T(("in", O_GQ), cb) for cb in range(4)]
            fill += [lambda tt=tt: inproj(("in", O_GV), tt) for tt in range(TT)]
            fill += [lambda tt=tt: inproj(("in", O_GG), tt) for tt in range(TT)]
            fill += [lambda tt=tt: inproj(("in", O_BG), tt) for tt in range(TT)]
            for u in range(NU + 1):
                ch, odd = (u - GLA_AT) // 2, (u - GLA_AT) % 2
                if u < NU:
                    attn_scores(u)
                if odd and 0 <= ch < TT:
                    gla_out(ch)
                if fill:
                    fill.pop(0)()
                if not odd and 0 < ch <= TT:
                    gla_turn(ch - 1)
                if u:
                    attn_out(u - 1)
                if not odd and 0 <= ch < TT:
                    gla_scores(ch)

            def gate_rows(dg, tag, names):
                for n, name in enumerate(names):
                    g = take(name, (tag, n))
                    nc.tensor.matmul(g[:, :], ones[:, :], dg[:, n * 512:(n + 1) * 512], start=True, stop=True).then_inc(bank[name].full, 1)

            pe.wait_ge(gd_ready, 1)
            gate_rows(diag, "gm", ("G", "O"))

            def branches(n, tt):
                split_wait(("proj", n))
                w = parts(("proj", n), KD)
                for b, key in enumerate(("g", "q")):
                    split_wait(key)
                    src = parts(key, 4)
                    a, full = take_next("A", ("y", n, tt, b))
                    for k in range(4):
                        last = split_matmul(a[:, :], [v[:, k, tt * P:(tt + 1) * P] for v in src], [v[:, 4 * b + k, :] for v in w], k == 0, k == 3)
                    last.then_inc(full, 1)
                if tt == TT - 1:
                    pe.wait_ge(full, bank[where[("y", n, tt, 1)]].at[("y", n, tt, 1)] + 1)
                    pe.sem_inc(ring_out, 1)

            for tt in range(TT):
                inproj(("in", O_BG + D), tt)
            for tt in range(TT):
                branches(0, tt)
            for ab in range(2):
                for tt in range(TT):
                    inproj(("in", O_BG + ab * D + 512), tt)
            for tt in range(TT):
                branches(1, tt)

            def mix_turn(tt):
                pe.wait_ge(mix_ready, TT + tt + 1)
                for half in range(2):
                    t, full = take_next("T", ("mix", tt, half))
                    for q in range(4):
                        k = 4 * half + q
                        last = nc.tensor.transpose(t[:, q * P:(q + 1) * P], mix[:, tt, k * P:(k + 1) * P], ident[:, :])
                    last.then_inc(full, 1)

            def out_proj(tt):
                for n in range(2):
                    split_wait(("out", n))
                    w = parts(("out", n), KD)
                    a, full = take_next("A", ("out", tt, n))
                    for k in range(KD):
                        if n == 0 and k == 0:
                            pe.wait_ge(mixT_ready[0], 2 * tt + 2)
                            pe.wait_ge(mixT_ready[1], 2 * tt + 2)
                        last = split_matmul(a[:, :], [mixT(tt % 2, part, P * k, P) for part in range(2)], [v[:, k, :] for v in w], k == 0, k == KD - 1)
                    last.then_inc(full, 1)
                if tt == TT - 1:
                    pe.wait_ge(full, bank[where[("out", tt, 1)]].at[("out", tt, 1)] + 1)
                    pe.sem_inc(ring_out, 2)

            def router(tt):
                pe.wait_ge(xn2_ready, tt + 1)
                for half in range(2):
                    t, full = take_next("T", ("x2", tt, half))
                    for q in range(4):
                        k = 4 * half + q
                        last = nc.tensor.transpose(t[:, q * P:(q + 1) * P], xn2[:, tt % 2, k * P:(k + 1) * P], ident[:, :])
                    last.then_inc(full, 1)
                for half in range(2):
                    pe.wait_ge(h2T_ready[half], 4 * (tt + 1))
                pe.wait_ge(ld_rt, 32)
                g = take("G", ("lg", tt))
                for k in range(KD):
                    last = nc.tensor.matmul(g[:, 0:GROUPS + NE], h2T[:, tt % 2, k, :], w_rt[:, k, :], start=(k == 0), stop=(k == KD - 1))
                last.then_inc(bank["G"].full, 1)

            def ranks(tt):
                o = take("O", "ranks") if tt == 0 else ps["O"]
                for i in range(tt + 1):
                    if i == tt:
                        pe.wait_ge(em_ready, tt + 1)
                    nc.tensor.matmul(o[:, tt * NE:(tt + 1) * NE], (before if i == tt else ones_b)[:, :], em[:, i, :], start=(i == 0), stop=(i == tt))
                if tt == TT - 1:
                    for i in range(TT):
                        last = nc.tensor.matmul(o[:, TT * NE:(TT + 1) * NE], ones_b[:, :], em[:, i, :], start=(i == 0), stop=(i == TT - 1))
                    last.then_inc(bank["O"].full, 1)

            mix_turn(0)
            for tt in range(TT + 1):
                if tt < TT - 1:
                    mix_turn(tt + 1)
                if tt < TT:
                    out_proj(tt)
                if tt >= 2:
                    ranks(tt - 2)
                if tt:
                    router(tt - 1)

            ranks(TT - 1)
            pe.wait_ge(ge_diag, 1)
            gate_rows(diag_e, "gf", ("S0", "S1"))
            g = take("G", "slots")
            for n in range(2 * TT):
                if n % TT == 0:
                    pe.wait_ge(pos_ready, n // TT + 1)
                last = nc.tensor.matmul(g[:, 0:2 * NPALL], lo_hot[:, n, :], hi_hot[:, n, :, :].rearrange("p w n -> p (w n)"), start=(n == 0), stop=(n == 2 * TT - 1))
            last.then_inc(bank["G"].full, 1)

            base = {n: len(b.at) for n, b in bank.items()}
            moe_base.update(base)

            def turn_rows(j, b):
                pe.wait_ge(xg_in, 16 * (j + 1))
                for half in range(2):
                    name = f"T{half}"
                    pe.wait_ge(bank[name].free, base[name] + j)
                    for q in range(4):
                        k = 4 * half + q
                        last = nc.tensor.transpose(ps[name][:, q * P:(q + 1) * P], xg[:, b, k * P:(k + 1) * P], ident[:, :])
                    last.then_inc(bank[name].full, 1)

            def pair(j, b, z, i, ahead=True):
                pe.wait_ge(bank["G"].free, base["G"] + j)
                pe.wait_ge(we_in[z], 16 * 8 * (i + 1))
                for half in range(2):
                    pe.wait_ge(h2g_ready[half], 4 * j + 4)
                for k in range(KD):
                    for q, w in enumerate(gu_sets[z]):
                        gu = w.rearrange("p (g k f) -> p g k f", g=2, k=KD)[:, :, k, :]
                        last = nc.tensor.matmul(ps["G"][64 * q:64 * q + 64, :].rearrange("p (g f) -> p g f", g=2), h2g[:, b, k, 64 * q:64 * q + 64], gu,
                                                start=(k == 0), stop=(k == KD - 1))
                last.then_inc(bank["G"].full, 1)
                if ahead:
                    turn_rows(j + 1, 1 - b)
                pe.wait_ge(act_ready, j + 1)
                pe.wait_ge(bank["O"].free, base["O"] + j)
                for q in range(2):
                    last = nc.tensor.transpose(ps["O"][:, q * P:(q + 1) * P], aact[:, b, q * P:(q + 1) * P], ident[:, :])
                last.then_inc(bank["O"].full, 1)
                pe.wait_ge(actT_ready, j + 1)
                for n in range(2):
                    name = f"A{n}"
                    pe.wait_ge(bank[name].free, base[name] + j)
                    for kf in range(2):
                        for q in range(2):
                            last = nc.tensor.matmul(ps[name][64 * q:64 * q + 64, :], actT[:, b, kf, 64 * q:64 * q + 64],
                                                    down_sets[z][q][kf][:, n * 512:(n + 1) * 512], start=(kf == 0), stop=(kf == 1))
                    last.then_inc(bank[name].full, 1)
                pe.wait_ge(bank["A1"].full, base["A1"] + j + 1)
                pe.sem_inc(we_used, 1)

            turn_rows(0, 0)
            for j in range(3):
                pair(j, j % 2, j, 0)
            with pe.Fori(1, NPAIR // 2 - 1) as i:
                pair(2 * i + 1, 1, 0, i)
                pair(2 * i + 2, 0, 1, i)
            pair(NPAIR - 1, 1, 0, NPAIR // 2 - 1, ahead=False)
            pe.wait_ge(route_ready, 1)
            n_ov = pe.value_load(ovi[0:1, NOV:NOV + 1], min_val=0, max_val=NOV // 2)
            with pe.If(n_ov > 0):
                with pe.Fori(0, n_ov) as v:
                    turn_rows(NPAIR + v, 0)
                    pair(NPAIR + v, 0, 1, NPAIR // 2 - 1 + v, ahead=False)

        @block.sync
        def _(sp):
            for tt in range(TT):
                sp.dma_start(x_in[:, tt, :], x_v[:, tt, :]).then_inc(ld_x[tt], 16)
            vecs = (g_pre_mix, g_pre_ffn, g_post_mix, g_post_ffn)
            for n, v in enumerate(vecs):
                sp.dma_start(vrows[8 * n:8 * n + 8, :], v[0].rearrange("(k p) -> k p", p=P)).then_inc(ld_vec, 16)
            sp.dma_start(vrows[32:34, :], b_gla_a[0].rearrange("(k p) -> k p", p=P)).then_inc(ld_vec, 16)
            sp.dma_start(vrows[34:42, :], c[0].rearrange("(k p) -> k p", p=P)).then_inc(ld_vec, 16)
            sp.dma_start(vrows[42:90, :], b_ada[0].rearrange("(k p) -> k p", p=P)).then_inc(ld_vec, 16)

            def load(n):
                it = items[n]
                if n >= 4:
                    sp.wait_ge(ring_out, {15: 13, 16: 14, 17: 15, 18: 16}.get(n, n - 3))
                dst, s = slot_of(it), ring_in[n % 4]
                if it[0] == "ada":
                    grp, q = it[1:]
                    sp.dma_start(dst.rearrange("p (k n) -> p k n", k=2), ada_v[:, 2 * q:2 * q + 2, grp * 2048:(grp + 1) * 2048]).then_inc(s, 16)
                elif it[0] == "in":
                    sp.dma_start(dst.rearrange("p (k n) -> p k n", k=KD), win_v[:, :, it[1]:it[1] + 512]).then_inc(s, 16)
                elif it[0] == "proj":
                    w = dst.rearrange("p (b k n) -> p b k n", b=2, k=4)
                    for b, src in enumerate((pg_v, pd_v)):
                        sp.dma_start(w[:, b, :, :], src[:, :, it[1] * 512:(it[1] + 1) * 512]).then_inc(s, 16)
                else:
                    sp.dma_start(dst.rearrange("p (k n) -> p k n", k=KD), wo_v[:, :, it[1] * 512:(it[1] + 1) * 512]).then_inc(s, 16)

            for n in range(4):
                load(n)
            load(4)
            load(5)
            sp.dma_start(w_small[:, :, 0:RANK], win_v[:, :, O_GA:O_GA + RANK]).then_inc(ld_small, 16)
            sp.dma_start(w_small[:, :, RANK:NS], win_v[:, :, O_IK:O_IK + 72]).then_inc(ld_small, 16)
            sp.dma_start(a2[:, :], w_gla_a2[0]).then_inc(ld_a2, 16)
            for n in range(6, len(items)):
                load(n)
                if n == 8:
                    sp.dma_start(w_rt[:, :, 0:GROUPS], w_router_g[0].rearrange("(k p) n -> p k n", p=P)).then_inc(ld_rt, 16)
                    sp.dma_start(w_rt[:, :, GROUPS:], w_router_e[0].rearrange("(k p) n -> p k n", p=P)).then_inc(ld_rt, 16)

            def gate_up(z, q, e):
                for n, src in enumerate((weg_v, weu_v)):
                    dst = gu_sets[z][q][:, 2048 * n:2048 * (n + 1)]
                    sp.dma_start(dst.rearrange("p (k f) -> p k f", k=KD), src[bass.ds(e, 1), :, :, :].rearrange("a p k f -> p (a k) f")).then_inc(we_in[z], 16)

            def down(z, q, e):
                for k in range(2):
                    sp.dma_start(down_sets[z][q][k], wed_v[bass.ds(e, 1), :, k, :].rearrange("a p n -> p (a n)")).then_inc(we_in[z], 16)

            def experts(z, e0, e1_):
                for q, e in enumerate((e0, e1_)):
                    gate_up(z, q, e)
                    down(z, q, e)

            sp.wait_ge(ring_out, item_at[("proj", 1)] + 1)
            experts(0, 0, 1)
            sp.wait_ge(ring_out, len(items))
            experts(1, 2, 3)
            gate_up(2, 0, 4)
            sp.wait_ge(bank["S1"].full, bank["S1"].at[("gf", 1)] + 1)
            sp.wait_ge(bank["G"].full, bank["G"].at["slots"] + 1)
            sp.wait_ge(xg_in, 16)
            gate_up(2, 1, 5)
            down(2, 1, 5)
            sp.wait_ge(route_ready, 1)
            down(2, 0, 4)
            sp.wait_ge(we_used, 1)
            experts(0, 6, 7)
            sp.wait_ge(we_used, 2)
            experts(1, 8, 9)
            with sp.Fori(2, NPAIR // 2 - 1) as i:
                sp.wait_ge(we_used, 2 * i)
                experts(0, 4 * i + 2, 4 * i + 3)
                sp.wait_ge(we_used, 2 * i + 1)
                experts(1, 4 * i + 4, 4 * i + 5)
            sp.wait_ge(we_used, NPAIR - 2)
            experts(0, NE - 2, NE - 1)
            n_ov = sp.value_load(ovi[0:1, NOV:NOV + 1], min_val=0, max_val=NOV // 2)
            with sp.If(n_ov > 0):
                with sp.Fori(0, n_ov) as v:
                    e_a = sp.value_load(ovi[0:1, bass.ds(2 * v, 1)], min_val=0, max_val=NE - 1)
                    e_b = sp.value_load(ovi[0:1, bass.ds(2 * v + 1, 1)], min_val=0, max_val=NE - 1)
                    sp.wait_ge(we_used, NPAIR + v)
                    experts(1, e_a, e_b)
            sp.wait_ge(y_stored[1], 16 * NPAIR // 2)
            sp.wait_ge(y_stored[0], 16 * (NPAIR // 2 + n_ov))
            for tt in range(TT):
                sp.dma_start(yc[:, tt, :, :], y_dram.rearrange("(w t p) n -> t p w n", w=2, p=P)[tt]).then_inc(yc_in[tt], 16)
            for tt in range(TT):
                sp.wait_ge(fin_ready, tt + 1)
                sp.dma_start(out_v[:, tt, :], x1(tt)).then_inc(out_done, 16)
            sp.wait_ge(out_done, 16 * TT)

        @block.gpsimd
        def _(pool):
            def step(ins):
                pstep_n[0] += 1
                ins.then_inc(pstep, 1)
                pool.wait_ge(pstep, pstep_n[0])

            pstep_n = [0]
            pool.dma_start(posi[:, :], positions[0].rearrange("(t p) -> p t", p=P), allow_slow_non_contiguous=True).then_inc(ld_pos, 16)
            pool.dma_start(rows[:, 0:128], g_gla_out).then_inc(ld_rows, 16)
            pool.dma_start(rows[:, 128:192], g_idx_k).then_inc(ld_rows, 16)
            pool.dma_start(rows[:, 192:196], b_router_g).then_inc(ld_rows, 16)
            pool.dma_start(rows[:, 196:228], b_router_e).then_inc(ld_rows, 16)
            step(pool.memset(ident[:, :], 0.0))
            pool.affine_select(out=ident[:, :], in_=ident[:, :], compare_op=ALU.not_equal, fill=1.0, base=0,
                               pattern=[[-1, P]], channel_multiplier=1).then_inc(const_ready, 1)
            pool.memset(ones[:, :], 1.0).then_inc(const_ready, 1)
            pool.wait_ge(const_ready, 2)
            step(pool.memset(ones_b[:, :], 1.0))
            step(pool.affine_select(out=before[:, :], in_=ones_b[:, :], compare_op=ALU.is_gt, fill=0.0, base=0,
                                    pattern=[[1, P]], channel_multiplier=-1))
            step(pool.affine_select(out=upto[:, :], in_=ones[:, :], compare_op=ALU.is_ge, fill=0.0, base=0,
                                    pattern=[[1, P]], channel_multiplier=-1))
            step(pool.memset(causal0[:, :], 0.0))
            step(pool.affine_select(out=causal0[:, :], in_=causal0[:, :], compare_op=ALU.is_ge, fill=HIDE, base=0,
                                    pattern=[[-1, P]], channel_multiplier=1))
            for dst, pattern, start, by_row in ((iotaf[:, :], [[1, NE]], 0, 0), (giota[:, :], [[1, GROUPS], [0, PER_GROUP]], 0, 0),
                                                (base_m[:, :], [[-SLOT, NE]], SLOT * (NE - 1), 0), (thr[:, :], [[SLOT, SEQ // SLOT]], SLOT, 0),
                                                (iota_hi[:, :], [[P, NPALL + 1]], 0, 0), (iota_lo[:, :], [[1, P]], -P, 0),
                                                (rowid[:, :, :, 0], [[0, 2], [-P, TT]], int(NONE), -1), (rowid[:, :, :, 1], [[-SEQ, 2], [-P, TT]], int(NONE), -1)):
                step(pool.iota(dst, pattern=pattern, base=start, channel_multiplier=by_row, allow_small_or_imprecise_dtypes=True))
            pool.memset(gp[:, :, :], HIDE).then_inc(const_ready, 1)
            pool.sem_inc(pstep_const, 1)

            def rotate(xv, cosv, sinv, nsinv, tmp):
                step(pool.tensor_tensor(tmp[..., 0:HALF], xv[..., HALF:ROT], nsinv, ALU.mult))
                step(pool.tensor_tensor(tmp[..., HALF:ROT], xv[..., 0:HALF], sinv, ALU.mult))
                step(pool.tensor_tensor(xv[..., 0:HALF], xv[..., 0:HALF], cosv, ALU.mult))
                step(pool.tensor_tensor(xv[..., HALF:ROT], xv[..., HALF:ROT], cosv, ALU.mult))
                return pool.tensor_tensor(xv[..., 0:ROT], xv[..., 0:ROT], tmp[..., 0:ROT], ALU.add)

            pool.wait_ge(rope_ready, 1)

            def rope_stage(n):
                pool.wait_ge(stage_in, n + 1)
                if n:
                    pool.wait_ge(stage_roped, n)
                tt = n % TT
                xv = stage[:, n % 4, :].rearrange("p (h d) -> p h d", h=HEADS)
                cs_, sn_, ns_ = (v.unsqueeze(1).broadcast_to([P, HEADS, HALF]) for v in (rope[:, 2, tt, :], rope[:, 3, tt, :], nsin[:, tt, :]))
                rotate(xv, cs_, sn_, ns_, rtmp[:, :, :]).then_inc(stage_roped, 1)

            for n in range(3 * TT):
                rope_stage(n)

            def gla_exponents(ch):
                if ch:
                    filled(pool, ("o", ch - 1), "G")
                    filled(pool, ("o", ch - 1), "O")
                for r in range(2):
                    b = bT[:, r, ch * P:(ch + 1) * P]
                    b3 = b.rearrange("p (i t) -> p i t", i=NB)
                    ref = b3[:, :, BLK // 2 - 1:BLK // 2]
                    pool.tensor_tensor(expo[:, r, 0:512].rearrange("p (i s) -> p i s", i=NB), ref.broadcast_to([P, NB, P]),
                                       b.unsqueeze(1).broadcast_to([P, NB, P]), ALU.subtract).then_inc(ex_sub, 1)
                    pool.tensor_tensor(expo[:, r, 512:640].rearrange("p (i t) -> p i t", i=NB), b3, ref.broadcast_to([P, NB, BLK]),
                                       ALU.subtract).then_inc(ex_sub, 1)

            pool.wait_ge(b_ready, 2 * TT)
            filled(pool, ("idx", TT - 1, PAIRS - 1), "S1")
            pool.wait_ge(rowb_ready, 1)
            for tt in range(TT):
                gla_exponents(tt)
                pool.wait_ge(gs_in, tt + 1)
                g3 = gs[:, tt, :].rearrange("p (h n) -> p h n", h=GLA_H)
                pool.tensor_tensor(g3, g3, g_out_b.unsqueeze(1).broadcast_to([P, GLA_H, P]), ALU.mult).then_inc(gs_ready, 1)
            pool.wait_ge(mixT_ready[1], 2 * TT)
            filled(pool, ("mix", TT - 1, 0))
            filled(pool, ("mix", TT - 1, 1))
            pool.memset(xg[:, :, :], 0.0).then_inc(xg_clear, 1)
            pool.wait_ge(xg_clear, 1)
            pool.wait_ge(h2m_ready, 1)
            pool.wait_ge(ring_out, len(items))
            pool.tensor_tensor(diag_e.rearrange("p (k n) -> p k n", k=KD), ident[:, :].unsqueeze(1).broadcast_to([P, KD, P]),
                               gatev[:, 1, :].unsqueeze(2).broadcast_to([P, KD, P]), ALU.mult).then_inc(ge_diag, 1)
            pool.wait_ge(slot_ready, 1)
            for b in range(2):
                pool.wait_ge(xn2_stored[b], 32)

            def index(table, which, b, j, count):
                pool.tensor_copy(idx_c[:, which, b:b + 1], table[:, bass.ds(j, 1)]).then_inc(idx_set, 1)
                pool.wait_ge(idx_set, count)
                pool.sem_inc(idx_seen, 1)

            def gather(j, b, count):
                index(src_i, 0, b, j, count)
                pool.indirect_dma_start(out=xg[:, b, :], out_offset=None, in_=xn_dram, in_offset=bass.IndirectOffsetOnAxis(ap=idx_c[:, 0, b:b + 1], axis=0),
                                        bounds_check=SEQ - 1, oob_is_err=False).then_inc(xg_in, 16)

            def gather2(j, b, count):
                pool.wait_ge(bank["T1"].full, moe_base["T1"] + j - 1)
                pool.wait_ge(xg_in, 16 * j)
                gather(j, b, count)

            def scatter(j, b, count, before):
                pool.wait_ge(yb_ready, j + 1)
                pool.wait_ge(yb_act, j + 1)
                if before is not None:
                    pool.wait_ge(y_stored[b], 16 * before)
                index(dst_i, 1, b, j, count)
                pool.indirect_dma_start(out=y_dram, out_offset=bass.IndirectOffsetOnAxis(ap=idx_c[:, 1, b:b + 1], axis=0), in_=yb[:, b, :], in_offset=None,
                                        bounds_check=2 * SEQ - 1, oob_is_err=False).then_inc(y_stored[b], 16)

            gather(0, 0, 1)
            pool.wait_ge(xg_in, 16)
            gather(1, 1, 2)
            pool.wait_ge(xg_in, 32)
            gather2(2, 0, 3)
            scatter(0, 0, 4, None)
            gather2(3, 1, 5)
            scatter(1, 1, 6, None)
            with pool.Fori(1, NPAIR // 2 - 1) as i:
                gather2(2 * i + 2, 0, 4 * i + 3)
                scatter(2 * i, 0, 4 * i + 4, i)
                gather2(2 * i + 3, 1, 4 * i + 5)
                scatter(2 * i + 1, 1, 4 * i + 6, i)
            for b in range(2):
                scatter(NPAIR - 2 + b, b, 2 * NPAIR - 1 + b, NPAIR // 2 - 1)
            n_ov = pool.value_load(ovi[0:1, NOV:NOV + 1], min_val=0, max_val=NOV // 2)
            with pool.If(n_ov > 0):
                with pool.Fori(0, n_ov) as v:
                    gather2(NPAIR + v, 0, 2 * NPAIR + 1 + 2 * v)
                    scatter(NPAIR + v, 0, 2 * NPAIR + 2 + 2 * v, NPAIR // 2 + v)
            for tt in range(TT):
                pool.wait_ge(fss_ready, tt + 1)
                pool.tensor_tensor(yc[:, tt, 1, :], yc[:, tt, 0, :], gfb, ALU.mult).then_inc(fg_ready, 1)

        @block.scalar
        def _(act):
            scratch = kv[:, 0:D]
            for tt in range(TT):
                act.wait_ge(ld_x[tt], 16)
                nc.scalar.activation(scratch[:, 0:D], x_in[:, tt, :], ACT.Square, accum_out=st[:, tt:tt + 1]).then_inc(ss_ready, 1)
                act.wait_ge(ss_ready, tt + 1)
            act.wait_ge(rs_ready, 1)
            nc.scalar.activation(st[:, 8:12], st[:, 4:8], ACT.Sqrt).then_inc(ss_ready, 1)
            act.wait_ge(vT_ready, 1)
            nc.scalar.activation(cs[:, :], vT[:, 34:42], ACT.Sigmoid).then_inc(c_ready, 1)
            act.wait_ge(sin_in, 1)
            nc.scalar.activation(rope[:, 3, :, :], rope[:, 0, :, :], ACT.Sin).then_inc(sin_out, 1)
            nc.scalar.activation(rope[:, 2, :, :], rope[:, 0, :, :], ACT.Sin, scale=0.5).then_inc(sin_out, 1)
            for k in range(0, KD, 2):
                t, free = filled(act, ("x", k))
                nc.scalar.copy(hT[:, k, :], t[:, :]).then_inc(free, 1)
                act.wait_ge(free, bank[where[("x", k)]].at[("x", k)] + 1)
                act.sem_inc(hraw, 1)

            def mod_row(grp):
                a, free = filled(act, ("ada", grp))
                if grp:
                    filled(act, ("mod", grp - 1))
                nc.scalar.copy(mrow[:, :], a[:, :]).then_inc(mrow_ready, 1)
                act.wait_ge(mrow_ready, grp + 1)
                act.sem_inc(free, 1)

            mod_row(0)

            nst = [0]

            def to_stage(turn):
                a, free = filled(act, turn)
                n = nst[0]
                if n >= 4:
                    filled(act, stage_turns[n - 4])
                nc.scalar.copy(stage[:, n % 4, :], a[:, :]).then_inc(stage_in, 1)
                act.wait_ge(stage_in, n + 1)
                act.sem_inc(free, 1)
                nst[0] += 1

            stage_turns = [("iq", t) for t in range(TT)] + [("dk", t) for t in range(TT)] + [("dq", t) for t in range(TT)]

            def spread(turn, dst, done):
                t, free = filled(act, turn)
                nc.scalar.copy(dst, t[:, :].rearrange("p (c n) -> p c n", c=4)).then_inc(done, 1)
                act.wait_ge(done, spread_n.setdefault(done.name, 0) + 1)
                spread_n[done.name] += 1
                act.sem_inc(free, 1)

            spread_n = {}
            def ada_load(m):
                act.dma_start(adab[:, m % 2, :], ada_v[:, m % KD, (1 + m // KD) * 2048:(2 + m // KD) * 2048]).then_inc(ada_in[m % 2], 16)

            for m in range(2):
                ada_load(m)
            for tt in range(TT):
                to_stage((("in", O_IQ), tt))
            for tt in range(TT):
                a, free = filled(act, ("small", tt))
                nc.scalar.copy(ikw[:, tt, :], a[:, 0:NS]).then_inc(ikw_in, 1)
                act.wait_ge(ikw_in, tt + 1)
                act.sem_inc(free, 1)
            act.wait_ge(lnv_ready, 1)
            nc.scalar.activation(st[:, 56:60], st[:, 52:56], ACT.Sqrt).then_inc(lnq_ready, 1)
            for tt in range(TT):
                spread(("iq", tt), qiT[:, :, tt * P:(tt + 1) * P], qiT_ready)
                to_stage((("in", O_DK), tt))
            t, free = filled(act, "ki")
            nc.scalar.copy(kiT, t[:, :]).then_inc(kiT_ready, 1)
            act.wait_ge(kiT_ready, 1)
            act.sem_inc(free, 1)
            t, free = filled(act, "ga")
            nc.scalar.copy(gaT[:, :], t[0:RANK, :]).then_inc(gaT_ready, 1)
            act.wait_ge(gaT_ready, 1)
            act.sem_inc(free, 1)

            def do_dq(tt):
                spread(("dk", tt), kT[:, :, tt * P:(tt + 1) * P], kT_ready)
                to_stage((("in", O_DQ), tt))

            def do_dv(tt):
                spread(("dq", tt), qT[:, :, tt * P:(tt + 1) * P], qT_ready)
                a, free = filled(act, (("in", O_DV), tt))
                nc.scalar.copy(val[:, tt, :], a[:, :]).then_inc(val_ready, 1)
                act.wait_ge(val_ready, tt + 1)
                act.sem_inc(free, 1)

            fill = [lambda tt=tt: do_dq(tt) for tt in range(TT)] + [lambda tt=tt: do_dv(tt) for tt in range(TT)]
            for n in range(3 * PAIRS):
                tq, hp = 1 + n // PAIRS, n % PAIRS
                w = (tq + 1) * P
                if n in (4, 8):
                    mod_row(n // 4)
                for hh in range(2):
                    s, free = filled(act, ("idx", tq, hp), f"S{hh}")
                    if n:
                        act.wait_ge(relu_used, 2 * (n - 1) + hh + 1)
                    nc.scalar.activation(relu[:, hh, 0:w], s[:, 0:w], ACT.Relu, scale=64 ** -0.5).then_inc(relu_ready, 1)
                    act.wait_ge(relu_ready, 2 * n + hh + 1)
                    act.sem_inc(free, 1)
                if n == 6:
                    act.wait_ge(z_in, 1)
                    nc.scalar.activation(zz[:, 1, :, :], zz[:, 1, :, :], ACT.Exp).then_inc(zexp_ready, 1)
                    act.wait_ge(zexp_ready, 1)
                    nc.scalar.activation(zz[:, 2, :, :], zz[:, 1, :, :], ACT.Ln, bias=1.0).then_inc(zexp_ready, 1)
                for m in range(2 * n + 2, min(2 * n + 4, 2 * KD)):
                    act.wait_ge(ada_out, m - 1)
                    ada_load(m)
                if n % 3 != 1:
                    fill.pop(0)()

            def simple(turn, dst, done, count, **kw):
                a, free = filled(act, turn)
                nc.scalar.activation(dst, a[:, :], kw.get("func", ACT.Copy), scale=kw.get("scale", 1.0)).then_inc(done, 1)
                act.wait_ge(done, count)
                act.sem_inc(free, 1)

            fill = [lambda cb=cb: simple((("in", O_GQ), cb), gqk[:, cb, :], gqk_ready, cb + 1, scale=GLA_DK ** -0.5 if cb < 2 else 1.0) for cb in range(4)]
            fill += [lambda tt=tt: simple((("in", O_GV), tt), gv[:, tt, :], gv_ready, tt + 1) for tt in range(TT)]
            fill += [lambda tt=tt: simple((("in", O_GG), tt), gs[:, tt, :], gs_in, tt + 1, func=ACT.Silu) for tt in range(TT)]

            def sigmoid(half, ab, tt):
                turn = (("in", O_BG + ab * D + 512 * half), tt)
                if half:
                    act.wait_ge(mix_ready, tt + 1)
                simple(turn, sig[:, ab, tt, :], sig_ready, half * 2 * TT + ab * TT + tt + 1, func=ACT.Sigmoid)

            fill += [lambda tt=tt: sigmoid(0, 0, tt) for tt in range(TT)]

            def gla_exp(ch):
                act.wait_ge(ex_in, ch + 1)
                nc.scalar.activation(expo[:, :, 0:640], expo[:, :, 0:640], ACT.Exp, scale=1.0 / TAU).then_inc(ex_exp, 1)
                b = bT[:, :, ch * P:(ch + 1) * P]
                nc.scalar.activation(expo[:, :, 640:768], b, ACT.Exp, scale=1.0 / TAU).then_inc(ex_exp, 1)
                for r in range(2):
                    nc.scalar.activation(expo[:, r, 768:896], b[:, r, :], ACT.Exp, bias=bend[:, r:r + 1], scale=-1.0 / TAU).then_inc(ex_exp, 1)

            gscr = stage_mem[:, 0:P]

            def gla_squares(ch):
                for h in range(GLA_H):
                    o, _ = filled(act, ("o", ch), "GO"[h % 2])
                    r = h // 2
                    nc.scalar.activation(gscr, o[:, r * P:(r + 1) * P], ACT.Square, accum_out=st[:, 16 + h:17 + h]).then_inc(oss_ready, 1)
                    act.wait_ge(oss_ready, 4 * ch + h + 1)
                act.wait_ge(oms_ready, ch + 1)
                nc.scalar.activation(st[:, 24:28], st[:, 20:24], ACT.Sqrt).then_inc(osq_ready, 1)

            for u in range(NU + 1):
                tq, hp = u // PAIRS, u % PAIRS
                n = (tq + 1) * P
                ch, odd = (u - GLA_AT) // 2, (u - GLA_AT) % 2
                if u < NU:
                    for hh in range(2):
                        act.wait_ge(s_masked, 2 * u + hh + 1)
                        z = 4 * (u % 2)
                        nc.scalar.activation(prob[:, u % 2, hh, 0:n], prob[:, u % 2, hh, 0:n], ACT.Exp, bias=sm[:, hh, z + 1:z + 2],
                                             scale=HD ** -0.5, accum_out=sm[:, hh, z + 2:z + 3]).then_inc(p_exp, 1)
                if not odd and 0 <= ch < TT:
                    gla_exp(ch)
                if odd and 0 <= ch < TT:
                    gla_squares(ch)
                if fill:
                    fill.pop(0)()
                if u:
                    v = u - 1
                    vq, vp = v // PAIRS, v % PAIRS
                    m = (vq + 1) * P
                    t, free = filled(act, ("p", v, 0))
                    if v >= 2:
                        filled(act, ("att", v - 2), "O")
                    nc.scalar.copy(probT[:, v % 2, 0, 0:m], t[:, 0:m]).then_inc(pT_ready[0], 1)
                    act.wait_ge(pT_ready[0], v + 1)
                    act.sem_inc(free, 1)
                    o, free = filled(act, ("att", v), "O")
                    nc.scalar.copy(qT[:, vp, vq * P:(vq + 1) * P], o[:, 0:P]).then_inc(ob_ready, 1)
                    act.wait_ge(ob_ready, v + 1)
                    act.sem_inc(free, 1)
                if not odd and 0 <= ch < TT:
                    t, free = filled(act, ("kN", ch))
                    if ch:
                        filled(act, ("state", ch - 1))
                    nc.scalar.copy(kN[:, :], t[:, 0:256]).then_inc(kN_ready, 1)
                    act.wait_ge(kN_ready, ch + 1)
                    act.sem_inc(free, 1)
            scratch = gla_mem[:, 0:D]

            def split_hi(key):
                src, _, hi = splits[key]
                nc.scalar.copy(hi, src).then_inc(hi_ready, 1)

            split_hi("h")
            sigmoid(0, 1, 0)
            act.wait_ge(ring_out, item_at[("in", O_BG)] + 1)
            ring_wait(act, ("proj", 0))
            split_hi(("proj", 0))
            sigmoid(0, 1, 1)
            act.wait_ge(oa_ready, TT)
            filled(act, ("gm", 0), "G")
            filled(act, ("gm", 1), "O")
            split_hi("g")
            split_hi("q")
            sigmoid(0, 1, 2)
            sigmoid(0, 1, 3)
            act.wait_ge(ring_out, item_at[("in", O_BG + D)] + 1)
            act.wait_ge(lo_ready, split_at["h"] + 1)
            ring_wait(act, ("in", O_BG + 512))
            split_hi(("in", O_BG + 512))
            for ab, (used, key) in enumerate(((("proj", 0), ("in", O_BG + D + 512)), (("in", O_BG + 512), ("proj", 1)))):
                sigmoid(1, ab, 0)
                act.wait_ge(ring_out, item_at[used] + 1)
                ring_wait(act, key)
                split_hi(key)
                for tt in range(1, TT):
                    sigmoid(1, ab, tt)
            act.wait_ge(ring_out, item_at[("in", O_BG + D + 512)] + 1)
            for n in range(2):
                ring_wait(act, ("out", n))
                split_hi(("out", n))

            def rms_of(tt):
                for n in range(2):
                    a, _ = filled(act, ("out", tt, n))
                    nc.scalar.activation(scratch[:, 0:512], a[:, :], ACT.Square, accum_out=st[:, 28 + n:29 + n]).then_inc(rss_ready, 1)
                    act.wait_ge(rss_ready, 2 * tt + n + 1)
                act.wait_ge(rms_ready, tt + 1)
                nc.scalar.activation(st[:, 31:32], st[:, 30:31], ACT.Sqrt).then_inc(rsq_ready, 1)
                act.wait_ge(x1_ready, tt + 1)
                if tt + 2 < TT:
                    act.dma_start(xres[:, tt % 2, :], x_v[:, tt + 2, :]).then_inc(ld_xr[tt % 2], 16)
                nc.scalar.activation(scratch[:, 0:D], x1(tt), ACT.Square, accum_out=st[:, 33:34]).then_inc(xss_ready, 1)
                act.wait_ge(xss_ready, tt + 1)
                act.wait_ge(xms_ready, tt + 1)
                nc.scalar.activation(st[:, 35:36], st[:, 34:35], ACT.Sqrt).then_inc(xsq_ready, 1)
                act.wait_ge(xn2_ready, tt + 1)
                act.dma_start(xn_dram[tt * P:(tt + 1) * P, :], xn2[:, tt % 2, :]).then_inc(xn2_stored[tt % 2], 16)

            def shifted(dst, src, k, done):
                return nc.scalar.activation(dst, src, ACT.Identity, bias=modT[:, 1, 8 + k:9 + k], scale=scale2[:, k:k + 1]).then_inc(done, 1)

            act.wait_ge(h2m_ready, 1)
            def mix_copy(tt):
                if tt == 1:
                    act.wait_ge(ring_out, item_at[("proj", 1)] + 1)
                if tt >= 2:
                    filled(act, ("out", tt - 2, 1))
                for half in range(2):
                    t, _ = filled(act, ("mix", tt, half))
                    nc.scalar.copy(mixT(tt % 2, 0, 512 * half, 512), t[:, :]).then_inc(mixT_ready[0], 1)

            mix_copy(0)
            act.wait_ge(ring_out, item_at[("proj", 1)] + 1)
            for tt in range(2):
                act.dma_start(xres[:, tt, :], x_v[:, tt, :]).then_inc(ld_xr[tt], 16)
            for tt in range(TT + 1):
                if tt < TT - 1:
                    mix_copy(tt + 1)
                if tt:
                    t, free = filled(act, ("x2", tt - 1, 1))
                    if tt >= 3:
                        filled(act, ("lg", tt - 3), "G")
                    for q in range(4):
                        shifted(h2T[:, (tt - 1) % 2, 4 + q, :], t[:, q * P:(q + 1) * P], 4 + q, h2T_ready[1])
                    act.wait_ge(h2T_ready[1], 4 * tt)
                    act.sem_inc(free, 1)
                if tt < TT:
                    rms_of(tt)
            act.wait_ge(x1_ready, TT)
            for n in range(2):
                g, free = filled(act, ("gf", n), f"S{n}")
                nc.scalar.copy(gfb[:, n * 512:(n + 1) * 512], g[:, :]).then_inc(free, 1)
            act.wait_ge(ge_in, 1)
            nc.scalar.activation(gp[:, :, 0:GROUPS], gp[:, :, 0:GROUPS], ACT.Exp)
            nc.scalar.activation(rt[:, 4, :], rt[:, 3, :], ACT.Exp).then_inc(ge_out, 1)

            def pair(j, b, back, stores):
                act.wait_ge(bank["T1"].full, moe_base["T1"] + j + 1)
                act.wait_ge(bank["G"].full, moe_base["G"] + back)
                for q in range(4):
                    shifted(h2g[:, b, 4 + q, :], ps["T1"][:, q * P:(q + 1) * P], 4 + q, h2g_ready[1])
                act.wait_ge(h2g_ready[1], 4 * j + 4)
                act.sem_inc(bank["T1"].free, 1)
                act.wait_ge(bank["G"].full, moe_base["G"] + j + 1)
                nc.scalar.activation(gact[:, b, :], ps["G"][:, 0:DE], ACT.Silu).then_inc(silu_ready, 1)
                act.wait_ge(bank["O"].full, moe_base["O"] + j + 1)
                act.wait_ge(bank["A1"].full, moe_base["A1"] + back)
                nc.scalar.copy(actT[:, b, :, :], ps["O"][:, 0:DE].rearrange("p (k n) -> p k n", k=2)).then_inc(actT_ready, 1)
                act.wait_ge(actT_ready, j + 1)
                act.sem_inc(bank["O"].free, 1)
                act.wait_ge(bank["A1"].full, moe_base["A1"] + j + 1)
                if stores is not None:
                    act.wait_ge(y_stored[b], 16 * stores)
                nc.scalar.copy(yb[:, b, 512:1024], ps["A1"][:, :]).then_inc(yb_act, 1)
                act.wait_ge(yb_act, j + 1)
                act.sem_inc(bank["A1"].free, 1)

            pair(0, 0, 0, None)
            pair(1, 1, 0, None)
            with act.Fori(1, NPAIR // 2) as i:
                pair(2 * i, 0, 2 * i - 1, i)
                pair(2 * i + 1, 1, 2 * i, i)
            n_ov = act.value_load(ovi[0:1, NOV:NOV + 1], min_val=0, max_val=NOV // 2)
            with act.If(n_ov > 0):
                with act.Fori(0, n_ov) as v:
                    pair(NPAIR + v, 0, NPAIR + v, NPAIR // 2 + v)
            scratch2 = stage_mem[:, 0:D]
            nc.scalar.activation(st[:, 44:45], st[:, 34:35], ACT.Sqrt).then_inc(fsq_early, 1)

            def first_choice(tt):
                act.wait_ge(yc_in[tt], 16)
                nc.scalar.activation(yc[:, tt, 0, :], yc[:, tt, 0, :], ACT.Copy, scale=rt[:, 9, tt:tt + 1]).then_inc(fw_ready, 1)

            first_choice(0)
            for tt in range(TT):
                if tt + 1 < TT:
                    first_choice(tt + 1)
                act.wait_ge(fss_ready, tt + 1)
                nc.scalar.activation(scratch2, yc[:, tt, 0, :], ACT.Square, accum_out=st[:, 40:41]).then_inc(fms_ready, 1)
                act.wait_ge(fms_ready, tt + 1)
                act.wait_ge(fsq_in, tt + 1)
                nc.scalar.activation(st[:, 42:43], st[:, 41:42], ACT.Sqrt).then_inc(fsq_ready, 1)

        @block.vector
        def _(dve):
            dn = [0]

            def step(ins):
                dn[0] += 1
                ins.then_inc(dstep, 1)
                dve.wait_ge(dstep, dn[0])

            V = nc.vector

            def rsqrt_in(dst, src, n):
                return V.tensor_scalar(dst, src, 1.0 / n, EPS, ALU.mult, ALU.add)

            t, free = filled(dve, "vec")
            V.tensor_copy(vT[:, :], t[:, 0:90]).then_inc(vT_ready, 1)
            dve.wait_ge(vT_ready, 1)
            dve.sem_inc(free, 1)
            dve.wait_ge(ld_pos, 16)
            step(V.tensor_copy(posf[:, :], posi[:, :]))
            for j in range(HALF):
                freq = float(np.power(np.float32(THETA), np.float32(-j * 2.0 / ROT)))
                V.tensor_scalar(rope[:, 0, :, j], posf[:, :], freq, None, ALU.mult).then_inc(sin_in2, 1)
            dve.wait_ge(sin_in2, HALF)
            magic = 1.5 * 2 ** 23
            step(V.tensor_scalar(rope[:, 1, :, :], rope[:, 0, :, :], 1 / (2 * np.pi), magic, ALU.mult, ALU.add))
            step(V.tensor_scalar(rope[:, 1, :, :], rope[:, 1, :, :], magic, None, ALU.subtract))
            rest = 2 * np.pi
            for bits in (2 ** 8, 2 ** 18, None):
                part = round(rest * bits) / bits if bits else rest
                rest -= part
                step(V.scalar_tensor_tensor(rope[:, 0, :, :], rope[:, 1, :, :], -part, rope[:, 0, :, :], ALU.mult, ALU.add))
            V.tensor_scalar(rope[:, 0, :, :], rope[:, 0, :, :], 3.1415925, -3.1415925, ALU.min, ALU.max).then_inc(sin_in, 1)
            dve.wait_ge(ss_ready, TT)
            rsqrt_in(st[:, 4:8], st[:, 0:4], D).then_inc(rs_ready, 1)
            dve.wait_ge(ss_ready, TT + 1)
            step(V.reciprocal(st[:, 12:16], st[:, 8:12]))
            for tt in range(TT):
                V.tensor_scalar(x_in[:, tt, :], x_in[:, tt, :], st[:, 12 + tt:13 + tt], None, ALU.mult).then_inc(xn_ready, 1)
            dve.wait_ge(c_ready, 1)
            V.tensor_tensor(c32[:, :, :], vT[:, 34:42].unsqueeze(2).broadcast_to([P, KD, 32]), cs[:, :].unsqueeze(2).broadcast_to([P, KD, 32]), ALU.mult).then_inc(c32_ready, 1)
            dve.wait_ge(sin_out, 2)
            step(V.tensor_tensor(rope[:, 1, :, :], rope[:, 2, :, :], rope[:, 2, :, :], ALU.mult))
            step(V.tensor_scalar(rope[:, 2, :, :], rope[:, 1, :, :], -2.0, 1.0, ALU.mult, ALU.add))
            step(V.tensor_scalar(nsin[:, :, :], rope[:, 3, :, :], -1.0, None, ALU.mult))
            dve.sem_inc(rope_ready, 1)
            g, free = filled(dve, "rows", "G")
            V.tensor_copy(rowb[:, :], g[:, 0:228]).then_inc(rowb_ready, 1)
            dve.wait_ge(rowb_ready, 1)
            dve.sem_inc(free, 1)
            for k in range(1, KD, 2):
                t, free = filled(dve, ("x", k))
                step(V.tensor_copy(hT[:, k, :], t[:, :]))
                dve.sem_inc(free, 1)

            def mod_take(grp):
                t, free = filled(dve, ("mod", grp))
                step(V.tensor_tensor(modT[:, grp, :].rearrange("p (j q) -> p j q", q=4), t[:, :].rearrange("p (q j r) -> p j q r", q=4, j=4)[:, :, :, 0],
                                     vT[:, 42 + 16 * grp:58 + 16 * grp].rearrange("p (j q) -> p j q", q=4), ALU.add))
                dve.sem_inc(free, 1)

            mod_take(0)
            step(V.scalar_tensor_tensor(scale1[:, :], modT[:, 0, 8:16], 1.0, vT[:, 0:8], ALU.add, ALU.mult))
            for k in range(KD):
                if k % 2 == 0:
                    dve.wait_ge(hraw, k // 2 + 1)
                V.tensor_scalar(hT[:, k, :], hT[:, k, :], scale1[:, k:k + 1], modT[:, 0, k:k + 1], ALU.mult, ALU.add).then_inc(h_ready, 1)

            dve.wait_ge(ikw_in, TT)
            ik = ikw[:, :, RANK:RANK + 64]
            step(V.tensor_reduce(st[:, 44:48], ik, AX.X, ALU.add))
            step(V.tensor_scalar(st[:, 44:48], st[:, 44:48], 1.0 / 64, None, ALU.mult))
            mu = st[:, 44:48].unsqueeze(2).broadcast_to([P, TT, 64])
            step(V.tensor_tensor(ik, ik, mu, ALU.subtract))
            step(V.tensor_tensor(kin[:, :, 0, :], ik, ik, ALU.mult))
            step(V.tensor_reduce(st[:, 48:52], kin[:, :, 0, :], AX.X, ALU.add))
            V.tensor_scalar(wi[:, :, :], ikw[:, :, RANK + 64:NS], 8 ** -0.5, None, ALU.mult).then_inc(wi_ready, 1)
            rsqrt_in(st[:, 52:56], st[:, 48:52], 64).then_inc(lnv_ready, 1)
            dve.wait_ge(lnq_ready, 1)
            step(V.reciprocal(st[:, 60:64], st[:, 56:60]))
            step(V.tensor_tensor(ik, ik, st[:, 60:64].unsqueeze(2).broadcast_to([P, TT, 64]), ALU.mult))
            step(V.tensor_tensor(kin[:, :, 0, :], ik, g_ki_b.unsqueeze(1).broadcast_to([P, TT, 64]), ALU.mult))
            ki = kin[:, :, 0, :]
            step(V.tensor_tensor(kin[:, :, 1, 0:HALF], ki[:, :, HALF:ROT], nsin[:, :, :], ALU.mult))
            step(V.tensor_tensor(kin[:, :, 1, HALF:ROT], ki[:, :, 0:HALF], rope[:, 3, :, :], ALU.mult))
            step(V.tensor_tensor(ki[:, :, 0:HALF], ki[:, :, 0:HALF], rope[:, 2, :, :], ALU.mult))
            step(V.tensor_tensor(ki[:, :, HALF:ROT], ki[:, :, HALF:ROT], rope[:, 2, :, :], ALU.mult))
            step(V.tensor_tensor(ki[:, :, 0:ROT], ki[:, :, 0:ROT], kin[:, :, 1, 0:ROT], ALU.add))
            V.tensor_copy(kin[:, :, 1, :], ki).then_inc(ki_ready, 1)

            queue = []

            def topk_round(tq, w):
                work = mask[:, tq - 1, 0:w]
                step(V.max(m8[:, :], work))
                step(V.match_replace(work, m8[:, :], work, TAKEN))

            def topk_end(tq, w):
                work = mask[:, tq - 1, 0:w]
                step(V.tensor_scalar(work, work, TAKEN * 0.7, HIDE, ALU.is_gt, ALU.mult))

            def some(n):
                for _ in range(n):
                    if queue:
                        queue.pop(0)()

            dve.wait_ge(const_ready, 3)
            dve.wait_ge(pstep_const, 1)
            for n in range(3 * PAIRS):
                tq, hp = 1 + n // PAIRS, n % PAIRS
                w = (tq + 1) * P
                acc = mask[:, tq - 1, 0:w]
                for hh in range(2):
                    h = 2 * hp + hh
                    dve.wait_ge(relu_ready, 2 * n + hh + 1)
                    if h == 0:
                        ins = V.tensor_scalar(acc, relu[:, hh, 0:w], wi[:, tq, 0:1], None, ALU.mult)
                    else:
                        ins = V.scalar_tensor_tensor(acc, relu[:, hh, 0:w], wi[:, tq, h:h + 1], acc, ALU.mult, ALU.add)
                    ins.then_inc(relu_used, 1)
                    dve.wait_ge(relu_used, 2 * n + hh + 1)
                if hp == PAIRS - 1:
                    step(V.tensor_tensor(mask[:, tq - 1, tq * P:w], mask[:, tq - 1, tq * P:w], causal0[:, :], ALU.add))
                some(4)
                if hp == PAIRS - 1:
                    assert not queue
                    queue += [lambda tq=tq, w=w: topk_round(tq, w)] * (TOPK // 8 - 1)
                    queue.append(lambda tq=tq, w=w: (topk_round(tq, w), topk_end(tq, w)))
                if n in (2, 5):
                    r = n // 5
                    z, free = filled(dve, ("z", r), "G")
                    step(V.tensor_scalar(zz[:, 0, r, :], z[:, :], vT[:, 32 + r:33 + r], None, ALU.add))
                    dve.sem_inc(free, 1)
                if n == 5:
                    V.scalar_tensor_tensor(zz[:, 1, :, :], zz[:, 0, :, :], -1.0, zz[:, 0, :, :], ALU.mult, ALU.min).then_inc(z_in, 1)
                if n == 8:
                    dve.wait_ge(zexp_ready, 2)
                    for r in range(2):
                        step(V.scalar_tensor_tensor(zz[:, 3, r, :], zz[:, 0, r, :], 0.0, zz[:, 2, r, :], ALU.min, ALU.subtract))
                        for ch in range(TT):
                            cut = slice(ch * P, (ch + 1) * P)
                            V.tensor_tensor_scan(bT[:, r, cut], ones[:, :], zz[:, 3, r, cut], 0.0, ALU.mult, ALU.add).then_inc(b_ready, 1)

                if n in (6, 10):
                    mod_take(1 + n // 10)
            step(V.scalar_tensor_tensor(scale2[:, :], modT[:, 2, 0:8], 1.0, vT[:, 8:16], ALU.add, ALU.mult))
            step(V.tensor_tensor(gatev[:, 0, :], modT[:, 1, 0:8], vT[:, 16:24], ALU.mult))
            step(V.tensor_tensor(gatev[:, 1, :], modT[:, 2, 8:16], vT[:, 24:32], ALU.mult))
            dve.sem_inc(h2m_ready, 1)

            def gla_clamp(ch):
                dve.wait_ge(ex_sub, 4 * ch + 4)
                step(V.tensor_scalar(bend[:, :], bT[:, :, ch * P + P - 1], 1.0 / TAU, None, ALU.mult))
                V.tensor_scalar(expo[:, :, 0:640], expo[:, :, 0:640], CLAMP * TAU, None, ALU.min).then_inc(ex_in, 1)

            def gla_factors(ch):
                dve.wait_ge(gqk_ready, 4)
                dve.wait_ge(ex_exp, 4 * ch + 4)
                step(V.tensor_copy(dec[:, :], expo[:, :, 767]))
                for r in range(2):
                    q, k = gqk[:, r, ch * P:(ch + 1) * P], gqk[:, 2 + r, ch * P:(ch + 1) * P]
                    for lo, n, f in ((0, NB, k), (512, 2, q), (768, 1, k)):
                        e = expo[:, r, lo:lo + n * P].rearrange("p (i s) -> p i s", i=n)
                        V.tensor_tensor(e, e, f.unsqueeze(1).broadcast_to([P, n, P]), ALU.mult).then_inc(ex_ready, 1)

            def gla_mask(ch):
                for hh in range(2):
                    sc, free = filled(dve, ("sc", ch), "GO"[hh])
                    V.tensor_tensor(scT.rearrange("p (r a) n -> p r a n", a=2)[:, :, hh, :], sc[:, 0:256].rearrange("p (r n) -> p r n", r=2),
                                    upto[:, :].unsqueeze(1).broadcast_to([P, 2, P]), ALU.mult).then_inc(sc_ready, 1)
                    dve.wait_ge(sc_ready, 2 * ch + hh + 1)
                    dve.sem_inc(free, 1)

            def gla_state(ch):
                if ch == TT - 1:
                    return
                t, free = filled(dve, ("state", ch))
                for r in range(2):
                    if ch == 0:
                        V.tensor_copy(state[:, r, :], t[:, r * P:(r + 1) * P]).then_inc(state_ready, 1)
                    else:
                        V.scalar_tensor_tensor(state[:, r, :], state[:, r, :], dec[:, r:r + 1], t[:, r * P:(r + 1) * P], ALU.mult, ALU.add).then_inc(state_ready, 1)
                dve.wait_ge(state_ready, 2 * ch + 2)
                dve.sem_inc(free, 1)

            def gla_norm(ch):
                dve.wait_ge(oss_ready, 4 * ch + 4)
                rsqrt_in(st[:, 20:24], st[:, 16:20], GLA_DV).then_inc(oms_ready, 1)
                dve.wait_ge(osq_ready, ch + 1)
                step(V.reciprocal(st[:, 36:40], st[:, 24:28]))
                dve.wait_ge(gs_ready, ch + 1)
                if ch:
                    filled(dve, ("oa", ch - 1))
                for h in range(GLA_H):
                    name, r = "GO"[h % 2], h // 2
                    V.scalar_tensor_tensor(oan[:, h * P:(h + 1) * P], ps[name][:, r * P:(r + 1) * P], st[:, 36 + h:37 + h],
                                           gs[:, ch, h * P:(h + 1) * P], ALU.mult, ALU.mult).then_inc(oan_ready, 1)
                dve.wait_ge(oan_ready, 4 * ch + 4)
                for name in ("G", "O"):
                    dve.sem_inc(bank[name].free, 1)

            def gla_take(ch):
                t, free = filled(dve, ("oa", ch))
                V.tensor_copy(gqk[:, :, ch * P:(ch + 1) * P], t[:, :].rearrange("p (c n) -> p c n", c=4)).then_inc(oa_ready, 1)
                dve.wait_ge(oa_ready, ch + 1)
                dve.sem_inc(free, 1)

            for u in range(NU + 1):
                tq, hp = u // PAIRS, u % PAIRS
                w = (tq + 1) * P
                z = 4 * (u % 2)
                ch, odd = (u - GLA_AT) // 2, (u - GLA_AT) % 2
                if u < TT * PAIRS:
                    for hh in range(2):
                        s, free = filled(dve, ("att", u), f"S{hh}")
                        if u >= 2:
                            filled(dve, ("p", u - 2, hh))
                        hidden = causal0[:, :] if tq == 0 else mask[:, tq - 1, 0:w]
                        step(V.tensor_tensor_reduce(out=prob[:, u % 2, hh, 0:w], in0=s[:, 0:w], in1=hidden, scale=1.0, scalar=-3e38,
                                                    op0=ALU.add, op1=ALU.max, accum_out=sm[:, hh, z:z + 1]))
                        dve.sem_inc(free, 1)
                        V.tensor_scalar(sm[:, hh, z + 1:z + 2], sm[:, hh, z:z + 1], -HD ** -0.5, None, ALU.mult).then_inc(s_masked, 1)
                    if not odd and 0 <= ch < TT:
                        gla_clamp(ch)
                    some(4)
                    for hh in range(2):
                        dve.wait_ge(p_exp, 2 * u + hh + 1)
                        step(V.reciprocal(sm[:, hh, z + 3:z + 4], sm[:, hh, z + 2:z + 3]))
                        V.tensor_scalar(prob[:, u % 2, hh, 0:w], prob[:, u % 2, hh, 0:w], sm[:, hh, z + 3:z + 4], None, ALU.mult).then_inc(p_ready, 1)
                if not odd and 0 <= ch < TT:
                    gla_factors(ch)
                if odd and 0 <= ch < TT:
                    gla_state(ch)
                    gla_norm(ch)
                if not odd and 0 < ch <= TT:
                    gla_take(ch - 1)
                if u:
                    v = u - 1
                    m = (v // PAIRS + 1) * P
                    t, free = filled(dve, ("p", v, 1))
                    if v >= 2:
                        filled(dve, ("att", v - 2), "O")
                    V.tensor_copy(probT[:, v % 2, 1, 0:m], t[:, 0:m]).then_inc(pT_ready[1], 1)
                    dve.wait_ge(pT_ready[1], v + 1)
                    dve.sem_inc(free, 1)
                if not odd and 0 <= ch < TT:
                    gla_mask(ch)

            def split_h_lo():
                dve.wait_ge(hi_ready, 1)
                filled(dve, ("o", TT - 1), "O")
                src, lo, hi = splits["h"]
                V.tensor_tensor(lo, src, hi, ALU.subtract).then_inc(lo_ready, 1)

            def diagonal():
                V.tensor_tensor(diag[:, :].rearrange("p (k n) -> p k n", k=KD), ident[:, :].unsqueeze(1).broadcast_to([P, KD, P]),
                                gatev[:, 0, :].unsqueeze(2).broadcast_to([P, KD, P]), ALU.mult).then_inc(gd_ready, 1)

            def gate_take(tag, dst):
                for n, name in enumerate(("G", "O")):
                    g, free = filled(dve, (tag, n), name)
                    step(V.tensor_copy(dst[:, n * 512:(n + 1) * 512], g[:, :]))
                    dve.sem_inc(free, 1)

            filled(dve, ("dq", TT - 1))
            diagonal()
            split_h_lo()
            gate_take("gm", gmb)

            def mixing(n, tt):
                for ab in range(2):
                    dve.wait_ge(sig_ready, n * 2 * TT + ab * TT + tt + 1)
                    a, free = filled(dve, ("y", n, tt, ab))
                    step(V.tensor_tensor(sig[:, ab, tt, :], a[:, :], sig[:, ab, tt, :], ALU.mult))
                    dve.sem_inc(free, 1)
                if n == 0 and tt == 0:
                    filled(dve, ("att", TT * PAIRS - 1), "O")
                V.tensor_tensor(mix[:, tt, n * 512:(n + 1) * 512], sig[:, 0, tt, :], sig[:, 1, tt, :], ALU.add).then_inc(mix_ready, 1)

            def split_lo(key):
                src, lo, hi = splits[key]
                dve.wait_ge(hi_ready, split_at[key] + 1)
                V.tensor_tensor(lo, src, hi, ALU.subtract).then_inc(lo_ready, 1)

            split_lo(("proj", 0))
            split_lo("g")
            split_lo("q")
            after = {(0, 0): ("in", O_BG + 512), (0, 3): ("in", O_BG + D + 512), (1, 1): ("out", 0), (1, 2): ("out", 1)}
            for n in range(2):
                for tt in range(TT):
                    mixing(n, tt)
                    if (n, tt) in after:
                        split_lo(after[n, tt])
                if n == 0:
                    split_lo(("proj", 1))
            dve.wait_ge(mix_ready, 2 * TT)

            def shifted(dst, src, k, done):
                return V.tensor_scalar(dst, src, scale2[:, k:k + 1], modT[:, 1, 8 + k:9 + k], ALU.mult, ALU.add).then_inc(done, 1)

            def residual(tt):
                dve.wait_ge(rss_ready, 2 * tt + 2)
                step(V.tensor_tensor(st[:, 28:29], st[:, 28:29], st[:, 29:30], ALU.add))
                rsqrt_in(st[:, 30:31], st[:, 28:29], D).then_inc(rms_ready, 1)
                dve.wait_ge(rsq_ready, tt + 1)
                step(V.reciprocal(st[:, 32:33], st[:, 31:32]))
                for n in range(2):
                    a, free = filled(dve, ("out", tt, n))
                    step(V.scalar_tensor_tensor(x1(tt)[:, n * 512:(n + 1) * 512], a[:, :], st[:, 32:33], gmb[:, n * 512:(n + 1) * 512], ALU.mult, ALU.mult))
                    dve.sem_inc(free, 1)
                dve.wait_ge(ld_xr[tt % 2], 16 * (tt // 2 + 1))
                V.tensor_tensor(x1(tt), x1(tt), xres[:, tt % 2, :], ALU.add).then_inc(x1_ready, 1)
                dve.wait_ge(xss_ready, tt + 1)
                rsqrt_in(st[:, 34:35], st[:, 33:34], D).then_inc(xms_ready, 1)
                dve.wait_ge(xsq_ready, tt + 1)
                step(V.reciprocal(st[:, 43:44], st[:, 35:36]))
                if tt >= 2:
                    dve.wait_ge(xn2_stored[tt % 2], 16)
                    filled(dve, ("x2", tt - 2, 1))
                V.tensor_scalar(xn2[:, tt % 2, :], x1(tt), st[:, 43:44], None, ALU.mult).then_inc(xn2_ready, 1)

            def mix_copy(tt):
                if tt >= 2:
                    filled(dve, ("out", tt - 2, 1))
                for half in range(2):
                    t, free = filled(dve, ("mix", tt, half))
                    dve.wait_ge(mixT_ready[0], 2 * tt + half + 1)
                    V.tensor_tensor(mixT(tt % 2, 1, 512 * half, 512), t[:, :], mixT(tt % 2, 0, 512 * half, 512), ALU.subtract).then_inc(mixT_ready[1], 1)
                    dve.wait_ge(mixT_ready[1], 2 * tt + half + 1)
                    dve.sem_inc(free, 1)

            def route(tt):
                g, free = filled(dve, ("lg", tt), "G")
                V.tensor_tensor(gp[:, tt, 0:GROUPS], g[:, 0:GROUPS], b_rt_b[:, 0:GROUPS], ALU.add).then_inc(dstep, 1)
                dn[0] += 1
                step(V.tensor_tensor(lg[:, :], g[:, GROUPS:GROUPS + NE], b_rt_b[:, GROUPS:], ALU.add))
                dve.sem_inc(free, 1)
                step(V.max(top[:, tt, :], gp[:, tt, :]))
                step(V.max_index(topi[:, tt, :], top[:, tt, :], gp[:, tt, :]))
                step(V.tensor_tensor(pen[:, :], giota[:, :], topi[:, tt, 0:1].broadcast_to([P, NE]), ALU.not_equal))
                step(V.scalar_tensor_tensor(el[:, :], pen[:, :], HIDE, lg[:, :], ALU.mult, ALU.add))
                step(V.max(etop[:, tt, :], el[:, :]))
                step(V.max_index(etopi[:, tt, :], etop[:, tt, :], el[:, :]))
                step(V.tensor_tensor(e12[:, :, tt, :], iotaf[:, :].unsqueeze(1).broadcast_to([P, 2, NE]),
                                     etopi[:, tt, 0:2].unsqueeze(2).broadcast_to([P, 2, NE]), ALU.is_equal))
                V.tensor_tensor(em[:, tt, :], e12[:, 0, tt, :], e12[:, 1, tt, :], ALU.add).then_inc(em_ready, 1)

            mix_copy(0)
            for tt in range(TT + 1):
                if tt < TT - 1:
                    mix_copy(tt + 1)
                if tt:
                    t, free = filled(dve, ("x2", tt - 1, 0))
                    if tt >= 3:
                        filled(dve, ("lg", tt - 3), "G")
                    for q in range(4):
                        shifted(h2T[:, (tt - 1) % 2, q, :], t[:, q * P:(q + 1) * P], q, h2T_ready[0])
                    dve.wait_ge(h2T_ready[0], 4 * tt)
                    dve.sem_inc(free, 1)
                if tt < TT:
                    residual(tt)
                if tt:
                    route(tt - 1)

            o, free = filled(dve, "ranks", "O")
            ranks = o[:, 0:TT * NE].rearrange("p (t e) -> p t e", t=TT)
            n_e = o[:, TT * NE:(TT + 1) * NE]
            x_e, cum, base_d = (cnt[:, n, :] for n in range(3))
            step(V.tensor_tensor(x_m, n_e.unsqueeze(2).broadcast_to([P, NE, SEQ // SLOT]), thr[:, :].unsqueeze(1).broadcast_to([P, NE, SEQ // SLOT]), ALU.is_gt))
            step(V.tensor_reduce(x_e, x_m, AX.X, ALU.add))
            step(V.tensor_tensor_scan(cum, ones[:, 0:NE], x_e, 0.0, ALU.mult, ALU.add))
            step(V.tensor_tensor(base_d, cum, x_e, ALU.subtract))
            step(V.scalar_tensor_tensor(base_d, base_d, float(SLOT), base_m[:, :], ALU.mult, ALU.add))
            step(V.scalar_tensor_tensor(rpos[:, :, :], ranks, float(SLOT), base_d.unsqueeze(1).broadcast_to([P, TT, NE]), ALU.is_ge, ALU.mult))
            step(V.tensor_tensor(rpos[:, :, :], rpos[:, :, :], ranks, ALU.add))
            dve.sem_inc(free, 1)
            step(V.tensor_tensor(rtmp4, e12[:, :, :, :], rpos[:, :, :].unsqueeze(1).broadcast_to([P, 2, TT, NE]), ALU.mult))
            step(V.tensor_reduce(spos[:, :, :], rtmp4, AX.X, ALU.add))
            step(V.scalar_tensor_tensor(spos[:, :, :], etopi[:, :, 0:2].rearrange("p t w -> p w t"), float(SLOT), spos[:, :, :], ALU.mult, ALU.add))
            pos = spos[:, :, :].rearrange("p w t -> p (w t)")
            names = rowid[:, :, :, :].rearrange("p w t a -> p (w t) a")
            nn = 2 * TT
            step(V.tensor_tensor(hi_ge[:, :, :], pos.unsqueeze(2).broadcast_to([P, nn, NPALL + 1]), iota_hi[:, :].unsqueeze(1).broadcast_to([P, nn, NPALL + 1]), ALU.is_ge))
            step(V.tensor_tensor(hi_d[:, :, :], hi_ge[:, :, 0:NPALL], hi_ge[:, :, 1:NPALL + 1], ALU.subtract))
            step(V.tensor_tensor(hi_hot, hi_d[:, :, :].unsqueeze(2).broadcast_to([P, nn, 2, NPALL]), names.unsqueeze(3).broadcast_to([P, nn, 2, NPALL]), ALU.mult))
            step(V.tensor_reduce(hi_n, hi_ge[:, :, :], AX.X, ALU.add))
            step(V.scalar_tensor_tensor(lo_n, hi_n, -float(P), pos, ALU.mult, ALU.add))
            for n in (0, TT):
                V.tensor_tensor(lo_hot[:, n:n + TT, :], lo_n[:, n:n + TT].unsqueeze(2).broadcast_to([P, TT, P]),
                                iota_lo[:, :].unsqueeze(1).broadcast_to([P, TT, P]), ALU.is_equal).then_inc(pos_ready, 1)
            g, free = filled(dve, "slots", "G")
            V.tensor_scalar(tables[:, :, :].rearrange("p w n -> p (w n)"), g[:, 0:2 * NPALL], -1.0, NONE, ALU.mult, ALU.add).then_inc(slot_ready, 1)
            dve.wait_ge(slot_ready, 1)
            dve.sem_inc(free, 1)
            step(V.tensor_tensor(ovc[:, :, :], iotaf[:, 0:NOV].unsqueeze(2).broadcast_to([P, NOV, NE]), cum.unsqueeze(1).broadcast_to([P, NOV, NE]), ALU.is_ge))
            step(V.tensor_reduce(ovf[:, 0:NOV], ovc[:, :, :], AX.X, ALU.add))
            step(V.tensor_scalar(ovf[:, 0:NOV], ovf[:, 0:NOV], float(NE - 1), None, ALU.min))
            step(V.tensor_scalar(cnt[:, 5, 0:NOV // 2], iotaf[:, 0:NOV // 2], 2.0, None, ALU.mult))
            step(V.tensor_tensor(cnt[:, 6, 0:NOV // 2], cnt[:, 5, 0:NOV // 2], cum[:, NE - 1:NE].broadcast_to([P, NOV // 2]), ALU.is_lt))
            step(V.tensor_reduce(ovf[:, NOV:NOV + 1], cnt[:, 6, 0:NOV // 2], AX.X, ALU.add))
            step(V.tensor_copy(ovi[:, 0:NOV + 1], ovf[:, 0:NOV + 1]))
            dve.sem_inc(route_ready, 1)
            step(V.tensor_tensor(gp[:, :, 0:GROUPS], gp[:, :, 0:GROUPS], top[:, :, 0:1].broadcast_to([P, TT, GROUPS]), ALU.subtract))
            step(V.tensor_tensor(rt[:, 3, :], etop[:, :, 1], etop[:, :, 0], ALU.subtract))
            dve.sem_inc(ge_in, 1)
            dve.wait_ge(ge_out, 1)
            step(V.tensor_reduce(rt[:, 7, :], gp[:, :, 0:GROUPS], AX.X, ALU.add))
            step(V.tensor_scalar(rt[:, 8, :], rt[:, 4, :], 1.0, None, ALU.add))
            step(V.tensor_tensor(rt[:, 7, :], rt[:, 7, :], rt[:, 8, :], ALU.mult))
            step(V.reciprocal(rt[:, 9, :], rt[:, 7, :]))
            step(V.tensor_tensor(rt[:, 10, :], rt[:, 9, :], rt[:, 4, :], ALU.mult))

            def pair(j, b, back, stores):
                dve.wait_ge(bank["T0"].full, moe_base["T0"] + j + 1)
                dve.wait_ge(bank["G"].full, moe_base["G"] + back)
                for q in range(4):
                    shifted(h2g[:, b, q, :], ps["T0"][:, q * P:(q + 1) * P], q, h2g_ready[0])
                dve.wait_ge(h2g_ready[0], 4 * j + 4)
                dve.sem_inc(bank["T0"].free, 1)
                dve.wait_ge(silu_ready, j + 1)
                V.tensor_tensor(aact[:, b, :], gact[:, b, :], ps["G"][:, DE:2 * DE], ALU.mult).then_inc(act_ready, 1)
                dve.wait_ge(act_ready, j + 1)
                dve.sem_inc(bank["G"].free, 1)
                dve.wait_ge(bank["A0"].full, moe_base["A0"] + j + 1)
                if stores is not None:
                    dve.wait_ge(y_stored[b], 16 * stores)
                V.tensor_copy(yb[:, b, 0:512], ps["A0"][:, :]).then_inc(yb_ready, 1)
                dve.wait_ge(yb_ready, j + 1)
                dve.sem_inc(bank["A0"].free, 1)

            pair(0, 0, 0, None)
            pair(1, 1, 0, None)
            with dve.Fori(1, NPAIR // 2) as i:
                pair(2 * i, 0, 2 * i - 1, i)
                pair(2 * i + 1, 1, 2 * i, i)
            n_ov = dve.value_load(ovi[0:1, NOV:NOV + 1], min_val=0, max_val=NOV // 2)
            with dve.If(n_ov > 0):
                with dve.Fori(0, n_ov) as v:
                    pair(NPAIR + v, 0, NPAIR + v, NPAIR // 2 + v)
            def both_choices(tt):
                y = yc[:, tt, :, :]
                dve.wait_ge(fw_ready, tt + 1)
                V.scalar_tensor_tensor(y[:, 0, :], y[:, 1, :], rt[:, 10, tt:tt + 1], y[:, 0, :], ALU.mult, ALU.add).then_inc(fss_ready, 1)
                dve.wait_ge(fss_ready, tt + 1)

            both_choices(0)
            for tt in range(TT):
                y = yc[:, tt, :, :]
                if tt + 1 < TT:
                    both_choices(tt + 1)
                dve.wait_ge(fms_ready, tt + 1)
                rsqrt_in(st[:, 41:42], st[:, 40:41], D).then_inc(fsq_in, 1)
                dve.wait_ge(fsq_ready, tt + 1)
                step(V.reciprocal(st[:, 43:44], st[:, 42:43]))
                dve.wait_ge(fg_ready, tt + 1)
                V.scalar_tensor_tensor(x1(tt), y[:, 1, :], st[:, 43:44], x1(tt), ALU.mult, ALU.add).then_inc(fin_ready, 1)
                dve.wait_ge(fin_ready, tt + 1)


_INS = ["x", "c", "positions", "w_ada", "b_ada", "g_pre_mix", "g_post_mix", "g_pre_ffn", "g_post_ffn", "w_in", "w_gla_a2", "b_gla_a",
        "g_gla_out", "g_idx_k", "w_proj_gla", "w_proj_dsa", "w_out", "w_router_g", "b_router_g", "w_router_e", "b_router_e",
        "w_e_gate", "w_e_up", "w_e_down"]
_OUTS = [((1, SEQ, D), "float32")]


def kernel(**inputs):
    import numpy as _np
    import concourse.bacc as _bacc
    from concourse import mybir as _mybir
    from concourse.bass_utils import run_bass_kernel_spmd as _run

    nc = _bacc.Bacc("TRN2", target_bir_lowering=False, num_devices=1)
    arrays, args = {}, []
    for name in _INS:
        a = _np.ascontiguousarray(inputs[name])
        arrays[f"in_{name}_dram"] = a
        args.append(nc.dram_tensor(f"in_{name}_dram", a.shape, _mybir.dt.from_np(a.dtype), kind="ExternalInput").ap())
    for i, (shape, dtype) in enumerate(_OUTS):
        dt = _mybir.dt.from_np(_np.dtype(dtype))
        args.append(nc.dram_tensor(f"out_{i}_dram", shape, dt, kind="ExternalOutput").ap())
    layer(nc, *args)
    r = _run(nc, [arrays], core_ids=[0])
    got = tuple(r.results[0][f"out_{i}_dram"] for i in range(len(_OUTS)))
    return got[0]
```
